# Optimizing a Trainium2 kernel written in Bass

```python
import jax, jax.numpy as jnp
from jax import lax
import numpy as np
import math

D_MODEL = 1024
BATCH = 1
SEQ = 256
DEPTH = 2

HEAD_DIM = 64
MOBA_HEADS = 8
MOBA_BLOCK = 256
MOBA_TOPK = 3
SB_HEADS = 8
MLA_HEADS = 8
MLA_Q_LORA = 256
MLA_KV_LORA = 128
MLA_NOPE = 64
MLA_ROPE = 32
MLA_V = 64
MLA_QK = MLA_NOPE + MLA_ROPE
ROPE_THETA = 500000.0
PARTIAL_ROT = HEAD_DIM // 4
Q_BLOCK = 128
D_FF = 2816
N_BRANCH = 3
BRANCH_W = 512
N_SUB = 3
EPS = 1e-6

MOBA_W = MOBA_HEADS * HEAD_DIM
SB_W = SB_HEADS * HEAD_DIM
SPLIT_1 = 3 * MOBA_W
SPLIT_2 = SPLIT_1 + 3 * SB_W
SPLIT_3 = SPLIT_2 + MLA_Q_LORA
SPLIT_4 = SPLIT_3 + MLA_KV_LORA
SPLIT_5 = SPLIT_4 + MLA_ROPE
N_IN = SPLIT_5 + N_BRANCH * D_MODEL


def rms_norm(x, g):
    xf = x.astype(jnp.float32)
    y = xf * lax.rsqrt(jnp.mean(xf * xf, axis=-1, keepdims=True) + EPS)
    return (y * g.astype(jnp.float32)).astype(x.dtype)

def rope_tables(n_rot, seq):
    inv = jnp.power(jnp.float32(ROPE_THETA), -jnp.arange(0, n_rot, 2, dtype=jnp.float32) / n_rot)
    ang = jnp.arange(seq, dtype=jnp.float32)[:, None] * inv[None, :]
    return jnp.cos(ang), jnp.sin(ang)

def apply_rope(x, cos, sin):
    x1, x2 = jnp.split(x, 2, axis=-1)
    cos = cos.astype(x.dtype)
    sin = sin.astype(x.dtype)
    return jnp.concatenate([x1 * cos - x2 * sin, x1 * sin + x2 * cos], axis=-1)

def partial_rope(x, cos, sin):
    return jnp.concatenate([apply_rope(x[..., :PARTIAL_ROT], cos, sin), x[..., PARTIAL_ROT:]], axis=-1)

def to_heads(x, n_heads):
    b, s, _ = x.shape
    return x.reshape(b, s, n_heads, -1).transpose(0, 2, 1, 3)

def from_heads(x):
    b, h, s, d = x.shape
    return x.transpose(0, 2, 1, 3).reshape(b, s, h * d)

def query_blocks(q):
    b, h, s, d = q.shape
    nq = s // Q_BLOCK
    return q.reshape(b, h, nq, Q_BLOCK, d).transpose(2, 0, 1, 3, 4), nq

def merge_query_blocks(o):
    nq, b, h, qb, d = o.shape
    return o.transpose(1, 2, 0, 3, 4).reshape(b, h, nq * qb, d)

def causal_softmax_attention(q, k, v):
    s_len = k.shape[2]
    scale = q.shape[-1] ** -0.5
    qb, nq = query_blocks(q)
    kpos = jnp.arange(s_len)

    def one(args):
        qc, i = args
        sc = jnp.einsum('bhqd,bhkd->bhqk', qc, k).astype(jnp.float32) * scale
        qpos = i * Q_BLOCK + jnp.arange(Q_BLOCK)
        sc = jnp.where(kpos[None, :] <= qpos[:, None], sc, -jnp.inf)
        p = jax.nn.softmax(sc, axis=-1).astype(v.dtype)
        return jnp.einsum('bhqk,bhkd->bhqd', p, v)

    return merge_query_blocks(lax.map(one, (qb, jnp.arange(nq))))

def stick_breaking_attention(q, k, v):
    s_len = k.shape[2]
    scale = q.shape[-1] ** -0.5
    qb, nq = query_blocks(q)
    kpos = jnp.arange(s_len)

    def one(args):
        qc, i = args
        z = jnp.einsum('bhqd,bhkd->bhqk', qc, k).astype(jnp.float32) * scale
        qpos = i * Q_BLOCK + jnp.arange(Q_BLOCK)
        mask = kpos[None, :] < qpos[:, None]
        log_1m = jnp.where(mask, jax.nn.log_sigmoid(-z), 0.0)
        suffix = lax.cumsum(log_1m, axis=3, reverse=True) - log_1m
        w = jnp.where(mask, jnp.exp(jax.nn.log_sigmoid(z) + suffix), 0.0).astype(v.dtype)
        return jnp.einsum('bhqk,bhkd->bhqd', w, v)

    return merge_query_blocks(lax.map(one, (qb, jnp.arange(nq))))

def moba_attention(q, k, v):
    b, h, s_len, d = q.shape
    n = b * h
    scale = d ** -0.5
    s_pad = -(-s_len // MOBA_BLOCK) * MOBA_BLOCK
    nb = s_pad // MOBA_BLOCK
    top = min(MOBA_TOPK, nb)
    qf = q.reshape(n, s_len, d)
    pad = ((0, 0), (0, s_pad - s_len), (0, 0))
    kb = jnp.pad(k.reshape(n, s_len, d), pad).reshape(n, nb, MOBA_BLOCK, d)
    vb = jnp.pad(v.reshape(n, s_len, d), pad).reshape(n, nb, MOBA_BLOCK, d)
    k_mean = jnp.mean(kb.astype(jnp.float32), axis=2)
    gate = jnp.einsum('nsd,nbd->nsb', qf.astype(jnp.float32), k_mean)
    qblk = jnp.arange(s_len) // MOBA_BLOCK
    past = jnp.arange(nb)[None, :] < qblk[:, None]
    gate = jnp.where(past[None], gate, -jnp.inf)
    _, sel = lax.top_k(gate, top)
    valid = sel < qblk[None, :, None]
    nq = s_len // Q_BLOCK
    q_all = qf.reshape(n, nq, Q_BLOCK, d).transpose(1, 0, 2, 3)
    sel_all = sel.reshape(n, nq, Q_BLOCK, top).transpose(1, 0, 2, 3)
    val_all = valid.reshape(n, nq, Q_BLOCK, top).transpose(1, 0, 2, 3)
    rows = jnp.arange(n)[:, None, None]

    def one(args):
        qc, sc, vc, i = args
        ks = kb[rows, sc]
        vs = vb[rows, sc]
        own = (i * Q_BLOCK) // MOBA_BLOCK
        ko = lax.dynamic_index_in_dim(kb, own, axis=1, keepdims=False)
        vo = lax.dynamic_index_in_dim(vb, own, axis=1, keepdims=False)
        s_sel = jnp.einsum('nqd,nqkjd->nqkj', qc, ks).astype(jnp.float32) * scale
        s_sel = jnp.where(vc[..., None], s_sel, -jnp.inf).reshape(n, Q_BLOCK, top * MOBA_BLOCK)
        s_own = jnp.einsum('nqd,njd->nqj', qc, ko).astype(jnp.float32) * scale
        qpos = i * Q_BLOCK + jnp.arange(Q_BLOCK)
        kpos = own * MOBA_BLOCK + jnp.arange(MOBA_BLOCK)
        s_own = jnp.where(kpos[None, :] <= qpos[:, None], s_own, -jnp.inf)
        p = jax.nn.softmax(jnp.concatenate([s_sel, s_own], axis=-1), axis=-1).astype(v.dtype)
        p_sel = p[..., :top * MOBA_BLOCK].reshape(n, Q_BLOCK, top, MOBA_BLOCK)
        p_own = p[..., top * MOBA_BLOCK:]
        return jnp.einsum('nqkj,nqkjd->nqd', p_sel, vs) + jnp.einsum('nqj,njd->nqd', p_own, vo)

    out = lax.map(one, (q_all, sel_all, val_all, jnp.arange(nq)))
    return out.transpose(1, 0, 2, 3).reshape(b, h, s_len, d)

def token_mixer(hn, w_in, b_gate, q_norm, w_uq, kv_norm, w_ukv, w_branch, w_out, cos_p, sin_p, cos_m, sin_m):
    bsz, s_len, _ = hn.shape
    proj = hn @ w_in
    moba_qkv, sb_qkv, c_q, c_kv, k_rope, gates = jnp.split(
        proj, [SPLIT_1, SPLIT_2, SPLIT_3, SPLIT_4, SPLIT_5], axis=-1)
    qa, ka, va = [to_heads(t, MOBA_HEADS) for t in jnp.split(moba_qkv, 3, axis=-1)]
    y_a = from_heads(moba_attention(partial_rope(qa, cos_p, sin_p), partial_rope(ka, cos_p, sin_p), va))
    qb_, kb_, vb_ = [to_heads(t, SB_HEADS) for t in jnp.split(sb_qkv, 3, axis=-1)]
    y_b = from_heads(stick_breaking_attention(qb_, kb_, vb_))
    qc = to_heads(rms_norm(c_q, q_norm) @ w_uq, MLA_HEADS)
    qc = jnp.concatenate([qc[..., :MLA_NOPE], apply_rope(qc[..., MLA_NOPE:], cos_m, sin_m)], axis=-1)
    kv = to_heads(rms_norm(c_kv, kv_norm) @ w_ukv, MLA_HEADS)
    k_nope, vc = kv[..., :MLA_NOPE], kv[..., MLA_NOPE:]
    kr = jnp.broadcast_to(apply_rope(k_rope, cos_m, sin_m)[:, None], (bsz, MLA_HEADS, s_len, MLA_ROPE))
    y_c = from_heads(causal_softmax_attention(qc, jnp.concatenate([k_nope, kr], axis=-1), vc))
    g = jax.nn.sigmoid(gates.reshape(bsz, s_len, N_BRANCH, D_MODEL) + b_gate)
    ys = jnp.stack([y_a, y_b, y_c], axis=2)
    merged = jnp.einsum('bsnk,nkd,bsnd->bsd', ys, w_branch, g)
    return merged @ w_out

def swiglu(h, w_gate, w_up, w_down):
    return (jax.nn.silu(h @ w_gate) * (h @ w_up)) @ w_down

def modulate(x, g_pre, shift, scale):
    return rms_norm(x, g_pre) * (1 + scale) + shift

def residual_add(x, y, g_post, gate, res_w):
    return x + res_w * (1 + gate) * rms_norm(y, g_post)

def first_inputs(seed: int = 0) -> dict:
    key = jax.random.key(seed)
    ks = jax.random.split(key, 20)
    f32 = jnp.float32
    nrm = lambda k, shape, fan: jax.random.normal(k, shape, f32) * fan ** -0.5
    return {
        'x': jax.random.normal(ks[0], (BATCH, SEQ, D_MODEL), f32),
        'c': jax.random.normal(ks[1], (BATCH, D_MODEL), f32),
        'ada_w': 0.2 * nrm(ks[2], (DEPTH, D_MODEL, N_SUB * 3 * D_MODEL), D_MODEL),
        'ada_b': 0.01 * jax.random.normal(ks[3], (DEPTH, N_SUB * 3 * D_MODEL), f32),
        'norm_pre': 1.0 + 0.05 * jax.random.normal(ks[4], (DEPTH, N_SUB, D_MODEL), f32),
        'norm_post': 1.0 + 0.05 * jax.random.normal(ks[5], (DEPTH, N_SUB, D_MODEL), f32),
        'ffn_w_gate': nrm(ks[6], (DEPTH, 2, D_MODEL, D_FF), D_MODEL),
        'ffn_w_up': nrm(ks[7], (DEPTH, 2, D_MODEL, D_FF), D_MODEL),
        'ffn_w_down': nrm(ks[8], (DEPTH, 2, D_FF, D_MODEL), D_FF),
        'mix_w_in': nrm(ks[9], (DEPTH, D_MODEL, N_IN), D_MODEL),
        'mix_b_gate': 0.1 * jax.random.normal(ks[10], (DEPTH, N_BRANCH, D_MODEL), f32),
        'mla_q_norm': 1.0 + 0.05 * jax.random.normal(ks[11], (DEPTH, MLA_Q_LORA), f32),
        'mla_w_uq': nrm(ks[12], (DEPTH, MLA_Q_LORA, MLA_HEADS * MLA_QK), MLA_Q_LORA),
        'mla_kv_norm': 1.0 + 0.05 * jax.random.normal(ks[13], (DEPTH, MLA_KV_LORA), f32),
        'mla_w_ukv': nrm(ks[14], (DEPTH, MLA_KV_LORA, MLA_HEADS * (MLA_NOPE + MLA_V)), MLA_KV_LORA),
        'mix_w_branch': nrm(ks[15], (DEPTH, N_BRANCH, BRANCH_W, D_MODEL), BRANCH_W),
        'mix_w_out': nrm(ks[16], (DEPTH, D_MODEL, D_MODEL), D_MODEL),
    }

def first_block(x, c, ada_w, ada_b, norm_pre, norm_post, ffn_w_gate, ffn_w_up, ffn_w_down, mix_w_in, mix_b_gate,
              mla_q_norm, mla_w_uq, mla_kv_norm, mla_w_ukv, mix_w_branch, mix_w_out):
    bsz, s_len, _ = x.shape
    cos_p, sin_p = rope_tables(PARTIAL_ROT, s_len)
    cos_m, sin_m = rope_tables(MLA_ROPE, s_len)
    c_act = jax.nn.silu(c)
    for l in range(DEPTH):
        mod = (c_act @ ada_w[l] + ada_b[l]).reshape(bsz, N_SUB, 3, D_MODEL)[:, :, :, None, :]
        h = modulate(x, norm_pre[l, 0], mod[:, 0, 0], mod[:, 0, 1])
        x = residual_add(x, swiglu(h, ffn_w_gate[l, 0], ffn_w_up[l, 0], ffn_w_down[l, 0]), norm_post[l, 0], mod[:, 0, 2], 0.5)
        h = modulate(x, norm_pre[l, 1], mod[:, 1, 0], mod[:, 1, 1])
        y = token_mixer(h, mix_w_in[l], mix_b_gate[l], mla_q_norm[l], mla_w_uq[l], mla_kv_norm[l], mla_w_ukv[l],
                        mix_w_branch[l], mix_w_out[l], cos_p, sin_p, cos_m, sin_m)
        x = residual_add(x, y, norm_post[l, 1], mod[:, 1, 2], 1.0)
        h = modulate(x, norm_pre[l, 2], mod[:, 2, 0], mod[:, 2, 1])
        x = residual_add(x, swiglu(h, ffn_w_gate[l, 1], ffn_w_up[l, 1], ffn_w_down[l, 1]), norm_post[l, 2], mod[:, 2, 2], 0.5)
    return x


ROPE_THETA_2 = 10000.0
NORM_EPS = 1e-6
BIG = 1e9

NSA_HEADS = 8
NSA_KV_GROUPS = 2
NSA_HEADS_PER_GROUP = NSA_HEADS // NSA_KV_GROUPS
CMP_BLOCK = 32
CMP_STRIDE = 16
CMP_HIDDEN = 256
SLC_BLOCK = 64
SLC_TOPK = 16
WINDOW = 512
NSA_WIDTH = NSA_HEADS * HEAD_DIM
NSA_KV_WIDTH = NSA_KV_GROUPS * HEAD_DIM

DIFF_HEADS = 4
DIFF_QK_WIDTH = DIFF_HEADS * 2 * HEAD_DIM
DIFF_V_DIM = 2 * HEAD_DIM
DIFF_WIDTH = DIFF_HEADS * DIFF_V_DIM

SGU_CHUNK = 128
SGU_GROUPS = 4
SGU_WIDTH = 512
SGU_GROUP_DIM = SGU_WIDTH // SGU_GROUPS

N_BRANCHES = 3
BRANCH_WIDTH = 512
D_FF_2 = -(-8 * D_MODEL // (3 * 256)) * 256

IN_SPLITS = [NSA_WIDTH, 6 * NSA_KV_WIDTH, NSA_HEADS * 3,
             DIFF_QK_WIDTH, DIFF_QK_WIDTH, DIFF_WIDTH, 2 * SGU_WIDTH]
D_IN = sum(IN_SPLITS)
IN_OFFSETS = [int(v) for v in np.cumsum(IN_SPLITS)[:-1]]


def rmsnorm(x, g):
    xf = x.astype(jnp.float32)
    y = xf * lax.rsqrt(jnp.mean(xf * xf, axis=-1, keepdims=True) + NORM_EPS)
    return y.astype(x.dtype) * g

def rope(x, positions):
    half = x.shape[-1] // 2
    inv_freq = ROPE_THETA_2 ** (-jnp.arange(half, dtype=jnp.float32) / half)
    ang = positions.astype(jnp.float32)[..., None] * inv_freq
    cos = jnp.cos(ang)[:, :, None, :].astype(x.dtype)
    sin = jnp.sin(ang)[:, :, None, :].astype(x.dtype)
    x1, x2 = x[..., :half], x[..., half:]
    return jnp.concatenate([x1 * cos - x2 * sin, x2 * cos + x1 * sin], axis=-1)

def masked_softmax(logits, mask):
    lf = jnp.where(mask, logits.astype(jnp.float32), -1e30)
    p = jax.nn.softmax(lf, axis=-1)
    return jnp.where(mask, p, 0.0)

def map_query_blocks(fn, seq):
    out = lax.map(fn, jnp.arange(seq // Q_BLOCK))
    nb, b, t, w = out.shape
    return out.transpose(1, 0, 2, 3).reshape(b, nb * t, w)

def nsa_attention(q, k_cmp, v_cmp, k_slc, v_slc, k_win, v_win, gates, positions,
                  pos_k, wk1, wk2, pos_v, wv1, wv2):
    B, S = q.shape[:2]
    G, HPG, d = NSA_KV_GROUPS, NSA_HEADS_PER_GROUP, HEAD_DIM
    scale = d ** -0.5
    q_rot = rope(q, positions)
    k_slc = rope(k_slc, positions)
    k_win = rope(k_win, positions)

    n_cmp = (S - CMP_BLOCK) // CMP_STRIDE + 1
    cmp_idx = np.arange(n_cmp)[:, None] * CMP_STRIDE + np.arange(CMP_BLOCK)[None, :]
    cmp_end = jnp.asarray(np.arange(n_cmp) * CMP_STRIDE + CMP_BLOCK - 1)

    def compress(kv, pos_emb, w1, w2):
        blocks = kv[:, cmp_idx] + pos_emb[:, None, :]
        blocks = blocks.transpose(0, 1, 3, 2, 4).reshape(B, n_cmp, G, CMP_BLOCK * d)
        return jax.nn.gelu(blocks @ w1) @ w2

    kc = compress(k_cmp, pos_k, wk1, wk2)
    vc = compress(v_cmp, pos_v, wv1, wv2)

    n_slc = S // SLC_BLOCK
    slc_k = min(SLC_TOPK, n_slc)
    c_start = np.arange(n_cmp)[:, None] * CMP_STRIDE
    s_start = np.arange(n_slc)[None, :] * SLC_BLOCK
    overlap = jnp.asarray(((c_start < s_start + SLC_BLOCK) &
                           (c_start + CMP_BLOCK > s_start)).astype(np.float32))
    slc_starts = jnp.arange(n_slc) * SLC_BLOCK
    blk_ids = jnp.arange(n_slc)

    kb = k_slc.reshape(B, n_slc, SLC_BLOCK, G, d).transpose(0, 3, 1, 2, 4)
    vb = v_slc.reshape(B, n_slc, SLC_BLOCK, G, d).transpose(0, 3, 1, 2, 4)
    gather = jax.vmap(jax.vmap(lambda blocks, ids: blocks[ids]))

    k_win_pad = jnp.pad(k_win, ((0, 0), (WINDOW, 0), (0, 0), (0, 0)))
    v_win_pad = jnp.pad(v_win, ((0, 0), (WINDOW, 0), (0, 0), (0, 0)))

    def block(i):
        s0 = i * Q_BLOCK
        t = s0 + jnp.arange(Q_BLOCK)
        qg = lax.dynamic_slice_in_dim(q, s0, Q_BLOCK, axis=1).reshape(B, Q_BLOCK, G, HPG, d)
        qrg = lax.dynamic_slice_in_dim(q_rot, s0, Q_BLOCK, axis=1).reshape(B, Q_BLOCK, G, HPG, d)
        gb = lax.dynamic_slice_in_dim(gates, s0, Q_BLOCK, axis=1).reshape(B, Q_BLOCK, G, HPG, 3)

        logit_c = jnp.einsum('btghd,bngd->bghtn', qg, kc) * scale
        p_c = masked_softmax(logit_c, cmp_end[None, :] <= t[:, None])
        o_cmp = jnp.einsum('bghtn,bngd->btghd', p_c.astype(vc.dtype), vc)

        imp = jnp.einsum('bghtn,nj->bgtj', p_c, overlap)
        eligible = slc_starts[None, :] <= t[:, None]
        cur = t // SLC_BLOCK
        forced = (blk_ids[None, :] == 0) | (blk_ids[None, :] == cur[:, None]) | \
                 (blk_ids[None, :] == cur[:, None] - 1)
        score = jnp.where(forced, BIG, jnp.where(eligible, imp, -BIG))
        _, idx = lax.top_k(score, slc_k)
        ks = gather(kb, idx).reshape(B, G, Q_BLOCK, slc_k * SLC_BLOCK, d)
        vs = gather(vb, idx).reshape(B, G, Q_BLOCK, slc_k * SLC_BLOCK, d)
        kpos = (idx[..., None] * SLC_BLOCK + jnp.arange(SLC_BLOCK)).reshape(B, G, Q_BLOCK, slc_k * SLC_BLOCK)
        mask_s = (kpos <= t[None, None, :, None])[:, :, None]
        logit_s = jnp.einsum('btghd,bgtkd->bghtk', qrg, ks) * scale
        p_s = masked_softmax(logit_s, mask_s)
        o_slc = jnp.einsum('bghtk,bgtkd->btghd', p_s.astype(vs.dtype), vs)

        kw = lax.dynamic_slice_in_dim(k_win_pad, s0, Q_BLOCK + WINDOW, axis=1)
        vw = lax.dynamic_slice_in_dim(v_win_pad, s0, Q_BLOCK + WINDOW, axis=1)
        wpos = s0 - WINDOW + jnp.arange(Q_BLOCK + WINDOW)
        mask_w = (wpos[None, :] <= t[:, None]) & (wpos[None, :] > t[:, None] - WINDOW) & (wpos[None, :] >= 0)
        logit_w = jnp.einsum('btghd,bkgd->bghtk', qrg, kw) * scale
        p_w = masked_softmax(logit_w, mask_w)
        o_win = jnp.einsum('bghtk,bkgd->btghd', p_w.astype(vw.dtype), vw)

        out = gb[..., 0:1] * o_cmp + gb[..., 1:2] * o_slc + gb[..., 2:3] * o_win
        return out.reshape(B, Q_BLOCK, NSA_WIDTH)

    return map_query_blocks(block, S)

def diff_attention(q, k, v, positions, lq1, lk1, lq2, lk2, subln_g, lambda_init):
    B, S = q.shape[:2]
    scale = HEAD_DIM ** -0.5
    q = rope(q, positions)
    k = rope(k, positions)
    lam = (jnp.exp(jnp.sum(lq1 * lk1).astype(jnp.float32))
           - jnp.exp(jnp.sum(lq2 * lk2).astype(jnp.float32)) + lambda_init)
    kpos = jnp.arange(S)

    def block(i):
        s0 = i * Q_BLOCK
        t = s0 + jnp.arange(Q_BLOCK)
        qb = lax.dynamic_slice_in_dim(q, s0, Q_BLOCK, axis=1)
        logits = jnp.einsum('bthd,bshd->bhts', qb, k) * scale
        p = masked_softmax(logits, kpos[None, :] <= t[:, None])
        p = p.reshape(B, DIFF_HEADS, 2, Q_BLOCK, S)
        a = p[:, :, 0] - lam * p[:, :, 1]
        o = jnp.einsum('bhts,bshe->bthe', a.astype(v.dtype), v)
        o = rmsnorm(o, subln_g) * (1.0 - lambda_init)
        return o.reshape(B, Q_BLOCK, DIFF_WIDTH)

    return map_query_blocks(block, S)

def chunked_sgu(uv, norm_g, w_s, b_s):
    B, S = uv.shape[:2]
    z = jax.nn.gelu(uv)
    u, v = z[..., :SGU_WIDTH], z[..., SGU_WIDTH:]
    v = rmsnorm(v, norm_g).reshape(B, S // SGU_CHUNK, SGU_CHUNK, SGU_GROUPS, SGU_GROUP_DIM)
    causal = jnp.tril(jnp.ones((SGU_CHUNK, SGU_CHUNK), dtype=bool))
    w = jnp.where(causal[None], w_s, 0.0)
    s = jnp.einsum('gts,bnsgc->bntgc', w, v) + b_s.T[:, :, None]
    return u * s.reshape(B, S, SGU_WIDTH)

def second_inputs(seed: int = 0) -> dict:
    key = jax.random.key(seed)
    ks = iter(jax.random.split(key, 40))
    L, D, d = DEPTH, D_MODEL, HEAD_DIM

    def normal(shape, scale):
        return jax.random.normal(next(ks), shape, jnp.float32) * scale

    def gain(shape):
        return 1.0 + normal(shape, 0.05)

    x = normal((BATCH, SEQ, D), 1.0)
    offset = jax.random.randint(next(ks), (BATCH, 1), 0, 4096, dtype=jnp.int32)
    positions = offset + jnp.arange(SEQ, dtype=jnp.int32)[None, :]
    return {
        "x": x,
        "positions": positions,
        "attn_norm": gain((L, D)),
        "w_in": normal((L, D, D_IN), D ** -0.5),
        "cmp_pos_k": normal((L, CMP_BLOCK, d), 0.1),
        "cmp_k_w1": normal((L, CMP_BLOCK * d, CMP_HIDDEN), (CMP_BLOCK * d) ** -0.5),
        "cmp_k_w2": normal((L, CMP_HIDDEN, d), CMP_HIDDEN ** -0.5),
        "cmp_pos_v": normal((L, CMP_BLOCK, d), 0.1),
        "cmp_v_w1": normal((L, CMP_BLOCK * d, CMP_HIDDEN), (CMP_BLOCK * d) ** -0.5),
        "cmp_v_w2": normal((L, CMP_HIDDEN, d), CMP_HIDDEN ** -0.5),
        "diff_lq1": normal((L, d), 0.1),
        "diff_lk1": normal((L, d), 0.1),
        "diff_lq2": normal((L, d), 0.1),
        "diff_lk2": normal((L, d), 0.1),
        "diff_subln": gain((L, DIFF_V_DIM)),
        "sgu_norm": gain((L, SGU_WIDTH)),
        "sgu_w": normal((L, SGU_GROUPS, SGU_CHUNK, SGU_CHUNK), 0.5 * SGU_CHUNK ** -0.5),
        "sgu_b": 1.0 + normal((L, SGU_GROUPS, SGU_CHUNK), 0.1),
        "w_branch_a": normal((L, NSA_WIDTH, D), NSA_WIDTH ** -0.5),
        "w_branch_b": normal((L, DIFF_WIDTH, D), DIFF_WIDTH ** -0.5),
        "w_branch_c": normal((L, SGU_WIDTH, D), SGU_WIDTH ** -0.5),
        "w_merge": normal((L, D, N_BRANCHES * D), D ** -0.5),
        "b_merge": normal((L, N_BRANCHES * D), 0.02),
        "w_out": normal((L, D, D), D ** -0.5),
        "ffn_norm": gain((L, D)),
        "w_ffn1": normal((L, D, D_FF_2), D ** -0.5),
        "w_ffn3": normal((L, D, D_FF_2), D ** -0.5),
        "w_ffn2": normal((L, D_FF_2, D), D_FF_2 ** -0.5),
        "final_norm": gain((D,)),
    }

def second_block(x, positions, attn_norm, w_in, cmp_pos_k, cmp_k_w1, cmp_k_w2, cmp_pos_v, cmp_v_w1,
              cmp_v_w2, diff_lq1, diff_lk1, diff_lq2, diff_lk2, diff_subln, sgu_norm, sgu_w, sgu_b,
              w_branch_a, w_branch_b, w_branch_c, w_merge, b_merge, w_out, ffn_norm, w_ffn1,
              w_ffn3, w_ffn2, final_norm):
    B, S, D = x.shape
    for l in range(DEPTH):
        lambda_init = 0.8 - 0.6 * math.exp(-0.3 * l)
        h = rmsnorm(x, attn_norm[l])
        proj = h @ w_in[l]
        q_a, kv_a, g_a, q_b, k_b, v_b, uv_c = jnp.split(proj, IN_OFFSETS, axis=-1)
        k_cmp, v_cmp, k_slc, v_slc, k_win, v_win = [
            t.reshape(B, S, NSA_KV_GROUPS, HEAD_DIM) for t in jnp.split(kv_a, 6, axis=-1)]
        o_a = nsa_attention(q_a.reshape(B, S, NSA_HEADS, HEAD_DIM), k_cmp, v_cmp, k_slc, v_slc,
                            k_win, v_win, jax.nn.sigmoid(g_a).reshape(B, S, NSA_HEADS, 3), positions,
                            cmp_pos_k[l], cmp_k_w1[l], cmp_k_w2[l], cmp_pos_v[l], cmp_v_w1[l], cmp_v_w2[l])
        o_b = diff_attention(q_b.reshape(B, S, 2 * DIFF_HEADS, HEAD_DIM),
                             k_b.reshape(B, S, 2 * DIFF_HEADS, HEAD_DIM),
                             v_b.reshape(B, S, DIFF_HEADS, DIFF_V_DIM), positions,
                             diff_lq1[l], diff_lk1[l], diff_lq2[l], diff_lk2[l], diff_subln[l], lambda_init)
        o_c = chunked_sgu(uv_c, sgu_norm[l], sgu_w[l], sgu_b[l])
        gates = jax.nn.sigmoid(h @ w_merge[l] + b_merge[l]).reshape(B, S, N_BRANCHES, D)
        mixed = (gates[:, :, 0] * (o_a @ w_branch_a[l])
                 + gates[:, :, 1] * (o_b @ w_branch_b[l])
                 + gates[:, :, 2] * (o_c @ w_branch_c[l]))
        x = x + mixed @ w_out[l]
        h = rmsnorm(x, ffn_norm[l])
        x = x + (jax.nn.silu(h @ w_ffn1[l]) * (h @ w_ffn3[l])) @ w_ffn2[l]
    return rmsnorm(x, final_norm)


def setup_inputs(seed=0):
    out = dict(first_inputs(seed))
    for name, value in second_inputs(seed + 1).items():
        if name != "x":
            out[name + "_2"] = value
    return out


def reference(
    x, c, ada_w, ada_b, norm_pre, norm_post, ffn_w_gate, ffn_w_up, ffn_w_down, mix_w_in,
    mix_b_gate, mla_q_norm, mla_w_uq, mla_kv_norm, mla_w_ukv, mix_w_branch, mix_w_out,
    positions_2, attn_norm_2, w_in_2, cmp_pos_k_2, cmp_k_w1_2, cmp_k_w2_2, cmp_pos_v_2,
    cmp_v_w1_2, cmp_v_w2_2, diff_lq1_2, diff_lk1_2, diff_lq2_2, diff_lk2_2, diff_subln_2,
    sgu_norm_2, sgu_w_2, sgu_b_2, w_branch_a_2, w_branch_b_2, w_branch_c_2, w_merge_2,
    b_merge_2, w_out_2, ffn_norm_2, w_ffn1_2, w_ffn3_2, w_ffn2_2, final_norm_2,
):
    x = first_block(
        x, c, ada_w, ada_b, norm_pre, norm_post, ffn_w_gate, ffn_w_up, ffn_w_down, mix_w_in,
        mix_b_gate, mla_q_norm, mla_w_uq, mla_kv_norm, mla_w_ukv, mix_w_branch, mix_w_out,
    )
    return second_block(
        x, positions_2, attn_norm_2, w_in_2, cmp_pos_k_2, cmp_k_w1_2, cmp_k_w2_2, cmp_pos_v_2,
        cmp_v_w1_2, cmp_v_w2_2, diff_lq1_2, diff_lk1_2, diff_lq2_2, diff_lk2_2, diff_subln_2,
        sgu_norm_2, sgu_w_2, sgu_b_2, w_branch_a_2, w_branch_b_2, w_branch_c_2, w_merge_2,
        b_merge_2, w_out_2, ffn_norm_2, w_ffn1_2, w_ffn3_2, w_ffn2_2, final_norm_2,
    )


_drawn_inputs = setup_inputs


def setup_inputs(seed=0):
    import zlib

    import numpy as np

    out = dict(_drawn_inputs(seed))
    spreads = {}
    factors = {'mla_q_norm': 4.281,
     'cmp_pos_k_2': 25.289,
     'cmp_k_w2_2': 2.675,
     'cmp_pos_v_2': 5.178,
     'diff_lq1_2': 4.712,
     'diff_lk1_2': 8.0,
     'diff_lq2_2': 3.483,
     'diff_lk2_2': 8.0,
     'diff_subln_2': 4.208,
     'sgu_norm_2': 8.0,
     'b_merge_2': 8.0,
     'sgu_b_2': 3.443,
     'ffn_norm_2': 2.92}
    for name, (base, spread) in spreads.items():
        noise = np.random.default_rng([zlib.crc32(name.encode()), seed]).standard_normal(out[name].shape)
        drawn = base * np.exp(spread * noise) if base else spread * noise
        out[name] = __import__('jax').numpy.asarray(drawn.astype(out[name].dtype))
    for name, factor in factors.items():
        out[name] = (out[name] * factor).astype(out[name].dtype)
    return out
```

```python
import math
from collections import Counter
from contextlib import ExitStack, contextmanager

import numpy as np

import concourse.bass as bass
from concourse import mybir

F32 = mybir.dt.float32
F32R = mybir.dt.float32r
I32 = mybir.dt.int32
ALU = mybir.AluOpType
ACT = mybir.ActivationFunctionType
AX = mybir.AxisListType

P = 128
S = 256
D = 1024
KD = D // P
DEPTH = 2
FF = 2816
HD = 64
HEADS = 8
NJ = FF // 256
TW = 2048
RING = 3
EPS = 1e-6
NEG = -1e30
MLA_NOPE, MLA_ROPE = 64, 32
MLA_QK = MLA_NOPE + MLA_ROPE
C_CMP, N_CMP = 32, (S - 32) // 16 + 1
G = 2

FFN_TILES = 3 * NJ
MIX1_TILES = 39
MIX2_TILES = 42
B1_TILES = 2 * FFN_TILES + MIX1_TILES
B2_TILES = MIX2_TILES + FFN_TILES
N_TILES = DEPTH * (B1_TILES + B2_TILES)
ADA_PER_SUB = 24
ADA_UNITS = DEPTH * 3 * ADA_PER_SUB

CONSTS = {}
_at = 0
for _name, _w in [("ident", 128), ("inv1024", 128), ("negmask", 256), ("cmask", 30), ("cmask01", 30),
                  ("invf", 1), ("rsign", 1), ("eps", 1), ("lam_init", 4)]:
    CONSTS[_name] = (_at, _at + _w)
    _at += _w
N_CONST = _at
BLOCK1 = {}
_at = 0
for _name, _w in [("perm_moba", 128), ("perm_mla", 128), ("neg_lower", 128), ("neg_ones", 128),
                  ("inv256", 128), ("inv128", 128), ("negmask_sb", 384)]:
    BLOCK1[_name] = (_at, _at + _w)
    _at += _w
N_BLOCK1 = _at
BLOCK2 = {}
_at = 0
for _name, _w in [("perm_half", 128), ("inv128", 128), ("b_merge", 24), ("subln", 1), ("sgu_norm", 4),
                  ("lvec", 256), ("sgu_b", 512), ("sgu_wT", 512), ("w2k", 256), ("w2v", 128), ("pos", 32)]:
    BLOCK2[_name] = (_at, _at + _w)
    _at += _w
N_BLOCK2 = _at
PAR1 = {}
_at = 0
for _name, _w in [("ada_b", 72), ("norm_pre", 24), ("norm_post", 24), ("b_gate", 24), ("q_norm", 2), ("kv_norm", 1)]:
    PAR1[_name] = (_at, _at + _w)
    _at += _w
N_PAR1 = _at

N_LOADS = 5

UNIT = {"raw_full0": 16, "raw_full1": 16, "raw_full2": 16, "ada_full0": 16, "ada_full1": 16}
LAYER1 = {
    "a_ready": 22, "ada_full0": 36, "ada_full1": 36, "ada_used": 72, "arg_ready": 8, "e_ready": 16, "fills":
    37, "g_chunks": 22, "gates": 12, "gu_free": 22, "h_ready": 27, "hh_ready": 27, "hi_ready": 105,
    "kr_ready": 1, "l_ready": 8, "lo_ready": 105, "m_free": 6, "merges": 6, "mh_ready": 1, "ml_ready": 1,
    "o_ready": 24, "p_ready": 16, "pairs": 12, "part_ready": 8, "pj_out": 37, "pt_ready": 16, "r_ready": 8,
    "raw_full0": 35, "raw_full1": 35, "raw_full2": 35, "rope_done": 9, "rot_ready": 9, "rstd_ready": 7,
    "s_ready": 16, "sil_ready": 22, "sm_ready": 16, "sp_ready": 8, "sq_ready": 26, "stat_ready": 7,
    "t2_ready": 27, "t_ready": 16, "tile_used": 105, "w_ready": 8, "x_ready": 12, "y_ready": 12, "yhi_ready":
    12, "z_ready": 8, "zm_ready": 8}
LAYER2 = {
    "a_ready": 11, "aux_out": 5, "aux_ready": 5, "cl_ready": 1, "cp_ready": 1, "cs_ready": 1, "ct_out": 1,
    "ct_ready": 1, "cx_ready": 1, "e_ready": 24, "fills": 32, "g_chunks": 11, "gates": 12, "gh_pre": 1,
    "gh_ready": 1, "gl_ready": 1, "gu_free": 11, "h_ready": 16, "hh_ready": 16, "hi_ready": 75, "hx_ready": 2,
    "lam_exp": 1, "lam_pre": 1, "lo_ready": 75, "m_free": 6, "merges": 6, "mh_ready": 1, "mix_done": 1,
    "ml_ready": 1, "o_ready": 20, "odt_ready": 4, "oh_ready": 4, "ol_ready": 1, "p_ready": 20, "pairs": 8,
    "part_ready": 2, "pj_out": 32, "pt_ready": 20, "raw_full0": 25, "raw_full1": 25, "raw_full2": 25,
    "rope_done": 8, "rot_ready": 8, "rstd_ready": 4, "s_ready": 24, "sg_ready": 1, "sil_ready": 11,
    "sm_ready": 24, "sq_ready": 10, "stat_ready": 4, "t2_ready": 16, "t_ready": 20, "tile_used": 75,
    "vq_ready": 1, "vr_ready": 1, "vs_ready": 1, "vsum_ready": 1, "wt_ready": 1, "x_ready": 8, "xb32_ready":
    2, "xb_ready": 2, "y_ready": 8, "yhi_ready": 4}
FFN_BODY = {
    "a_ready": 2, "ada_full0": 2, "ada_full1": 2, "ada_used": 4, "g_chunks": 2, "gu_free": 2, "hi_ready": 6,
    "lo_ready": 6, "raw_full0": 2, "raw_full1": 2, "raw_full2": 2, "sil_ready": 2, "tile_used": 6}


class Tally:

    def __init__(self, eng, sems):
        self.eng, self.sems, self.n, self.loops = eng, sems, Counter(), []

    def value(self, name, n):
        v = n * UNIT.get(name, 1)
        for turn, per in self.loops:
            if per.get(name):
                v = turn * (per[name] * UNIT.get(name, 1)) + v
        return v

    def counts(self, name):
        self.n[name] += 1
        return self.sems[name], UNIT.get(name, 1)

    def next(self, name, k=1):
        self.n[name] += k
        return self.sems[name], self.value(name, self.n[name])

    def nth(self, name, n):
        assert n >= 1, (name, n)
        return self.sems[name], self.value(name, n)

    @contextmanager
    def loop(self, count, per):
        before = Counter(self.n)
        with self.eng.Fori(0, count) as turn:
            self.loops.append((turn, per))
            yield turn
            self.loops.pop()
        for name in set(self.n) | set(per):
            made = self.n[name] - before[name]
            assert made in (0, per.get(name, 0)), (name, made)
            if made or not self.loops:
                self.n[name] = before[name] + per.get(name, 0) * count


def build(nc, w, ada, xin, cin, posin, const_in, block1_in, par1_in, block2_in, norms2_in, out):
    ctx = ExitStack()
    with ctx:
        def sb(name, shape, dt=F32):
            return ctx.enter_context(nc.sbuf_tensor(name, [P] + list(shape), dt))

        raw = sb("raw", [RING, TW])
        whi = sb("whi", [RING, TW], F32R)
        wlo = sb("wlo", [RING, TW], F32R)
        x = sb("x", [KD, S])
        hhi = sb("hhi", [KD, S], F32R)
        hlo = sb("hlo", [KD, S], F32R)
        yhi = sb("yhi", [2, 4, S], F32R)
        ylo = sb("ylo", [2, 4, S], F32R)
        smallhi = sb("smallhi", [768], F32R)
        smalllo = sb("smalllo", [768], F32R)
        ff = sb("ff", [4, S])
        adat = sb("adat", [2, D])
        cact = sb("cact", [D])
        merged = sb("merged", [KD, S])
        set_a = sb("set_a", [20, S])
        set_b = sb("set_b", [12, S])
        bufA = sb("bufA", [2, 384])
        bufB = sb("bufB", [2, 384])
        bufC = sb("bufC", [2, 384])
        rstd = sb("rstd", [2, S])
        tables = sb("tables", [4, S])
        const = sb("const", [N_CONST])
        blk = sb("blk", [max(N_BLOCK1, N_BLOCK2)])
        par1_all = sb("par1_all", [DEPTH * N_PAR1])
        par1 = sb("par1", [N_PAR1])
        norms2_all = sb("norms2_all", [DEPTH * 16])
        norms2 = sb("norms2", [16])
        final_norm = sb("final_norm", [KD])
        modc = sb("modc", [3, 24])
        modf = sb("modf", [3, 24])
        adac = sb("adac", [2])
        nmax = sb("nmax", [2, 2])
        esum = sb("esum", [2, 2])
        rsum = sb("rsum", [2, 2])
        gts = sb("gts", [2, 24])
        hidT = sb("hidT", [2, 30])
        kcT = sb("kcT", [30])
        vcm = sb("vcm", [2, HD])
        cml = sb("cml", [3, 16])
        lam = sb("lam", [8])
        spare = sb("spare", [1])
        ps = ctx.enter_context(nc.psum_tensor("ps", [P, 8, 512], F32))

        def c(name, rows=P):
            a, b = CONSTS[name]
            return const[0:rows, a:b]

        def c1(name):
            a, b = BLOCK1[name]
            return blk[:, a:b]

        def c2(name):
            a, b = BLOCK2[name]
            return blk[:, a:b]

        def p1(name, i=0, n=None):
            a, b = PAR1[name]
            return par1[:, a + i:a + i + n] if n else par1[:, a:b]

        sq = set_a[:, 0:8, :]
        tmp = set_a[:, 8:16, :]
        ident = c("ident")
        acc = ps[:, 0:4, :].rearrange("p b (c s) -> p (b c) s", c=2)
        stat = ps[:, 6, :].rearrange("p (c s) -> p c s", c=2)

        names = ["raw_full0", "raw_full1", "raw_full2", "hi_ready", "lo_ready", "tile_used",
                 "ada_full0", "ada_full1", "ada_used", "c_ready",
                 "x_ready", "sq_ready", "stat_ready", "t2_ready", "hh_ready", "h_ready",
                 "sil_ready", "gu_free", "a_ready",
                 "pj_out", "rot_ready", "rope_done",
                 "s_ready", "sm_ready", "e_ready", "p_ready", "t_ready", "pt_ready", "o_ready",
                 "yhi_ready", "y_ready",
                 "z_ready", "zm_ready", "l_ready", "sp_ready", "r_ready", "arg_ready", "w_ready",
                 "kr_ready", "m_free", "mh_ready", "ml_ready",
                 "aux_ready", "aux_out", "xb_ready", "cl_ready", "cs_ready", "cx_ready", "cp_ready",
                 "ct_ready", "ct_out", "rstd_ready", "vsum_ready", "vr_ready", "oh_ready", "ol_ready",
                 "vs_ready", "sg_ready", "gh_pre", "gh_ready", "gl_ready", "lam_pre", "lam_exp",
                 "ang_ready", "tab_ready", "mix_done", "part_ready",
                 "xb32_ready", "hx_ready", "vq_ready", "odt_ready", "wt_ready"]
        sems = {n: ctx.enter_context(nc.semaphore(n)) for n in names}
        s_load = ctx.enter_context(nc.semaphore("s_load"))
        s_x = ctx.enter_context(nc.semaphore("s_x"))
        s_pos = ctx.enter_context(nc.semaphore("s_pos"))
        s_blk1 = ctx.enter_context(nc.semaphore("s_blk1"))
        s_blk2 = ctx.enter_context(nc.semaphore("s_blk2"))
        s_final = ctx.enter_context(nc.semaphore("s_final"))
        s_out = ctx.enter_context(nc.semaphore("s_out"))
        block = ctx.enter_context(nc.Block())

        def q_moba(h, lo, hi):
            return set_a[64 * (h % 2):64 * (h % 2) + 64, h // 2, lo:hi]

        def k_moba(h, lo, hi):
            return set_a[64 * (h % 2):64 * (h % 2) + 64, 4 + h // 2, lo:hi]

        va = set_a[:, 8:12, :].rearrange("p (t c) s -> p t (c s)", t=2)
        vb = set_b[:, 8:12, :].rearrange("p (t c) s -> p t (c s)", t=2)
        vm = set_a[:, 16:20, :].rearrange("p (t c) s -> p t (c s)", t=2)

        def q_sb(h, lo, hi):
            return set_b[64 * (h % 2):64 * (h % 2) + 64, h // 2, lo:hi]

        def k_sb(h, lo, hi):
            return set_b[64 * (h % 2):64 * (h % 2) + 64, 4 + h // 2, lo:hi]

        def q_mla(h, lo, hi):
            return set_a[0:MLA_QK, h, lo:hi]

        def k_mla(h, lo, hi):
            return set_a[0:MLA_QK, 8 + h, lo:hi]

        cq_raw = set_a[:, 12:15, :]
        kr = ff[64:96, 0, :]
        gs = ff[:, :, :]
        sil = ff[:, 0:2, :]
        a32 = ff[:, 2:4, :]
        x2 = set_a[:, 16:20, :].rearrange("p (i g) s -> p i g s", i=2)
        v_slc = set_a[:, 12:14, :]
        v_win = set_a[:, 14:16, :]

        def q_nsa(u, lo, hi):
            h = u // 2
            return set_a[64 * (h % 2):64 * (h % 2) + 64, 4 + h // 2, lo:hi]

        def k_nsa(u, lo, hi):
            h = u // 2
            return set_a[64 * (h % 2):64 * (h % 2) + 64, 8 + 2 * (u % 2) + h // 4, lo:hi]

        pcT = merged[0:N_CMP, :, :].rearrange("p a (b t) -> p (a b) t", b=2)
        od = set_a[:, 8:12, :]
        odt = set_a[:, 12:16, :]
        sq_od = set_a[:, 16:20, :]
        u_act = set_a[:, 0:4, :]
        vg = set_a[:, 4:8, :].rearrange("p (t c) s -> p t (c s)", t=2)
        hid = bufC[0:32, 0, 0:256]
        gT = bufC[0:32, 1, 0:256]
        xb32 = bufA[:, :, :].rearrange("p a b -> p (a b)")[:, 0:480]
        cmpl = bufB[:, 0, 0:240]

        class Instance:

            def __init__(self, q, k, units, scale, turns, values, pair_units, rows, double_turn, fused=False):
                self.q, self.k, self.units, self.scale = q, k, units, scale
                self.turns, self.values, self.pair_units = turns, values, pair_units
                self.rows, self.double_turn, self.fused = rows, double_turn, fused

        def head_values(v, h, kb):
            return v[:, kb, HD * h:HD * h + HD]

        moba = Instance(q_moba, k_moba, 8, HD ** -0.5, 8, lambda u, kb: head_values(va, u, kb), 2,
                        lambda u: (64 * (u % 2), 64 * (u % 2) + 64), True)
        mla = Instance(q_mla, k_mla, 8, MLA_QK ** -0.5, 8, lambda u, kb: head_values(vm, u, kb), 2,
                       lambda u: (64 * (u % 2), 64 * (u % 2) + 64), False)
        nsa = Instance(q_nsa, k_nsa, 16, HD ** -0.5, 16,
                       lambda u, kb: (v_slc, v_win)[u % 2][:, kb, 128 + HD * (u // 8):128 + HD * (u // 8) + HD], 4,
                       lambda u: (64 * (u // 2 % 2), 64 * (u // 2 % 2) + 64), True)
        diff = Instance(q_sb, k_sb, 8, HD ** -0.5, 4, lambda u, kb: vb[:, kb, 128 * u:128 * u + 128], 1,
                        lambda u: (0, 128), False, fused=True)

        @block.sync
        def _(sp):
            T = Tally(sp, sems)
            sp.dma_start(tmp, xin).then_inc(s_x, 16)
            for j in range(RING):
                sp.dma_start(raw[:, j, :], w[j]).then_inc(sems[f"raw_full{j}"], 16)
            with sp.Fori(0, N_TILES // RING - 1) as turn:
                for j in range(RING):
                    sp.wait_ge(sems["lo_ready"], turn * RING + j + 1)
                    sp.dma_start(raw[:, j, :], w[bass.ds(turn * RING + (RING + j), 1), :, :]
                                 .rearrange("a p n -> p (a n)")).then_inc(sems[f"raw_full{j}"], 16)
            sp.wait_ge(s_final, 1)
            sp.dma_start(out, tmp).then_inc(s_out, 16)
            sp.wait_ge(s_out, 16)

        @block.tensor
        def _(pe):
            T = Tally(pe, sems)
            mm = nc.tensor.matmul
            free6 = [None]

            def blocks(out_ap, pairs, start=True, stop=True, skip=False):
                last = None
                for i, (sh, sl, mh, ml) in enumerate(pairs):
                    first, end = i == 0, i == len(pairs) - 1
                    mm(out_ap, sh, mh, start=start and first, stop=False, skip_group_check=skip)
                    mm(out_ap, sh, ml, start=False, stop=False, skip_group_check=skip)
                    last = mm(out_ap, sl, mh, start=False, stop=stop and end, skip_group_check=skip)
                return last

            def tile():
                slot = T.n["lo_ready"] % RING
                pe.wait_ge(*T.next("lo_ready"))
                return slot

            def wait_bank6():
                if free6[0]:
                    pe.wait_ge(*T.nth(*free6[0]))

            def open_fill():
                k = T.n["fills"]
                T.n["fills"] += 1
                if k >= 2:
                    pe.wait_ge(*T.nth("pj_out", k - 1))
                return 4 + k % 2

            def features(bank, slot, width=256, nk=KD, chunks=2):
                for i in range(chunks):
                    last = blocks(ps[:, bank, i * S:(i + 1) * S],
                                  [(whi[:, slot, k * width + i * P:k * width + (i + 1) * P],
                                    wlo[:, slot, k * width + i * P:k * width + (i + 1) * P],
                                    hhi[:, k, :], hlo[:, k, :]) for k in range(nk)])
                return last

            def tokens(bank, slot):
                for t in range(2):
                    last = blocks(ps[:, bank, t * S:(t + 1) * S],
                                  [(hhi[:, k, t * P:(t + 1) * P], hlo[:, k, t * P:(t + 1) * P],
                                    whi[:, slot, k * S:(k + 1) * S], wlo[:, slot, k * S:(k + 1) * S])
                                   for k in range(KD)])
                return last

            def project(kind):
                slot = tile()
                bank = open_fill()
                last = features(bank, slot) if kind == "features" else tokens(bank, slot)
                last.then_inc(*T.counts("tile_used"))

            def mean(chunks, weights=None):
                for i in range(chunks):
                    if i % 2 == 0:
                        pe.wait_ge(*T.next("sq_ready"))
                    last = mm(stat[:, 0, :], c("inv1024"), sq[:, i, :], start=(i == 0), stop=(i == chunks - 1))
                last.then_inc(*T.counts("stat_ready"))

            def wait_h(n=KD):
                pe.wait_ge(*T.next("h_ready", n))

            def rotate(perm, src, out_ap):
                wait_bank6()
                k = T.n["rot_ready"]
                if k >= 1:
                    pe.wait_ge(*T.nth("rope_done", k))
                mm(out_ap, perm, src, start=True, stop=True).then_inc(*T.counts("rot_ready"))
                free6[0] = ("rope_done", T.n["rot_ready"])

            def aux(emit):
                wait_bank6()
                emit().then_inc(*T.counts("aux_ready"))
                free6[0] = ("aux_out", T.n["aux_ready"])

            def scores(ins, u):
                k = T.n["s_ready"]
                if u >= 2:
                    pe.wait_ge(*T.nth("sm_ready", k - 1))
                bank = k % 2
                mm(ps[:, bank, 0:128], ins.q(u, 0, 128), ins.k(u, 0, 128), start=True, stop=True)
                mm(ps[:, bank, 128:384], ins.q(u, 128, 256), ins.k(u, 0, 256), start=True, stop=True)\
                    .then_inc(*T.counts("s_ready"))

            def turn(ins, u):
                k = T.n["t_ready"]
                pe.wait_ge(*T.next("p_ready"))
                back = 1 if ins.double_turn else 0
                if u > back:
                    pe.wait_ge(*T.nth("pt_ready", k - back))
                bank = 7 if ins.double_turn and u % 2 else 2
                src = bufB[:, 0 if ins.fused else u % 2, :]
                for i in range(3):
                    last = nc.tensor.transpose(ps[:, bank, i * P:(i + 1) * P], src[:, i * P:(i + 1) * P], ident)
                last.then_inc(*T.counts("t_ready"))

            def weigh(ins, u, before=None):
                per = ins.pair_units
                if u % per == 0:
                    k = T.n["pairs"]
                    T.n["pairs"] += 1
                    if k >= 1:
                        pe.wait_ge(*T.nth("y_ready", k))
                pe.wait_ge(*T.next("pt_ready"))
                a, b = ins.rows(u)
                o = ps[a:b, 3, 0:S]
                pT = bufC[:, u % 2, :]
                first = True
                if before:
                    before(o)
                    first = False
                if per == 4 and u % 2:
                    first = False
                mm(o, ins.values(u, 0), pT[:, 0:256], start=first, stop=False, skip_group_check=True)
                mm(o[:, 128:256], ins.values(u, 1), pT[:, 256:384], start=False, stop=True, skip_group_check=True)\
                    .then_inc(*T.counts("o_ready"))

            def attend(ins, beside, before=lambda u: None):
                for s in range(ins.units + 2):
                    if s < ins.units:
                        scores(ins, s)
                    beside(s)
                    if ins.fused:
                        if 1 <= s <= ins.units and s % 2 == 0:
                            turn(ins, s // 2 - 1)
                        if s >= 3 and s % 2:
                            weigh(ins, s // 2 - 1)
                    else:
                        if 1 <= s <= ins.units:
                            turn(ins, s - 1)
                        if s >= 2:
                            weigh(ins, s - 2, before(s - 2))

            def sticks(beside):
                for s in range(HEADS + 3):
                    if s < HEADS:
                        k = T.n["z_ready"]
                        if s >= 2:
                            pe.wait_ge(*T.nth("zm_ready", k - 1))
                        mm(ps[:, k % 2, 0:256], k_sb(s, 0, 128), q_sb(s, 0, 256), start=True, stop=True)
                        mm(ps[:, k % 2, 256:384], k_sb(s, 128, 256), q_sb(s, 128, 256), start=True, stop=True)\
                            .then_inc(*T.counts("z_ready"))
                    beside(s)
                    if 1 <= s <= HEADS:
                        u = s - 1
                        pe.wait_ge(*T.next("sp_ready"))
                        if u >= 1:
                            pe.wait_ge(*T.nth("arg_ready", T.n["r_ready"]))
                        sp_ = bufB[:, u % 2, :]
                        mm(ps[:, 2, 0:256], c1("neg_lower"), sp_[:, 0:256], start=True, stop=False,
                           skip_group_check=True)
                        mm(ps[:, 2, 128:256], c1("neg_ones"), sp_[:, 256:384], start=False, stop=True,
                           skip_group_check=True)
                        mm(ps[:, 2, 256:384], c1("neg_lower"), sp_[:, 256:384], start=True, stop=True,
                           skip_group_check=True).then_inc(*T.counts("r_ready"))
                    if s >= 3:
                        u = s - 3
                        if u % 2 == 0:
                            k = T.n["pairs"]
                            T.n["pairs"] += 1
                            if k >= 1:
                                pe.wait_ge(*T.nth("y_ready", k))
                        pe.wait_ge(*T.next("w_ready"))
                        a = HD * (u % 2)
                        o = ps[a:a + HD, 3, 0:S]
                        mm(o, vb[:, 0, HD * u:HD * u + HD], bufC[:, u % 2, 0:256], start=True, stop=False,
                           skip_group_check=True)
                        mm(o[:, 128:256], vb[:, 1, HD * u:HD * u + HD], bufC[:, u % 2, 256:384], start=False,
                           stop=True, skip_group_check=True).then_inc(*T.counts("o_ready"))

            def merge_gate():
                project("features")

            def merge_branch(n):
                slot = tile()
                k = T.n["merges"]
                T.n["merges"] += 1
                if k >= 1:
                    pe.wait_ge(*T.nth("m_free", k))
                for i in range(4):
                    last = blocks(ps[:, 6 + i // 2, (i % 2) * S:(i % 2 + 1) * S],
                                  [(whi[:, slot, kk * 512 + i * P:kk * 512 + (i + 1) * P],
                                    wlo[:, slot, kk * 512 + i * P:kk * 512 + (i + 1) * P],
                                    yhi[:, n % 2, kk, :], ylo[:, n % 2, kk, :]) for kk in range(4)])
                last.then_inc(*T.counts("tile_used"))
                free6[0] = ("m_free", T.n["merges"])

            def wait_pairs():
                pe.wait_ge(*T.nth("y_ready", T.n["pairs"]))

            def output_projection():
                for i in range(4):
                    slot = tile()
                    if i == 0:
                        pe.wait_ge(*T.next("ml_ready"))
                    for j in range(2):
                        last = blocks(acc[:, 2 * i + j, :],
                                      [(whi[:, slot, k * 256 + j * P:k * 256 + (j + 1) * P],
                                        wlo[:, slot, k * 256 + j * P:k * 256 + (j + 1) * P],
                                        hhi[:, k, :], hlo[:, k, :]) for k in range(KD)])
                    last.then_inc(*T.counts("tile_used"))

            def gate_up():
                if T.n["g_chunks"] >= 1:
                    pe.wait_ge(*T.nth("gu_free", T.n["g_chunks"]))
                T.n["g_chunks"] += 1
                for bank in (4, 5):
                    slot = tile()
                    features(bank, slot).then_inc(*T.counts("tile_used"))

            def down(parity, first=False, end=False):
                slot = tile()
                pe.wait_ge(*T.next("a_ready"))
                for m in range(KD):
                    last = blocks(acc[:, m, :],
                                  [(whi[:, slot, cc * D + m * P:cc * D + (m + 1) * P],
                                    wlo[:, slot, cc * D + m * P:cc * D + (m + 1) * P],
                                    yhi[:, parity, cc, :], ylo[:, parity, cc, :]) for cc in range(2)],
                                  start=first and m % 2 == 0, stop=end, skip=True)
                last.then_inc(*T.counts("tile_used"))

            def ffn():
                gate_up()
                gate_up()
                down(0, first=True)
                with T.loop((NJ - 3) // 2, FFN_BODY):
                    for parity in (1, 0):
                        gate_up()
                        down(parity)
                gate_up()
                down(1)
                down(0, end=True)

            pe.wait_ge(s_load, 16 * N_LOADS)
            pe.wait_ge(s_blk1, 32)
            with T.loop(DEPTH, LAYER1):
                mean(KD)
                wait_h()
                ffn()
                mean(KD)
                mean(KD)
                wait_h()
                free6[0] = None
                for i in range(4):
                    project("features")
                    if i:
                        pe.wait_ge(*T.nth("pj_out", T.n["fills"] - 1))
                        rotate(c1("perm_moba"), set_a[:, 2 * i - 2:2 * i, :], ps[:, 6, :])
                project("tokens")
                pe.wait_ge(*T.nth("pj_out", T.n["fills"] - 1))
                rotate(c1("perm_moba"), set_a[:, 6:8, :], ps[:, 6, :])
                project("tokens")
                pe.wait_ge(*T.nth("pj_out", T.n["fills"]))
                pe.wait_ge(*T.nth("rope_done", T.n["rot_ready"]))

                def beside_moba(s):
                    if s < 4:
                        project("features")
                    elif s < 6:
                        project("tokens")
                    elif s == 6:
                        project("features")
                    elif s == 7:
                        slot = tile()
                        features(open_fill(), slot, width=128, chunks=1).then_inc(*T.counts("tile_used"))

                attend(moba, beside_moba)
                pe.wait_ge(*T.nth("pj_out", T.n["fills"]))

                def beside_sticks(s):
                    if s == 0:
                        slot = tile()
                        bank = open_fill()
                        blocks(ps[0:96, bank, 0:S], [(whi[:, slot, k * 96:(k + 1) * 96],
                                                      wlo[:, slot, k * 96:(k + 1) * 96],
                                                      hhi[:, k, :], hlo[:, k, :]) for k in range(KD)])\
                            .then_inc(*T.counts("tile_used"))
                        wait_bank6()
                        pe.wait_ge(*T.next("sq_ready", 2))
                        mm(stat[:, 0, :], c1("inv256"), sq[:, 0, :], start=True, stop=False)
                        mm(stat[:, 0, :], c1("inv256"), sq[:, 1, :], start=False, stop=True)
                        mm(stat[:, 1, :], c1("inv128"), sq[:, 2, :], start=True, stop=True)\
                            .then_inc(*T.counts("stat_ready"))
                        free6[0] = None
                    elif s == 1:
                        slot = tile()
                        wait_h(3)
                        for i in range(4):
                            bank = open_fill()
                            for j in range(2):
                                col = (2 * i + j) * MLA_QK
                                last = blocks(ps[0:96, bank, j * S:(j + 1) * S],
                                              [(whi[:, slot, k * 768 + col:k * 768 + col + MLA_QK],
                                                wlo[:, slot, k * 768 + col:k * 768 + col + MLA_QK],
                                                smallhi[:, k * S:(k + 1) * S], smalllo[:, k * S:(k + 1) * S])
                                               for k in range(2)])
                            last.then_inc(*T.counts("tile_used" if i == 3 else "part_ready"))
                        pe.wait_ge(*T.nth("pj_out", T.n["fills"] - 4))
                        rotate(c1("perm_mla")[64:96, 64:128], kr, ps[64:128, 6, 0:S])
                    elif s == 2:
                        slot = tile()
                        for i in range(4):
                            bank = open_fill()
                            for j in range(2):
                                col = (2 * i + j) * P
                                last = blocks(ps[:, bank, j * S:(j + 1) * S],
                                              [(whi[:, slot, col:col + P], wlo[:, slot, col:col + P],
                                                smallhi[:, 512:768], smalllo[:, 512:768])])
                            last.then_inc(*T.counts("part_ready"))
                        for t in range(2):
                            bank = open_fill()
                            wv = [w_[:, slot, 0:1024].rearrange("p (h c) -> p h c", c=P)[:, :, HD:P]
                                  for w_ in (whi, wlo)]
                            last = blocks(ps[:, bank, :],
                                          [(smallhi[:, 512 + t * P:512 + (t + 1) * P],
                                            smalllo[:, 512 + t * P:512 + (t + 1) * P], wv[0], wv[1])])
                            last.then_inc(*T.counts("tile_used" if t == 1 else "part_ready"))
                        for i in range(4):
                            rotate(c1("perm_mla")[64:96, 64:128], set_a[64:96, 2 * i:2 * i + 2, :], ps[64:128, 6, :])
                    elif s < 9:
                        if s % 3 == 2:
                            if s == 5:
                                wait_bank6()
                            merge_branch(0)
                        else:
                            merge_gate()

                sticks(beside_sticks)
                wait_pairs()
                pe.wait_ge(*T.nth("pj_out", T.n["fills"]))
                pe.wait_ge(*T.nth("rope_done", T.n["rot_ready"]))
                pe.wait_ge(*T.next("kr_ready"))

                def beside_mla(s):
                    if s < 6:
                        if s % 3 == 2:
                            merge_branch(1)
                        else:
                            merge_gate()

                attend(mla, beside_mla)
                for half in range(2):
                    merge_gate()
                    merge_gate()
                    if half == 0:
                        wait_pairs()
                    merge_branch(2)
                output_projection()
                wait_bank6()
                free6[0] = None
                mean(KD)
                mean(KD)
                wait_h()
                ffn()
                mean(KD)

            with T.loop(DEPTH, LAYER2) as layer:
                mean(KD)
                wait_h()
                pe.wait_ge(s_blk2, layer * 16 + 16)
                free6[0] = None
                project("features")
                project("features")
                pe.wait_ge(*T.nth("pj_out", T.n["fills"] - 1))
                rotate(c2("perm_half"), set_a[:, 0:2, :], ps[:, 6, :])
                project("features")
                pe.wait_ge(*T.nth("pj_out", T.n["fills"] - 1))
                rotate(c2("perm_half"), set_a[:, 2:4, :], ps[:, 6, :])
                for i in range(2):
                    slot = tile()
                    features(open_fill(), slot, chunks=1).then_inc(*T.counts("part_ready"))
                    tokens(open_fill(), slot).then_inc(*T.counts("tile_used"))
                    pe.wait_ge(*T.nth("pj_out", T.n["fills"] - 1))
                    rotate(c2("perm_half"), set_a[:, 8 + 2 * i:10 + 2 * i, :], ps[:, 6, :])
                slot = tile()
                features(open_fill(), slot, width=128, chunks=1).then_inc(*T.counts("tile_used"))
                pe.wait_ge(*T.nth("pj_out", T.n["fills"]))

                def gates_by_token():
                    for t in range(2):
                        last = mm(ps[:, 6, t * 32:t * 32 + 24], gT[0:24, t * P:(t + 1) * P],
                                  c("ident", 24)[:, 0:24], start=True, stop=True)
                    return last

                aux(gates_by_token)
                for kind in range(2):
                    pe.wait_ge(*T.next("xb_ready"))
                    bank = open_fill()
                    for i in range(2):
                        slot = tile()
                        last = blocks(ps[:, bank, 0:S],
                                      [(smallhi[:, (8 * i + k) * 30:(8 * i + k) * 30 + P],
                                        smalllo[:, (8 * i + k) * 30:(8 * i + k) * 30 + P],
                                        whi[:, slot, k * S:(k + 1) * S], wlo[:, slot, k * S:(k + 1) * S])
                                       for k in range(8)], start=(i == 0), stop=(i == 1))
                        last.then_inc(*T.counts("tile_used"))
                    pe.wait_ge(*T.nth("pj_out", T.n["fills"]))

                    def hidden_by_feature():
                        for k in range(2):
                            last = mm(ps[:, 6, k * 32:k * 32 + 30], hid[0:30, k * P:(k + 1) * P],
                                      c("ident", 30)[:, 0:30], start=True, stop=True)
                        return last

                    aux(hidden_by_feature)
                    pe.wait_ge(*T.nth("aux_out", T.n["aux_ready"]))

                    def second_layer():
                        if kind == 0:
                            for k in range(2):
                                last = mm(ps[:, 6, 0:30], c2("w2k")[:, k * P:(k + 1) * P], hidT[:, k, :],
                                          start=(k == 0), stop=(k == 1))
                            return last
                        for g in range(G):
                            for k in range(2):
                                last = mm(ps[0:N_CMP, 6, g * HD:(g + 1) * HD], hidT[:, k, g * N_CMP:(g + 1) * N_CMP],
                                          c2("w2v")[:, k * HD:(k + 1) * HD], start=(k == 0), stop=(k == 1))
                        return last

                    aux(second_layer)
                pe.wait_ge(*T.nth("aux_out", T.n["aux_ready"]))
                for h in range(HEADS):
                    a = HD * (h % 2)
                    for t in range(2):
                        col = (h - h % 2 + t) * N_CMP
                        last = mm(ps[:, 6 + h % 2, col:col + N_CMP], set_a[a:a + HD, h // 2, t * P:(t + 1) * P],
                                  kcT[a:a + HD, (h // 4) * N_CMP:(h // 4 + 1) * N_CMP], start=True, stop=True)
                last.then_inc(*T.counts("cl_ready"))
                pe.wait_ge(*T.next("cp_ready"))
                for h in range(HEADS):
                    for t in range(2):
                        i = 2 * h + t
                        last = nc.tensor.transpose(ps[0:N_CMP, i // 4, (i % 4) * P:(i % 4 + 1) * P],
                                                   cmpl[:, i * N_CMP:(i + 1) * N_CMP], ident)
                last.then_inc(*T.counts("ct_ready"))
                pe.wait_ge(*T.next("ct_out"))
                pe.wait_ge(*T.nth("pj_out", T.n["fills"]))
                pe.wait_ge(*T.nth("rope_done", T.n["rot_ready"]))

                def beside_nsa(s):
                    if s in (1, 3, 5, 7):
                        project("features")
                    elif s in (9, 11):
                        project("tokens")

                def compressed(u):
                    if u % 2:
                        return None
                    h = u // 2
                    return lambda o: mm(o, vcm[0:N_CMP, h // 4, :], pcT[:, 2 * h:2 * h + 2, :]
                                        .rearrange("p a t -> p (a t)"), start=True, stop=False,
                                        skip_group_check=True)

                attend(nsa, beside_nsa, compressed)
                pe.wait_ge(*T.nth("pj_out", T.n["fills"]))
                for i in range(4):
                    rotate(c2("perm_half"), set_b[:, 2 * i:2 * i + 2, :], ps[:, 6, :])
                wait_pairs()
                pe.wait_ge(*T.nth("rope_done", T.n["rot_ready"]))

                def beside_diff(s):
                    if s < 2:
                        project("features")
                    elif s < 4:
                        project("tokens")
                    elif s < 10:
                        if (s - 4) % 3 == 2:
                            if s == 6:
                                wait_bank6()
                            merge_branch(0)
                        else:
                            merge_gate()

                attend(diff, beside_diff)
                wait_bank6()
                for i in range(2):
                    pe.wait_ge(*T.next("sq_ready"))
                    if i:
                        pe.wait_ge(*T.nth("rstd_ready", T.n["stat_ready"]))
                    for j in range(2):
                        last = mm(stat[:, j, :], c2("inv128"), sq_od[:, 2 * i + j, :], start=True, stop=True)
                    last.then_inc(*T.counts("stat_ready"))
                pe.wait_ge(*T.next("vs_ready"))
                pe.wait_ge(*T.next("wt_ready"))
                for g in range(4):
                    for n in range(2):
                        last = mm(ps[:, g // 2, (g % 2) * S + n * P:(g % 2) * S + (n + 1) * P],
                                  vg[:, n, g * P:(g + 1) * P], c2("sgu_wT")[:, g * P:(g + 1) * P],
                                  start=True, stop=True)
                last.then_inc(*T.counts("sg_ready"))
                pe.wait_ge(*T.next("ol_ready"))
                free6[0] = None
                for n in (1, 2):
                    for half in range(2):
                        merge_gate()
                        merge_gate()
                        if n == 2 and half == 0:
                            pe.wait_ge(*T.next("gl_ready"))
                        merge_branch(n)
                output_projection()
                wait_bank6()
                free6[0] = None
                mean(KD)
                wait_h()
                ffn()
            mean(KD)

        @block.scalar
        def _(act):
            T = Tally(act, sems)
            A = nc.scalar.activation
            tiles_end = [0]

            def split_high():
                k = T.n["hi_ready"]
                slot = k % RING
                act.wait_ge(*T.next(f"raw_full{slot}"))
                if k - (RING - 1) >= 1:
                    act.wait_ge(*T.nth("tile_used", k - (RING - 1)))
                A(whi[:, slot, :], raw[:, slot, :], ACT.Copy).then_inc(*T.counts("hi_ready"))

            def tile_done(wait=True):
                if T.n["hi_ready"] < tiles_end[0]:
                    split_high()
                if wait:
                    act.wait_ge(*T.next("tile_used"))
                else:
                    T.n["tile_used"] += 1

            def open_layer(tiles):
                tiles_end[0] = T.n["hi_ready"] + tiles
                split_high()
                split_high()

            def taken(rows=P):
                bank = 4 + T.n["pj_out"] % 2
                return ps[0:rows, bank, :]

            def take(dst, scale=1.0, rows=P):
                A(dst, taken(rows).rearrange("p (a s) -> p a s", a=2) if len(dst.shape) == 3 else taken(rows),
                  ACT.Copy, scale=scale).then_inc(*T.counts("pj_out"))

            def squares(src, n, ready, dst=None):
                for j in range(n // 2):
                    if ready:
                        act.wait_ge(*T.next(ready))
                    A((sq if dst is None else dst)[:, 2 * j:2 * j + 2, :], src[:, 2 * j:2 * j + 2, :], ACT.Square)\
                        .then_inc(*T.counts("sq_ready"))

            def root(n=1):
                act.wait_ge(*T.next("stat_ready"))
                A(rstd[:, 0:n, :], stat[:, 0:n, :], ACT.Ln, bias=c("eps"))
                act.drain()
                A(rstd[:, 0:n, :], rstd[:, 0:n, :], ACT.Exp, scale=-0.5).then_inc(*T.counts("rstd_ready"))

            def high_parts(shift=None):
                for m in range(KD):
                    act.wait_ge(*T.next("t2_ready"))
                    if shift is None:
                        A(hhi[:, m, :], tmp[:, m, :], ACT.Copy).then_inc(*T.counts("hh_ready"))
                    else:
                        A(hhi[:, m, :], tmp[:, m, :], ACT.Identity, bias=modf[:, shift, m:m + 1])\
                            .then_inc(*T.counts("hh_ready"))

            def pair_taken(dst, n_units):
                T.n["o_ready"] += n_units
                act.wait_ge(*T.nth("o_ready", T.n["o_ready"]))
                A(dst, ps[:, 3, 0:S], ACT.Copy).then_inc(*T.counts("yhi_ready"))

            def exps(ins, u, t0):
                act.wait_ge(*T.next("sm_ready"))
                if u >= 2:
                    act.wait_ge(*T.nth("t_ready", t0 + (u // 2 if ins.fused else u - 1)))
                for i, (a, b) in enumerate(((0, 128), (128, 384))):
                    last = A(bufB[:, u % 2, a:b], bufA[:, u % 2, a:b], ACT.Exp, bias=nmax[:, u % 2, i:i + 1],
                             scale=-1.0, accum_out=esum[:, u % 2, i:i + 1])
                last.then_inc(*T.counts("e_ready"))

            def turned(ins, u, o0):
                act.wait_ge(*T.next("t_ready"))
                if u >= 2:
                    act.wait_ge(*T.nth("o_ready", o0 + u - 1))
                bank = 7 if ins.double_turn and u % 2 else 2
                A(bufC[:, u % 2, :], ps[:, bank, 0:384], ACT.Copy).then_inc(*T.counts("pt_ready"))

            def attend(ins, n, beside):
                t0, o0 = T.n["t_ready"], T.n["o_ready"]
                for s in range(ins.units + 2):
                    if s < ins.units:
                        exps(ins, s, t0)
                    beside(s)
                    if ins.fused:
                        if 1 <= s <= ins.units and s % 2 == 0:
                            turned(ins, s // 2 - 1, o0)
                    else:
                        if 1 <= s <= ins.units:
                            turned(ins, s - 1, o0)
                        if s >= 2 and (s - 1) % ins.pair_units == 0:
                            pair_taken(yhi[:, n % 2, (s - 2) // ins.pair_units, :], ins.pair_units)

            def sticks(n, beside):
                r0, o0 = T.n["r_ready"], T.n["o_ready"]
                for s in range(HEADS + 3):
                    if 2 <= s <= HEADS + 1:
                        u = s - 2
                        act.wait_ge(*T.next("arg_ready"))
                        if u >= 2:
                            act.wait_ge(*T.nth("o_ready", o0 + u - 1))
                        A(bufC[:, u % 2, :], bufA[:, u % 2, :], ACT.Exp).then_inc(*T.counts("w_ready"))
                    if s < HEADS:
                        act.wait_ge(*T.next("zm_ready"))
                        if s >= 2:
                            act.wait_ge(*T.nth("r_ready", r0 + s - 1))
                        l = bufB[:, s % 2, :]
                        A(l, bufA[:, s % 2, :], ACT.Abs)
                        act.drain()
                        A(l, l, ACT.Exp, scale=-1.0)
                        act.drain()
                        A(l, l, ACT.Ln, bias=1.0).then_inc(*T.counts("l_ready"))
                    beside(s)
                    if s >= 3 and s % 2 == 0:
                        pair_taken(yhi[:, n % 2, (s - 4) // 2, :], 2)
                T.n["r_ready"] += HEADS

            def gate(i, columns):
                tile_done()
                if T.n["gates"] >= 2 and i == 0:
                    act.wait_ge(*T.nth("m_free", T.n["gates"] // 2))
                T.n["gates"] += 1
                bank = taken()
                for j in range(2):
                    last = A(gs[:, 2 * i + j, :], bank[:, j * S:(j + 1) * S], ACT.Sigmoid,
                             bias=columns[:, j:j + 1])
                last.then_inc(*T.counts("pj_out"))

            def merge_step(k, n, half, columns):
                if k < 2:
                    c0 = n * KD + 4 * half + 2 * k
                    gate(k, columns[:, c0:c0 + 2])
                else:
                    tile_done(False)

            def merged_parts():
                act.wait_ge(*T.nth("m_free", T.n["gates"] // 2))
                A(hhi[:, :, :], merged[:, :, :], ACT.Copy).then_inc(*T.counts("mh_ready"))

            def output_projection():
                for i in range(4):
                    tile_done(wait=(i == 3))

            def ffn():
                def gate_up():
                    tile_done()
                    if T.n["sil_ready"] >= 1:
                        act.wait_ge(*T.nth("gu_free", T.n["sil_ready"]))
                    A(sil, ps[:, 4, :].rearrange("p (c s) -> p c s", c=2), ACT.Silu)\
                        .then_inc(*T.counts("sil_ready"))
                    tile_done(False)

                gate_up()
                gate_up()
                tile_done(False)
                with T.loop((NJ - 3) // 2, FFN_BODY):
                    for _ in range(2):
                        gate_up()
                        tile_done(False)
                gate_up()
                tile_done(False)
                tile_done()

            act.wait_ge(s_load, 16 * N_LOADS)
            A(cact[:, :], cact[:, :], ACT.Silu).then_inc(*T.counts("c_ready"))
            with T.loop(DEPTH, LAYER1):
                open_layer(B1_TILES)
                squares(x, KD, "x_ready")
                root()
                high_parts(0)
                ffn()
                squares(acc, KD, None)
                root()
                squares(x, KD, "x_ready")
                root()
                high_parts(1)
                for i in range(4):
                    tile_done()
                    take(set_a[:, 2 * i:2 * i + 2, :])
                for i in range(2):
                    tile_done()
                    take(va[:, :, i * S:(i + 1) * S])

                def beside_moba(s):
                    if s >= 8:
                        return
                    tile_done()
                    if s < 4:
                        take(set_b[:, 2 * s:2 * s + 2, :], scale=HD ** -0.5 if s < 2 else 1.0)
                    elif s < 6:
                        take(vb[:, :, (s - 4) * S:(s - 3) * S])
                    elif s == 6:
                        take(cq_raw[:, 0:2, :])
                    else:
                        A(cq_raw[:, 2, :], taken()[:, 0:S], ACT.Copy).then_inc(*T.counts("pj_out"))

                attend(moba, 0, beside_moba)

                def beside_sticks(s):
                    if s == 0:
                        A(sq[:, 0:2, :], cq_raw[:, 0:2, :], ACT.Square).then_inc(*T.counts("sq_ready"))
                        A(sq[:, 2, :], cq_raw[:, 2, :], ACT.Square).then_inc(*T.counts("sq_ready"))
                        root(2)
                        tile_done()
                        A(kr, ps[64:96, 4 + T.n["pj_out"] % 2, 0:S], ACT.Copy).then_inc(*T.counts("pj_out"))
                        for i in range(3):
                            act.wait_ge(*T.next("t2_ready"))
                            A(smallhi[:, i * S:(i + 1) * S], set_a[:, 4 + i, :], ACT.Copy)\
                                .then_inc(*T.counts("hh_ready"))
                    elif s == 1:
                        for i in range(4):
                            if i < 3:
                                act.wait_ge(*T.next("part_ready"))
                            else:
                                tile_done()
                            take(set_a[0:96, 2 * i:2 * i + 2, :], rows=96)
                    elif s == 2:
                        for i in range(4):
                            act.wait_ge(*T.next("part_ready"))
                            take(set_a[0:64, 8 + 2 * i:10 + 2 * i, :], rows=64)
                        act.wait_ge(*T.next("part_ready"))
                        take(vm[:, 0, :])
                        tile_done()
                        take(vm[:, 1, :])
                        act.wait_ge(*T.next("kr_ready"))
                    elif s < 9:
                        merge_step(s % 3, 0, s // 6, p1("b_gate"))

                sticks(1, beside_sticks)

                def beside_mla(s):
                    if s < 6:
                        merge_step(s % 3, 1, s // 3, p1("b_gate"))

                attend(mla, 2, beside_mla)
                for half in range(2):
                    for k in range(3):
                        merge_step(k, 2, half, p1("b_gate"))
                merged_parts()
                output_projection()
                squares(acc, KD, None)
                root()
                squares(x, KD, "x_ready")
                root()
                high_parts(2)
                ffn()
                squares(acc, KD, None)
                root()

            act.wait_ge(*T.next("ang_ready"))
            A(tables[:, 0:2, :], tables[:, 0:2, :], ACT.Sin).then_inc(*T.counts("tab_ready"))
            with T.loop(DEPTH, LAYER2) as layer:
                open_layer(B2_TILES)
                squares(x, KD, "x_ready")
                root()
                high_parts()
                act.wait_ge(s_blk2, layer * 16 + 16)
                act.wait_ge(*T.next("lam_pre"))
                A(lam[:, 2:4], lam[:, 0:2], ACT.Exp).then_inc(*T.counts("lam_exp"))
                for i in range(2):
                    tile_done()
                    take(set_a[:, 2 * i:2 * i + 2, :])
                tile_done()
                bank = taken()
                for i in range(2):
                    for g in range(G):
                        A(x2[0:64, i, g, :], bank[64 * g:64 * g + 64, i * S:(i + 1) * S], ACT.Copy)
                        last = A(x2[64:128, i, g, 0:255], bank[64 * g:64 * g + 64, i * S + 1:(i + 1) * S], ACT.Copy)
                last.then_inc(*T.counts("pj_out"))
                for i in range(2):
                    act.wait_ge(*T.next("part_ready"))
                    bank = taken()
                    for g in range(G):
                        for half in range(2):
                            last = A(set_a[64 * half:64 * half + 64, 8 + 2 * i + g, :],
                                     bank[64 * g:64 * g + 64, 0:S], ACT.Copy)
                    last.then_inc(*T.counts("pj_out"))
                    tile_done()
                    take((v_slc, v_win)[i])
                tile_done()
                A(gT[0:24, :], taken(24)[:, 0:S], ACT.Sigmoid).then_inc(*T.counts("pj_out"))

                def aux(dst, src):
                    act.wait_ge(*T.next("aux_ready"))
                    A(dst, src, ACT.Copy).then_inc(*T.counts("aux_out"))

                bank6 = ps[:, 6, 0:64].rearrange("p (a b) -> p a b", a=2)
                aux(gts[:, :, :], bank6[:, :, 0:24])
                for kind in range(2):
                    act.wait_ge(*T.next("xb32_ready"))
                    A(smallhi[:, 0:480], xb32, ACT.Copy).then_inc(*T.counts("hx_ready"))
                    tile_done(False)
                    tile_done()
                    A(hid[0:30, :], taken(30)[:, 0:S], ACT.Gelu_apprx_tanh).then_inc(*T.counts("pj_out"))
                    aux(hidT[:, :, :], bank6[:, :, 0:30])
                    if kind == 0:
                        aux(kcT[:, :], ps[:, 6, 0:30])
                    else:
                        aux(vcm[0:N_CMP, :, :], ps[0:N_CMP, 6, 0:128].rearrange("p (g d) -> p g d", g=G))
                act.wait_ge(*T.next("cs_ready"))
                A(cmpl, cmpl, ACT.Exp).then_inc(*T.counts("cx_ready"))
                act.wait_ge(*T.next("ct_ready"))
                A(merged[0:N_CMP, :, :].rearrange("p a b -> p (a b)"), ps[0:N_CMP, 0:4, :].rearrange("p a b -> p (a b)"),
                  ACT.Copy).then_inc(*T.counts("ct_out"))

                def beside_nsa(s):
                    if s in (1, 3, 5, 7):
                        tile_done()
                        take(set_b[:, s - 1:s + 1, :])
                    elif s in (9, 11):
                        tile_done()
                        take(vb[:, :, (s - 9) * 128:(s - 9) * 128 + S])

                attend(nsa, 0, beside_nsa)

                def beside_diff(s):
                    if s < 2:
                        tile_done()
                        A(u_act[:, 2 * s:2 * s + 2, :], taken().rearrange("p (c s) -> p c s", c=2),
                          ACT.Gelu_apprx_tanh).then_inc(*T.counts("pj_out"))
                    elif s < 4:
                        tile_done()
                        A(vg[:, :, (s - 2) * S:(s - 1) * S], taken().rearrange("p (t s) -> p t s", t=2),
                          ACT.Gelu_apprx_tanh).then_inc(*T.counts("pj_out"))
                    elif s < 10:
                        merge_step((s - 4) % 3, 0, (s - 4) // 3, c2("b_merge"))

                attend(diff, 1, beside_diff)
                T.n["o_ready"] += 4
                act.wait_ge(*T.next("y_ready", 8))
                squares(od, 4, None, sq_od)
                for t in range(2):
                    last = A(bufA[:, t, 0:256], vg[:, t, 0:256], ACT.Square, accum_out=esum[:, t, 0:1])
                    last = A(bufB[:, t, 0:256], vg[:, t, 256:512], ACT.Square, accum_out=esum[:, t, 1:2])
                last.then_inc(*T.counts("vq_ready"))
                act.wait_ge(*T.next("vsum_ready"))
                A(rsum[:, 0, :], rsum[:, 0, :], ACT.Ln, bias=c("eps"), scale=1.0 / 512)
                act.drain()
                A(rsum[:, 0, :], rsum[:, 0, :], ACT.Exp, scale=-0.5).then_inc(*T.counts("vr_ready"))
                for i in range(2):
                    root(2)
                    for j in range(2):
                        act.wait_ge(*T.next("odt_ready"))
                        A(yhi[:, 1, 2 * i + j, :], odt[:, 2 * i + j, :], ACT.Copy, scale=lam[:, 5:6])\
                            .then_inc(*T.counts("oh_ready"))
                for half in range(2):
                    for k in range(3):
                        merge_step(k, 1, half, c2("b_merge"))
                    if half == 0:
                        act.wait_ge(*T.next("gh_pre"))
                        A(yhi[:, 0, :, :], set_b[:, 0:4, :], ACT.Copy).then_inc(*T.counts("gh_ready"))
                for half in range(2):
                    for k in range(3):
                        merge_step(k, 2, half, c2("b_merge"))
                merged_parts()
                output_projection()
                squares(x, KD, "x_ready")
                root()
                high_parts()
                ffn()
            squares(x, KD, "x_ready")
            root()

        @block.vector
        def _(v):
            T = Tally(v, sems)
            tt, ts, stt = nc.vector.tensor_tensor, nc.vector.tensor_scalar, nc.vector.scalar_tensor_tensor
            tiles_end = [0]

            def over(ap, n, axis=1):
                shape = list(ap.shape)
                shape.insert(axis, n)
                return ap.unsqueeze(axis).broadcast_to(shape)

            def apart():
                nc.vector.memset(spare[:, :], 0.0)
                v.drain()

            def split_low():
                slot = T.n["lo_ready"] % RING
                v.wait_ge(*T.next("hi_ready"))
                tt(wlo[:, slot, :], raw[:, slot, :], whi[:, slot, :].bitcast(F32), ALU.subtract)\
                    .then_inc(*T.counts("lo_ready"))

            def tile_done(wait=True):
                if T.n["lo_ready"] < tiles_end[0]:
                    split_low()
                if wait:
                    v.wait_ge(*T.next("tile_used"))
                else:
                    T.n["tile_used"] += 1

            def open_layer(tiles):
                tiles_end[0] = T.n["lo_ready"] + tiles
                split_low()
                split_low()

            def ada_unit(out_ap):
                slot = T.n["ada_used"] % 2
                v.wait_ge(*T.next(f"ada_full{slot}"))
                nc.vector.tensor_tensor_reduce(adat[:, slot, :], adat[:, slot, :], cact[:, :], 1.0, 0.0,
                                               ALU.mult, ALU.add, out_ap).then_inc(*T.counts("ada_used"))

            def modulation(s, weight):
                v.drain()
                tt(modf[:, s, :], modc[:, s, :], p1("ada_b", 24 * s, 24), ALU.add)
                v.drain()
                stt(out=modf[:, s, 8:16], in0=modf[:, s, 8:16], scalar=1.0, in1=p1("norm_pre", 8 * s, 8),
                    op0=ALU.add, op1=ALU.mult)
                stt(out=modf[:, s, 16:24], in0=modf[:, s, 16:24], scalar=1.0, in1=p1("norm_post", 8 * s, 8),
                    op0=ALU.add, op1=ALU.mult)
                if weight != 1.0:
                    v.drain()
                    ts(modf[:, s, 16:24], modf[:, s, 16:24], weight, None, ALU.mult)
                v.drain()

            def root():
                v.wait_ge(*T.next("rstd_ready"))

            def normed(gain, shift=None):
                root()
                for m in range(KD):
                    stt(out=tmp[:, m, :], in0=x[:, m, :], scalar=gain[:, m:m + 1], in1=rstd[:, 0, :],
                        op0=ALU.mult, op1=ALU.mult).then_inc(*T.counts("t2_ready"))
                v.drain()
                for m in range(KD):
                    v.wait_ge(*T.next("hh_ready"))
                    if shift is None:
                        last = tt(hlo[:, m, :], tmp[:, m, :], hhi[:, m, :].bitcast(F32), ALU.subtract)
                    else:
                        last = stt(out=hlo[:, m, :], in0=tmp[:, m, :], scalar=shift[:, m:m + 1],
                                   in1=hhi[:, m, :].bitcast(F32), op0=ALU.add, op1=ALU.subtract)
                    last.then_inc(*T.counts("h_ready"))

            def add_normed(gate_):
                root()
                for m in range(KD):
                    stt(out=tmp[:, m, :], in0=acc[:, m, :], scalar=gate_[:, m:m + 1], in1=rstd[:, 0, :],
                        op0=ALU.mult, op1=ALU.mult)
                v.drain()
                for j in range(4):
                    tt(x[:, 2 * j:2 * j + 2, :], x[:, 2 * j:2 * j + 2, :], tmp[:, 2 * j:2 * j + 2, :], ALU.add)\
                        .then_inc(*T.counts("x_ready"))

            def add_plain():
                for j in range(4):
                    tt(x[:, 2 * j:2 * j + 2, :], x[:, 2 * j:2 * j + 2, :], acc[:, 2 * j:2 * j + 2, :], ALU.add)\
                        .then_inc(*T.counts("x_ready"))

            def rope(dst, src, rot, cos, sin, scratch):
                v.wait_ge(*T.next("rot_ready"))
                tt(dst, src, cos, ALU.mult)
                tt(scratch, rot, sin, ALU.mult)
                v.drain()
                tt(dst, dst, scratch, ALU.add).then_inc(*T.counts("rope_done"))
                v.drain()

            rot6 = ps[:, 6, :].rearrange("p (c s) -> p c s", c=2)

            def masks(ins, u, e0):
                bank = T.n["s_ready"] % 2
                v.wait_ge(*T.next("s_ready"))
                if u >= 2:
                    v.wait_ge(*T.nth("e_ready", e0 + u - 1))
                apart()
                for i, (a, b, m) in enumerate(((0, 128, c("negmask")[:, 128:256]), (128, 384, c("negmask")))):
                    last = nc.vector.tensor_tensor_reduce(bufA[:, u % 2, a:b], ps[:, bank, a:b], m, -ins.scale, 3e38,
                                                          ALU.add, ALU.min, nmax[:, u % 2, i:i + 1])
                last.then_inc(*T.counts("sm_ready"))

            def norms(ins, u, factor):
                v.wait_ge(*T.next("e_ready"))
                r = rsum[:, u % 2, :]
                nc.vector.reciprocal(r, esum[:, u % 2, :])
                v.drain()
                if factor is not None:
                    tt(r, r, factor, ALU.mult)
                    v.drain()
                elif ins.fused and u % 2:
                    ts(r, r, lam[:, 4:5], None, ALU.mult)
                    v.drain()
                for i, (a, b) in enumerate(((0, 128), (128, 384))):
                    if ins.fused and u % 2:
                        last = stt(out=bufB[:, 0, a:b], in0=bufB[:, 1, a:b], scalar=r[:, i:i + 1],
                                   in1=bufB[:, 0, a:b], op0=ALU.mult, op1=ALU.add)
                    else:
                        last = ts(bufB[:, u % 2, a:b], bufB[:, u % 2, a:b], r[:, i:i + 1], None, ALU.mult)
                if not ins.fused or u % 2:
                    last.then_inc(*T.counts("p_ready"))

            def pair_low(n, pair):
                v.wait_ge(*T.next("yhi_ready"))
                tt(ylo[:, n % 2, pair, :], ps[:, 3, 0:S],
                   yhi[:, n % 2, pair, :].bitcast(F32), ALU.subtract).then_inc(*T.counts("y_ready"))

            def attend(ins, n, beside, factor=lambda u: None):
                e0, o0 = T.n["e_ready"], T.n["o_ready"]
                for s in range(ins.units + 2):
                    if s < ins.units:
                        masks(ins, s, e0)
                    if not ins.fused:
                        beside(s)
                    if 1 <= s <= ins.units:
                        norms(ins, s - 1, factor(s - 1))
                    if ins.fused:
                        beside(s)
                    if ins.fused:
                        if s >= 3 and s % 2:
                            v.wait_ge(*T.nth("o_ready", o0 + s // 2))
                            nc.vector.tensor_copy(od[:, s // 2 - 1, :], ps[:, 3, 0:S])\
                                .then_inc(*T.counts("y_ready"))
                    elif s >= 2 and (s - 1) % ins.pair_units == 0:
                        pair_low(n, (s - 2) // ins.pair_units)
                T.n["o_ready"] += ins.turns

            def sticks(n, beside):
                w0 = T.n["w_ready"]
                for s in range(HEADS + 3):
                    if 2 <= s <= HEADS + 1:
                        u = s - 2
                        v.wait_ge(*T.next("r_ready"))
                        tt(bufA[:, u % 2, :], bufA[:, u % 2, :], ps[:, 2, 0:384], ALU.add)\
                            .then_inc(*T.counts("arg_ready"))
                    if s < HEADS:
                        bank = T.n["z_ready"] % 2
                        v.wait_ge(*T.next("z_ready"))
                        if s >= 2:
                            v.wait_ge(*T.nth("w_ready", w0 + s - 1))
                        tt(bufA[:, s % 2, :], ps[:, bank, 0:384], c1("negmask_sb"), ALU.add)\
                            .then_inc(*T.counts("zm_ready"))
                    beside(s)
                    if 1 <= s <= HEADS:
                        u = s - 1
                        v.wait_ge(*T.next("l_ready"))
                        stt(out=bufB[:, u % 2, :], in0=bufA[:, u % 2, :], scalar=0.0, in1=bufB[:, u % 2, :],
                            op0=ALU.max, op1=ALU.add).then_inc(*T.counts("sp_ready"))
                    if s >= 4 and s % 2 == 0:
                        pair_low(n, (s - 4) // 2)
                T.n["w_ready"] += HEADS
                T.n["o_ready"] += HEADS

            def merge_step(k, n, half, ada_chunks=None):
                if k < 2:
                    tile_done(False)
                    T.n["pj_out"] += 1
                    return
                tile_done()
                v.wait_ge(*T.nth("pj_out", T.n["pj_out"]))
                m = merged[:, 4 * half:4 * half + 4, :]
                branch = ps[:, 6:8, :].rearrange("p b (c s) -> p (b c) s", c=2)
                if n == 0:
                    tt(m, gs, branch, ALU.mult).then_inc(*T.counts("m_free"))
                else:
                    tt(gs[:, :, :], gs[:, :, :], branch, ALU.mult)
                    v.drain()
                    tt(m, m, gs[:, :, :], ALU.add).then_inc(*T.counts("m_free"))
                if ada_chunks is not None:
                    for i in range(4):
                        ada_unit(modc[:, 2, ada_chunks + i:ada_chunks + i + 1])
                v.drain()

            def merged_parts():
                v.wait_ge(*T.next("mh_ready"))
                tt(hlo[:, :, :], merged[:, :, :], hhi[:, :, :].bitcast(F32), ALU.subtract)\
                    .then_inc(*T.counts("ml_ready"))

            def output_projection():
                for i in range(4):
                    tile_done(wait=(i == 3))

            def ffn(ada_sub=None, ada_if=None):
                chunk = [0]

                def ada(col, turn=None):
                    if ada_sub is None:
                        return

                    def units():
                        for i in range(2):
                            ada_unit(adac[:, i:i + 1])
                        v.drain()
                        at = turn * 4 + col if turn is not None else col
                        nc.vector.tensor_copy(modc[:, ada_sub, bass.ds(at, 2)], adac[:, :])
                        v.drain()

                    if ada_if is None:
                        units()
                    else:
                        apart()
                        with v.If(ada_if):
                            units()

                def gate_up():
                    v.drain()
                    tile_done(False)
                    tile_done()
                    v.wait_ge(*T.next("sil_ready"))
                    tt(a32, sil, ps[:, 5, :].rearrange("p (c s) -> p c s", c=2), ALU.mult)\
                        .then_inc(*T.counts("gu_free"))
                    v.drain()
                    parity = chunk[0] % 2
                    chunk[0] += 1
                    nc.vector.tensor_copy(yhi[:, parity, 0:2, :], a32)
                    v.drain()
                    tt(ylo[:, parity, 0:2, :], a32, yhi[:, parity, 0:2, :].bitcast(F32), ALU.subtract)\
                        .then_inc(*T.counts("a_ready"))

                gate_up()
                ada(0)
                gate_up()
                tile_done(False)
                ada(2)
                with T.loop((NJ - 3) // 2, FFN_BODY) as turn:
                    for i in range(2):
                        gate_up()
                        tile_done(False)
                        ada(4 + 2 * i, turn)
                gate_up()
                tile_done(False)
                ada(20)
                tile_done()
                ada(22)

            v.wait_ge(s_load, 16 * N_LOADS)
            v.wait_ge(s_blk1, 32)
            v.wait_ge(s_x, 16)
            for j in range(4):
                nc.vector.tensor_copy(x[:, 2 * j:2 * j + 2, :], tmp[:, 2 * j:2 * j + 2, :])\
                    .then_inc(*T.counts("x_ready"))
            v.wait_ge(*T.next("c_ready"))
            for i in range(ADA_PER_SUB):
                ada_unit(modc[:, 0, i:i + 1])
            v.drain()
            cos1, sin1 = tables[:, 0, :], tables[:, 1, :]
            cosm, sinm = tables[64:96, 2, :], tables[64:96, 3, :]
            with T.loop(DEPTH, LAYER1) as layer:
                open_layer(B1_TILES)
                nc.vector.tensor_copy(par1[:, :], par1_all[:, bass.ds(layer * N_PAR1, N_PAR1)])
                modulation(0, 0.5)
                normed(modf[:, 0, 8:16], modf[:, 0, 0:8])
                ffn(ada_sub=1)
                add_normed(modf[:, 0, 16:24])
                modulation(1, 1.0)
                normed(modf[:, 1, 8:16], modf[:, 1, 0:8])
                for i in range(4):
                    tile_done(False)
                    if i:
                        rope(set_a[:, 2 * i - 2:2 * i, :], set_a[:, 2 * i - 2:2 * i, :], rot6, over(cos1, 2),
                             over(sin1, 2), rstd[:, :, :])
                tile_done(False)
                rope(set_a[:, 6:8, :], set_a[:, 6:8, :], rot6, over(cos1, 2), over(sin1, 2), rstd[:, :, :])
                tile_done(False)
                T.n["pj_out"] += 6

                def beside_moba(s):
                    if s < 8:
                        tile_done(False)
                        T.n["pj_out"] += 1

                attend(moba, 0, beside_moba)

                def beside_sticks(s):
                    if s == 0:
                        tile_done(False)
                        T.n["pj_out"] += 1
                        root()
                        for i in range(3):
                            g = p1("q_norm", i, 1) if i < 2 else p1("kv_norm")
                            stt(out=set_a[:, 4 + i, :], in0=cq_raw[:, i, :], scalar=g, in1=rstd[:, i // 2, :],
                                op0=ALU.mult, op1=ALU.mult).then_inc(*T.counts("t2_ready"))
                        v.drain()
                        for i in range(3):
                            v.wait_ge(*T.next("hh_ready"))
                            tt(smalllo[:, i * S:(i + 1) * S], set_a[:, 4 + i, :],
                               smallhi[:, i * S:(i + 1) * S].bitcast(F32), ALU.subtract)\
                                .then_inc(*T.counts("h_ready"))
                    elif s == 1:
                        tile_done(False)
                        T.n["pj_out"] += 4
                        rope(kr, kr, ps[64:96, 6, 0:S], cosm, sinm, rstd[64:96, 0, :])
                        nc.vector.tensor_copy(set_a[64:96, 8:16, :], over(kr, HEADS))\
                            .then_inc(*T.counts("kr_ready"))
                    elif s == 2:
                        tile_done(False)
                        T.n["pj_out"] += 6
                        for i in range(4):
                            q_ = set_a[64:96, 2 * i:2 * i + 2, :]
                            rope(q_, q_, rot6[64:96], over(cosm, 2), over(sinm, 2), rstd[64:96, :, :])
                    elif s < 9:
                        merge_step(s % 3, 0, s // 6, 4 * (s // 3 - 1))

                sticks(1, beside_sticks)

                def beside_mla(s):
                    if s < 6:
                        merge_step(s % 3, 1, s // 3, 8 + 4 * (s // 3))

                attend(mla, 2, beside_mla)
                for half in range(2):
                    for k in range(3):
                        merge_step(k, 2, half, 16 + 4 * half)
                merged_parts()
                output_projection()
                add_normed(modf[:, 1, 16:24])
                modulation(2, 0.5)
                normed(modf[:, 2, 8:16], modf[:, 2, 0:8])
                ffn(ada_sub=0, ada_if=layer < DEPTH - 1)
                add_normed(modf[:, 2, 16:24])

            v.wait_ge(s_pos, 16)
            posf, ang, kf = bufA[:, 0, 0:S], bufA[:, 1, 0:S], bufB[:, 0, 0:S]
            nc.vector.tensor_copy(posf, adat[:, 0, 0:S].bitcast(I32))
            v.drain()
            ts(ang, posf, c("invf"), None, ALU.mult)
            v.drain()
            for i, quarter in enumerate((0.25, 0.0)):
                ts(kf, ang, 1.0 / (2 * math.pi), quarter, ALU.mult, ALU.add)
                v.drain()
                ts(kf, kf, ROUND, ROUND, ALU.add, ALU.subtract)
                v.drain()
                r = tables[:, i, :]
                stt(out=r, in0=kf, scalar=-PI2[0], in1=ang, op0=ALU.mult, op1=ALU.add)
                v.drain()
                stt(out=r, in0=kf, scalar=-PI2[1], in1=r, op0=ALU.mult, op1=ALU.add)
                v.drain()
                stt(out=r, in0=kf, scalar=-PI2[2], in1=r, op0=ALU.mult, op1=ALU.add)
                v.drain()
                if i == 0:
                    ts(r, r, math.pi / 2, None, ALU.add)
                else:
                    ts(r, r, c("rsign"), None, ALU.mult)
                v.drain()
                last = ts(r, r, -3.1415925, 3.1415925, ALU.max, ALU.min)
            last.then_inc(*T.counts("ang_ready"))
            v.wait_ge(*T.next("tab_ready"))
            with T.loop(DEPTH, LAYER2) as layer:
                open_layer(B2_TILES)
                nc.vector.tensor_copy(norms2[:, :], norms2_all[:, bass.ds(layer * 16, 16)])
                nc.vector.tensor_copy(lam[:, 6:8], c("lam_init")[:, bass.ds(layer * 2, 2)])
                v.drain()
                normed(norms2[:, 0:8])
                v.wait_ge(s_blk2, layer * 16 + 16)
                lv = c2("lvec")
                for i in range(2):
                    last = nc.vector.tensor_tensor_reduce(lv[:, 128 * i:128 * i + 64], lv[:, 128 * i:128 * i + 64],
                                                          lv[:, 128 * i + 64:128 * i + 128], 1.0, 0.0,
                                                          ALU.mult, ALU.add, lam[:, i:i + 1])
                last.then_inc(*T.counts("lam_pre"))
                for i in range(2):
                    tile_done(False)
                rope(set_a[:, 4:6, :], set_a[:, 0:2, :], rot6, over(cos1, 2), over(sin1, 2), rstd[:, :, :])
                tile_done()
                T.n["pj_out"] += 3
                v.wait_ge(*T.nth("pj_out", T.n["pj_out"]))
                rope(set_a[:, 6:8, :], set_a[:, 2:4, :], rot6, over(cos1, 2), over(sin1, 2), rstd[:, :, :])
                v.wait_ge(*T.next("lam_exp"))
                stt(out=lam[:, 4:5], in0=lam[:, 3:4], scalar=lam[:, 2:3], in1=lam[:, 6:7],
                    op0=ALU.subtract, op1=ALU.subtract)
                tt(lam[:, 5:6], c2("subln"), lam[:, 7:8], ALU.mult)
                for i in range(2):
                    tile_done(False)
                    k_ = set_a[:, 8 + 2 * i:10 + 2 * i, :]
                    rope(k_, k_, rot6, over(cos1, 2), over(sin1, 2), rstd[:, :, :])
                tile_done(False)
                T.n["pj_out"] += 5
                for kind in range(2):
                    pos = c2("pos")[:, 16 * kind:16 * kind + 16]
                    for g in range(G):
                        for half in range(2):
                            src = x2[:, kind, g, 16 * half:16 * half + 240].rearrange("p (n c) -> p c n", c=16)
                            dst = xb32.rearrange("p (c g n) -> p c g n", g=G, n=N_CMP)[:, 8 * half:8 * half + 8, g, :]
                            last = tt(dst, src[:, 0:16:2, :], over(pos[:, 8 * half:8 * half + 8], N_CMP, 2), ALU.add)
                    last.then_inc(*T.counts("xb32_ready"))
                    v.drain()
                    v.wait_ge(*T.next("hx_ready"))
                    tt(smalllo[:, 0:480], xb32, smallhi[:, 0:480].bitcast(F32), ALU.subtract)\
                        .then_inc(*T.counts("xb_ready"))
                    v.drain()
                    tile_done(False)
                    tile_done()
                T.n["pj_out"] += 2
                v.wait_ge(*T.next("cl_ready"))
                l30 = cmpl.rearrange("p (h a) -> p h a", h=HEADS)
                l15 = cmpl.rearrange("p (a n) -> p a n", n=N_CMP)
                for i in range(2):
                    stt(out=l30[:, i:HEADS:2, :], in0=ps[:, 6 + i, 0:120].rearrange("p (h a) -> p h a", h=HEADS // 2),
                        scalar=HD ** -0.5, in1=over(c("cmask"), HEADS // 2), op0=ALU.mult, op1=ALU.add)
                v.drain()
                nc.vector.tensor_reduce(cml[:, 0, :], l15, AX.X, ALU.max)
                v.drain()
                tt(l15, l15, over(cml[:, 0, :], N_CMP, 2), ALU.subtract).then_inc(*T.counts("cs_ready"))
                v.wait_ge(*T.next("cx_ready"))
                nc.vector.tensor_reduce(cml[:, 1, :], l15, AX.X, ALU.add)
                v.drain()
                nc.vector.reciprocal(cml[:, 2, :], cml[:, 1, :])
                v.drain()
                v.wait_ge(*T.next("aux_out", 5))
                tt(cml[:, 2, :].rearrange("p (h t) -> p h t", t=2), cml[:, 2, :].rearrange("p (h t) -> p h t", t=2),
                   gts[:, :, :].rearrange("p t (h b) -> p h t b", b=3)[:, :, :, 0], ALU.mult)
                v.drain()
                tt(l15, l15, over(cml[:, 2, :], N_CMP, 2), ALU.mult)
                v.drain()
                tt(l30, l30, over(c("cmask01"), HEADS), ALU.mult).then_inc(*T.counts("cp_ready"))

                def beside_nsa(s):
                    if s in (1, 3, 5, 7, 9, 11):
                        tile_done(False)
                        T.n["pj_out"] += 1

                def branch_gate(u):
                    return gts[:, :, 3 * (u // 2) + 1 + u % 2]

                attend(nsa, 0, beside_nsa, branch_gate)
                for i in range(4):
                    q_ = set_b[:, 2 * i:2 * i + 2, :]
                    rope(q_, q_, rot6, over(cos1, 2), over(sin1, 2), rstd[:, :, :])

                def beside_diff(s):
                    if s < 4:
                        tile_done(False)
                        T.n["pj_out"] += 1
                    elif s < 10:
                        merge_step((s - 4) % 3, 0, (s - 4) // 3)

                attend(diff, 1, beside_diff)
                v.wait_ge(*T.next("vq_ready"))
                tt(rsum[:, 0, :], esum[:, :, 0], esum[:, :, 1], ALU.add).then_inc(*T.counts("vsum_ready"))
                for i in range(2):
                    root()
                    for j in range(2):
                        tt(odt[:, 2 * i + j, :], od[:, 2 * i + j, :], rstd[:, j, :], ALU.mult)\
                            .then_inc(*T.counts("odt_ready"))
                v.wait_ge(*T.next("vr_ready"))
                for t in range(2):
                    last = ts(vg[:, t, :], vg[:, t, :], rsum[:, 0, t:t + 1], None, ALU.mult)
                last.then_inc(*T.counts("vs_ready"))
                for i in range(4):
                    v.wait_ge(*T.next("oh_ready"))
                    last = stt(out=ylo[:, 1, i, :], in0=odt[:, i, :], scalar=lam[:, 5:6],
                               in1=yhi[:, 1, i, :].bitcast(F32), op0=ALU.mult, op1=ALU.subtract)
                last.then_inc(*T.counts("ol_ready"))
                v.wait_ge(*T.next("sg_ready"))
                sg = ps[:, 0:2, :].rearrange("p b (g s) -> p (b g) s", g=2)
                for g in range(4):
                    stt(out=set_b[:, g, :].rearrange("p (n t) -> p n t", n=2),
                        in0=sg[:, g, :].rearrange("p (n t) -> p n t", n=2), scalar=c2("sgu_norm")[:, g:g + 1],
                        in1=over(c2("sgu_b")[:, g * P:(g + 1) * P], 2), op0=ALU.mult, op1=ALU.add)
                v.drain()
                tt(set_b[:, 0:4, :], set_b[:, 0:4, :], u_act, ALU.mult).then_inc(*T.counts("gh_pre"))
                v.drain()
                for half in range(2):
                    for k in range(3):
                        merge_step(k, 1, half)
                    if half == 0:
                        v.wait_ge(*T.next("gh_ready"))
                        tt(ylo[:, 0, :, :], set_b[:, 0:4, :], yhi[:, 0, :, :].bitcast(F32), ALU.subtract)\
                            .then_inc(*T.counts("gl_ready"))
                for half in range(2):
                    for k in range(3):
                        merge_step(k, 2, half)
                v.nop().then_inc(*T.counts("mix_done"))
                merged_parts()
                output_projection()
                add_plain()
                normed(norms2[:, 8:16])
                ffn()
                add_plain()
            root()
            for m in range(KD):
                last = stt(out=tmp[:, m, :], in0=x[:, m, :], scalar=final_norm[:, m:m + 1], in1=rstd[:, 0, :],
                           op0=ALU.mult, op1=ALU.mult)
            last.then_inc(s_final, 1)

        @block.gpsimd
        def _(g):
            g.dma_start(cact[:, :], cin.partition_broadcast(P)).then_inc(s_load, 16)
            g.dma_start(const[:, :], const_in).then_inc(s_load, 16)
            g.dma_start(par1_all[:, :], par1_in).then_inc(s_load, 16)
            for i in range(2):
                g.dma_start(adat[:, i, :], ada[i]).then_inc(sems[f"ada_full{i}"], 16)
            g.dma_start(norms2_all[:, :], norms2_in[:, 0:16 * DEPTH]).then_inc(s_load, 16)
            g.dma_start(final_norm[:, :], norms2_in[:, 16 * DEPTH:16 * DEPTH + KD]).then_inc(s_load, 16)
            g.dma_start(tables[:, :, :], block1_in[:, N_BLOCK1:N_BLOCK1 + 4 * S]
                        .rearrange("p (a s) -> p a s", a=4)).then_inc(s_blk1, 16)
            g.dma_start(blk[:, 0:N_BLOCK1], block1_in[:, 0:N_BLOCK1]).then_inc(s_blk1, 16)
            with g.Fori(0, ADA_UNITS // 2 - 1) as turn:
                for i in range(2):
                    g.wait_ge(sems["ada_used"], turn * 2 + i + 1)
                    g.dma_start(adat[:, i, :], ada[bass.ds(turn * 2 + (2 + i), 1), :, :]
                                .rearrange("a p n -> p (a n)")).then_inc(sems[f"ada_full{i}"], 16)
            g.wait_ge(sems["ada_used"], ADA_UNITS)
            g.dma_start(adat[:, 0, 0:S].bitcast(I32), posin.partition_broadcast(P)).then_inc(s_pos, 16)
            g.wait_ge(sems["ang_ready"], 1)
            for l in range(DEPTH):
                if l:
                    g.wait_ge(sems["mix_done"], l)
                g.dma_start(blk[:, 0:N_BLOCK2], block2_in[l]).then_inc(s_blk2, 16)
                g.wait_ge(s_blk2, 16 * (l + 1))
                wt = c2("sgu_wT").rearrange("p (g t) -> p g t", g=4)
                g.affine_select(out=wt, in_=wt, compare_op=ALU.is_ge, fill=0.0, base=0, pattern=[[0, 4], [1, P]],
                                channel_multiplier=-1).then_inc(sems["wt_ready"], 1)


PI2 = (6.28125, 2029.0 / 2 ** 20, 2 * math.pi - 6.28125 - 2029.0 / 2 ** 20)
ROUND = 1.5 * 2.0 ** 23


def constants():
    f = np.float32
    c = np.zeros((P, N_CONST), f)
    i = np.arange(P)

    def put(into, table, name, value):
        a, b = table[name]
        into[:, a:b] = value

    put(c, CONSTS, "ident", np.eye(P))
    put(c, CONSTS, "inv1024", 1.0 / D)
    put(c, CONSTS, "eps", EPS)
    mask = np.zeros((P, S), f)
    mask[:, P:] = np.where(i[None, :] <= i[:, None], 0.0, NEG)
    put(c, CONSTS, "negmask", mask)
    ends = 16 * np.arange(N_CMP) + 31
    seen = np.concatenate([ends[None, :] <= (i[:, None] + t * P) for t in range(2)], axis=1)
    put(c, CONSTS, "cmask", np.where(seen, 0.0, NEG))
    put(c, CONSTS, "cmask01", seen.astype(f))
    half = HD // 2
    inv = (f(10000.0) ** (-np.arange(half, dtype=f) / f(half))).astype(f)
    put(c, CONSTS, "invf", inv[i % half][:, None])
    put(c, CONSTS, "rsign", np.where(i % HD < half, -1.0, 1.0)[:, None])
    put(c, CONSTS, "lam_init", np.array([v for l in range(DEPTH)
                                         for v in (0.8 - 0.6 * math.exp(-0.3 * l), 1 - (0.8 - 0.6 * math.exp(-0.3 * l)))]))

    b1 = np.zeros((P, N_BLOCK1 + 4 * S), f)

    def swap(size, start, halfrot):
        m = np.zeros((P, P), f)
        for p in range(P):
            q = p % size - start
            if 0 <= q < 2 * halfrot:
                m[p + halfrot if q < halfrot else p - halfrot, p] = 1.0
        return m

    def rotation(n_rot, size, start):
        h = n_rot // 2
        fr = np.power(f(500000.0), -np.arange(0, n_rot, 2, dtype=f) / f(n_rot)).astype(f)
        ang = (np.arange(S, dtype=f)[:, None] * fr[None, :]).astype(f)
        cos, sin = np.cos(ang).astype(f).T, np.sin(ang).astype(f).T
        ct, st = np.ones((P, S), f), np.zeros((P, S), f)
        for p in range(P):
            q = p % size - start
            if 0 <= q < n_rot:
                ct[p] = cos[q % h]
                st[p] = -sin[q % h] if q < h else sin[q % h]
        return ct, st

    put(b1, BLOCK1, "perm_moba", swap(HD, 0, HD // 8))
    put(b1, BLOCK1, "perm_mla", swap(P, MLA_NOPE, MLA_ROPE // 2))
    put(b1, BLOCK1, "neg_lower", np.where(i[:, None] >= i[None, :], -1.0, 0.0))
    put(b1, BLOCK1, "neg_ones", -1.0)
    put(b1, BLOCK1, "inv256", 1.0 / 256)
    put(b1, BLOCK1, "inv128", 1.0 / 128)
    sbm = np.zeros((P, 384), f)
    tri = np.where(i[:, None] < i[None, :], 0.0, NEG)
    sbm[:, 0:128] = tri
    sbm[:, 256:384] = tri
    put(b1, BLOCK1, "negmask_sb", sbm)
    ct, st = rotation(HD // 4, HD, 0)
    cm, sm = rotation(MLA_ROPE, P, MLA_NOPE)
    b1[:, N_BLOCK1:] = np.stack([ct, st, cm, sm], axis=1).reshape(P, 4 * S)
    return c, b1, swap(HD, 0, half)


def columns(vec):
    return np.asarray(vec).reshape(-1, P).T


def slab(wm, c0, n=256):
    k = wm.shape[0] // P
    return wm[:, c0:c0 + n].reshape(k, P, n).transpose(1, 0, 2).reshape(P, k * n)


def weight_tiles(inp):
    tiles = np.zeros((N_TILES, P, TW), np.float32)
    n = [0]

    def put(a):
        tiles[n[0], :, :a.shape[1]] = a
        n[0] += 1

    def ffn(wg, wu, wd):
        def down(j):
            put(slab(wd[256 * j:256 * j + 256], 0, D))

        for j in range(NJ):
            put(slab(wg, 256 * j))
            put(slab(wu, 256 * j))
            if j >= 1:
                down(j - 1)
        down(NJ - 1)

    def merge(gates, g0, branch, n_):
        for half in range(2):
            put(slab(gates, g0 + n_ * D + 512 * half))
            put(slab(gates, g0 + n_ * D + 512 * half + 256))
            put(slab(branch, 512 * half, 512))

    for l in range(DEPTH):
        ffn(inp["ffn_w_gate"][l, 0], inp["ffn_w_up"][l, 0], inp["ffn_w_down"][l, 0])
        w = inp["mix_w_in"][l]
        for j in range(12):
            put(slab(w, 256 * j))
        c_q, c_kv, k_r, gates = 3072, 3328, 3456, 3488
        put(slab(w, c_q))
        put(slab(w, c_kv, P))
        put(slab(w, k_r - 64, 96))
        put(slab(inp["mla_w_uq"][l], 0, HEADS * MLA_QK))
        put(slab(inp["mla_w_ukv"][l], 0, HEADS * P))
        for b in range(3):
            merge(w, gates, inp["mix_w_branch"][l, b], b)
        for j in range(4):
            put(slab(inp["mix_w_out"][l], 256 * j))
        ffn(inp["ffn_w_gate"][l, 1], inp["ffn_w_up"][l, 1], inp["ffn_w_down"][l, 1])
    for l in range(DEPTH):
        w = inp["w_in_2"][l]
        for j in range(5):
            put(slab(w, 256 * j))
        put(slab(w, 1280, P))
        for name in ("cmp_k_w1_2", "cmp_v_w1_2"):
            put(slab(inp[name][l][0:1024], 0))
            put(slab(inp[name][l][1024:2048], 0))
        for j in range(10):
            put(slab(w, 1304 + 256 * j))
        for b, name in enumerate(("w_branch_a_2", "w_branch_b_2", "w_branch_c_2")):
            merge(inp["w_merge_2"][l], 0, inp[name][l], b)
        for j in range(4):
            put(slab(inp["w_out_2"][l], 256 * j))
        ffn(inp["w_ffn1_2"][l], inp["w_ffn3_2"][l], inp["w_ffn2_2"][l])
    assert n[0] == N_TILES, n[0]
    return tiles


def pack(table, width, parts):
    out = np.zeros((P, width), np.float32)
    for name, value in parts.items():
        a, b = table[name]
        out[:, a:b] = value
    return out


def kernel(**inputs):
    from concourse import bacc
    from concourse.bass_utils import run_bass_kernel_spmd

    inp = {k: np.asarray(v) for k, v in inputs.items()}
    const, block1, perm_half = constants()
    ada = inp["ada_w"].reshape(DEPTH, D, 3 * ADA_PER_SUB, P).transpose(0, 2, 3, 1).reshape(ADA_UNITS, P, D)
    par1 = np.concatenate([pack(PAR1, N_PAR1, {
        "ada_b": columns(inp["ada_b"][l]), "norm_pre": columns(inp["norm_pre"][l]),
        "norm_post": columns(inp["norm_post"][l]), "b_gate": columns(inp["mix_b_gate"][l]),
        "q_norm": columns(inp["mla_q_norm"][l]), "kv_norm": columns(inp["mla_kv_norm"][l])}) for l in range(DEPTH)], axis=1)
    block2 = []
    for l in range(DEPTH):
        w2k = inp["cmp_k_w2_2"][l].reshape(2, P, HD).transpose(1, 0, 2)
        block2.append(pack(BLOCK2, N_BLOCK2, {
            "perm_half": perm_half, "inv128": 1.0 / 128, "b_merge": columns(inp["b_merge_2"][l]),
            "subln": columns(inp["diff_subln_2"][l]), "sgu_norm": columns(inp["sgu_norm_2"][l]),
            "lvec": np.concatenate([inp[f"diff_{k}_2"][l] for k in ("lq1", "lk1", "lq2", "lk2")])[None, :],
            "sgu_b": inp["sgu_b_2"][l].reshape(1, 512),
            "sgu_wT": inp["sgu_w_2"][l].transpose(2, 0, 1).reshape(P, 512),
            "w2k": np.concatenate([w2k, w2k], axis=2).reshape(P, 256),
            "w2v": inp["cmp_v_w2_2"][l].reshape(2, P, HD).transpose(1, 0, 2).reshape(P, 128),
            "pos": np.concatenate([inp[k][l].reshape(16, 2 * HD).T for k in ("cmp_pos_k_2", "cmp_pos_v_2")], axis=1)}))
    norms2 = np.concatenate([columns(inp[k][l]) for l in range(DEPTH) for k in ("attn_norm_2", "ffn_norm_2")]
                            + [columns(inp["final_norm_2"])], axis=1)
    arrays = {
        "w": weight_tiles(inp), "ada": ada,
        "x": inp["x"][0].T.reshape(KD, P, S).transpose(1, 0, 2),
        "c": inp["c"].reshape(D), "positions": inp["positions_2"].reshape(S),
        "const": const, "block1": block1, "par1": par1, "block2": np.stack(block2), "norms2": norms2,
    }
    arrays = {f"in_{k}": np.ascontiguousarray(v) for k, v in arrays.items()}
    nc = bacc.Bacc("TRN2", target_bir_lowering=False, num_devices=1)
    args = [nc.dram_tensor(k, v.shape, mybir.dt.from_np(v.dtype), kind="ExternalInput").ap() for k, v in arrays.items()]
    args.append(nc.dram_tensor("out_x", (P, KD, S), F32, kind="ExternalOutput").ap())
    build(nc, *args)
    r = run_bass_kernel_spmd(nc, [arrays], core_ids=[0])
    got = r.results[0]["out_x"]
    return got.transpose(2, 1, 0).reshape(1, S, D)
```

```python
import math
from collections import Counter
from contextlib import ExitStack, contextmanager

import numpy as np

import concourse.bass as bass
from concourse import mybir

F32 = mybir.dt.float32
F32R = mybir.dt.float32r
I32 = mybir.dt.int32
ALU = mybir.AluOpType
ACT = mybir.ActivationFunctionType
AX = mybir.AxisListType

P = 128
S = 256
D = 1024
KD = D // P
DEPTH = 2
FF = 2816
HD = 64
HEADS = 8
NJ = FF // 256
TW = 2048
RING = 3
EPS = 1e-6
NEG = -1e30
MLA_NOPE, MLA_ROPE = 64, 32
MLA_QK = MLA_NOPE + MLA_ROPE
C_CMP, N_CMP = 32, (S - 32) // 16 + 1
G = 2

FFN_TILES = 3 * NJ
MIX1_TILES = 39
MIX2_TILES = 42
B1_TILES = 2 * FFN_TILES + MIX1_TILES
B2_TILES = MIX2_TILES + FFN_TILES
N_TILES = DEPTH * (B1_TILES + B2_TILES)
ADA_PER_SUB = 24
ADA_UNITS = DEPTH * 3 * ADA_PER_SUB

CONSTS = {}
_at = 0
for _name, _w in [("ident", 128), ("inv1024", 128), ("negmask", 256), ("cmask", 30), ("cmask01", 30),
                  ("invf", 1), ("rsign", 1), ("eps", 1), ("lam_init", 4)]:
    CONSTS[_name] = (_at, _at + _w)
    _at += _w
N_CONST = _at
BLOCK1 = {}
_at = 0
for _name, _w in [("perm_moba", 128), ("perm_mla", 128), ("neg_lower", 128), ("neg_ones", 128),
                  ("inv256", 128), ("inv128", 128), ("negmask_sb", 384)]:
    BLOCK1[_name] = (_at, _at + _w)
    _at += _w
N_BLOCK1 = _at
BLOCK2 = {}
_at = 0
for _name, _w in [("perm_half", 128), ("inv128", 128), ("b_merge", 24), ("subln", 1), ("sgu_norm", 4),
                  ("lvec", 256), ("sgu_b", 512), ("sgu_wT", 512), ("w2k", 256), ("w2v", 128), ("pos", 32)]:
    BLOCK2[_name] = (_at, _at + _w)
    _at += _w
N_BLOCK2 = _at
PAR1 = {}
_at = 0
for _name, _w in [("ada_b", 72), ("norm_pre", 24), ("norm_post", 24), ("b_gate", 24), ("q_norm", 2), ("kv_norm", 1)]:
    PAR1[_name] = (_at, _at + _w)
    _at += _w
N_PAR1 = _at

N_LOADS = 3

UNIT = {"raw_full0": 16, "raw_full1": 16, "raw_full2": 16, "ada_full0": 16, "ada_full1": 16}
LAYER1 = {
    "a_ready": 22, "ada_full0": 36, "ada_full1": 36, "ada_used": 72, "arg_ready": 8, "e_ready": 16, "fills":
    37, "g_chunks": 22, "gates": 12, "gt_ready": 2, "gu_free": 22, "h_ready": 27, "hh_ready": 27, "hi_ready":
    105, "kr_ready": 1, "l_ready": 8, "lo_ready": 105, "m_free": 6, "merges": 6, "mh_ready": 1, "ml_ready": 1,
    "o_ready": 24, "p_ready": 16, "pairs": 12, "part_ready": 8, "pj_out": 37, "pt_ready": 16, "r_ready": 8,
    "raw_full0": 35, "raw_full1": 35, "raw_full2": 35, "rope_done": 9, "rot_ready": 9, "rstd_ready": 7,
    "s_ready": 16, "sil_ready": 22, "sm_ready": 16, "sp_ready": 8, "sq_ready": 26, "stat_ready": 7,
    "sum_ready": 12, "t2_ready": 27, "t_ready": 16, "tile_used": 105, "w_ready": 8, "x_ready": 12, "y_ready":
    12, "yhi_ready": 12, "z_ready": 8, "zm_ready": 8}
LAYER2 = {
    "a_ready": 11, "aux_out": 5, "aux_ready": 5, "cl_ready": 1, "cp_ready": 1, "cs_ready": 1, "ct_out": 1,
    "ct_ready": 1, "cx_ready": 1, "e_ready": 24, "fills": 32, "g_chunks": 11, "gates": 12, "gh_pre": 1,
    "gh_ready": 1, "gl_ready": 1, "gu_free": 11, "h_ready": 16, "hh_ready": 16, "hi_ready": 75, "hx_ready": 2,
    "lam_exp": 1, "lam_pre": 1, "lo_ready": 75, "m_free": 6, "merges": 6, "mh_ready": 1, "mix_done": 1,
    "ml_ready": 1, "o_ready": 20, "odt_ready": 4, "oh_ready": 4, "ol_ready": 1, "p_ready": 20, "pairs": 8,
    "part_ready": 2, "pj_out": 32, "pt_ready": 20, "raw_full0": 25, "raw_full1": 25, "raw_full2": 25,
    "rope_done": 8, "rot_ready": 8, "rstd_ready": 4, "s_ready": 24, "sg_ready": 1, "sil_ready": 11,
    "sm_ready": 24, "sq_ready": 10, "stat_ready": 4, "sum_ready": 4, "t2_ready": 16, "t_ready": 20,
    "tile_used": 75, "ug_ready": 1, "vq_ready": 1, "vr_ready": 1, "vs_ready": 1, "vsum_ready": 1, "wt_ready":
    1, "x_ready": 8, "xb32_ready": 2, "xb_ready": 2, "y_ready": 8, "yhi_ready": 4}
FFN_BODY = {"a_ready": 2, "g_chunks": 2, "gu_free": 2, "hi_ready": 6, "lo_ready": 6, "raw_full0": 2, "raw_full1": 2,
            "raw_full2": 2, "sil_ready": 2, "tile_used": 6}
ADA_BESIDE_1 = {"ada_used": 6, "ada_full0": 3, "ada_full1": 3}
ADA_BESIDE_2 = {"ada_used": 4, "ada_full0": 2, "ada_full1": 2}


class Tally:

    def __init__(self, eng, sems):
        self.eng, self.sems, self.n, self.loops = eng, sems, Counter(), []

    def value(self, name, n):
        v = n * UNIT.get(name, 1)
        for turn, per in self.loops:
            if per.get(name):
                v = turn * (per[name] * UNIT.get(name, 1)) + v
        return v

    def counts(self, name):
        self.n[name] += 1
        return self.sems[name], UNIT.get(name, 1)

    def next(self, name, k=1):
        self.n[name] += k
        return self.sems[name], self.value(name, self.n[name])

    def nth(self, name, n):
        assert n >= 1, (name, n)
        return self.sems[name], self.value(name, n)

    @contextmanager
    def loop(self, count, per):
        before = Counter(self.n)
        with self.eng.Fori(0, count) as turn:
            self.loops.append((turn, per))
            yield turn
            self.loops.pop()
        for name in set(self.n) | set(per):
            made = self.n[name] - before[name]
            assert made in (0, per.get(name, 0)), (name, made)
            if made or not self.loops:
                self.n[name] = before[name] + per.get(name, 0) * count


def build(nc, w, ada, xin, cin, posin, const_in, block1_in, par1_in, block2_in, norms2_in, out):
    ctx = ExitStack()
    with ctx:
        def sb(name, shape, dt=F32):
            return ctx.enter_context(nc.sbuf_tensor(name, [P] + list(shape), dt))

        raw = sb("raw", [RING, TW])
        whi = sb("whi", [RING, TW], F32R)
        wlo = sb("wlo", [RING, TW], F32R)
        x = sb("x", [KD, S])
        hhi = sb("hhi", [KD, S], F32R)
        hlo = sb("hlo", [KD, S], F32R)
        yhi = sb("yhi", [2, 4, S], F32R)
        ylo = sb("ylo", [2, 4, S], F32R)
        smallhi = sb("smallhi", [768], F32R)
        smalllo = sb("smalllo", [768], F32R)
        ff = sb("ff", [4, S])
        adat = sb("adat", [2, D])
        cact = sb("cact", [D])
        merged = sb("merged", [KD, S])
        set_a = sb("set_a", [20, S])
        set_b = sb("set_b", [12, S])
        bufA = sb("bufA", [2, 384])
        bufB = sb("bufB", [2, 384])
        bufC = sb("bufC", [2, 384])
        rstd = sb("rstd", [2, S])
        tables = sb("tables", [4, S])
        tables2 = sb("tables2", [2, S])
        const = sb("const", [N_CONST])
        blk = sb("blk", [max(N_BLOCK1, N_BLOCK2)])
        par1_all = sb("par1_all", [DEPTH * N_PAR1])
        par1 = sb("par1", [N_PAR1])
        norms2_all = sb("norms2_all", [DEPTH * 16])
        norms2 = sb("norms2", [16])
        final_norm = sb("final_norm", [KD])
        modc = sb("modc", [3, 24])
        modf = sb("modf", [3, 24])
        adac = sb("adac", [3])
        nmax = sb("nmax", [2, 2])
        esum = sb("esum", [2, 2])
        rsum = sb("rsum", [2, 2])
        gts = sb("gts", [2, 24])
        hidT = sb("hidT", [2, 30])
        kcT = sb("kcT", [30])
        vcm = sb("vcm", [2, HD])
        cml = sb("cml", [3, 16])
        lam = sb("lam", [8])
        gate_b = sb("gate_b", [24])
        spare = sb("spare", [1])
        ps = ctx.enter_context(nc.psum_tensor("ps", [P, 8, 512], F32))

        def c(name, rows=P):
            a, b = CONSTS[name]
            return const[0:rows, a:b]

        def c1(name):
            a, b = BLOCK1[name]
            return blk[:, a:b]

        def c2(name):
            a, b = BLOCK2[name]
            return blk[:, a:b]

        def p1(name, i=0, n=None):
            a, b = PAR1[name]
            return par1[:, a + i:a + i + n] if n else par1[:, a:b]

        sq = set_a[:, 0:8, :]
        tmp = set_a[:, 8:16, :]
        ident = c("ident")
        acc = ps[:, 0:4, :].rearrange("p b (c s) -> p (b c) s", c=2)
        stat = ps[:, 6, :].rearrange("p (c s) -> p c s", c=2)

        names = ["raw_full0", "raw_full1", "raw_full2", "hi_ready", "lo_ready", "tile_used",
                 "ada_full0", "ada_full1", "ada_used", "c_ready", "block1_over", "gt_ready", "first_used",
                 "x_ready", "sq_ready", "sum_ready", "stat_ready", "t2_ready", "hh_ready", "h_ready",
                 "sil_ready", "gu_free", "a_ready",
                 "pj_out", "rot_ready", "rope_done",
                 "s_ready", "sm_ready", "e_ready", "p_ready", "t_ready", "pt_ready", "o_ready",
                 "yhi_ready", "y_ready",
                 "z_ready", "zm_ready", "l_ready", "sp_ready", "r_ready", "arg_ready", "w_ready",
                 "kr_ready", "m_free", "mh_ready", "ml_ready",
                 "aux_ready", "aux_out", "xb_ready", "cl_ready", "cs_ready", "cx_ready", "cp_ready",
                 "ct_ready", "ct_out", "rstd_ready", "vsum_ready", "ug_ready", "vr_ready", "oh_ready", "ol_ready",
                 "vs_ready", "sg_ready", "gh_pre", "gh_ready", "gl_ready", "lam_pre", "lam_exp",
                 "ang_ready", "tab_ready", "mix_done", "part_ready",
                 "xb32_ready", "hx_ready", "vq_ready", "odt_ready", "wt_ready"]
        sems = {n: ctx.enter_context(nc.semaphore(n)) for n in names}
        s_load = ctx.enter_context(nc.semaphore("s_load"))
        s_x = ctx.enter_context(nc.semaphore("s_x"))
        s_first = [ctx.enter_context(nc.semaphore(f"s_first{i}")) for i in range(4)]
        s_c = ctx.enter_context(nc.semaphore("s_c"))
        s_const = ctx.enter_context(nc.semaphore("s_const"))
        s_pos = ctx.enter_context(nc.semaphore("s_pos"))
        s_blk1 = ctx.enter_context(nc.semaphore("s_blk1"))
        s_blk2 = ctx.enter_context(nc.semaphore("s_blk2"))
        s_final = ctx.enter_context(nc.semaphore("s_final"))
        s_out = ctx.enter_context(nc.semaphore("s_out"))
        block = ctx.enter_context(nc.Block())

        def q_moba(h, lo, hi):
            return set_a[64 * (h % 2):64 * (h % 2) + 64, h // 2, lo:hi]

        def k_moba(h, lo, hi):
            return set_a[64 * (h % 2):64 * (h % 2) + 64, 4 + h // 2, lo:hi]

        va = set_a[:, 8:12, :].rearrange("p (t c) s -> p t (c s)", t=2)
        vb = set_b[:, 8:12, :].rearrange("p (t c) s -> p t (c s)", t=2)
        vm = set_a[:, 16:20, :].rearrange("p (t c) s -> p t (c s)", t=2)

        def q_sb(h, lo, hi):
            return set_b[64 * (h % 2):64 * (h % 2) + 64, h // 2, lo:hi]

        def k_sb(h, lo, hi):
            return set_b[64 * (h % 2):64 * (h % 2) + 64, 4 + h // 2, lo:hi]

        def q_mla(h, lo, hi):
            return set_a[0:MLA_QK, h, lo:hi]

        def k_mla(h, lo, hi):
            return set_a[0:MLA_QK, 8 + h, lo:hi]

        pos_in = bufC[:, 0, 0:S].bitcast(I32)
        cq_raw = set_a[:, 12:15, :]
        kr = ff[64:96, 0, :]
        gs = ff[:, :, :]
        sil = ff[:, 0:2, :]
        a32 = ff[:, 2:4, :]
        x2 = set_a[:, 16:20, :].rearrange("p (i g) s -> p i g s", i=2)
        v_slc = set_a[:, 12:14, :]
        v_win = set_a[:, 14:16, :]

        def q_nsa(u, lo, hi):
            h = u // 2
            return set_a[64 * (h % 2):64 * (h % 2) + 64, 4 + h // 2, lo:hi]

        def k_nsa(u, lo, hi):
            h = u // 2
            return set_a[64 * (h % 2):64 * (h % 2) + 64, 8 + 2 * (u % 2) + h // 4, lo:hi]

        pcT = merged[0:N_CMP, :, :].rearrange("p a (b t) -> p (a b) t", b=2)
        od = set_a[:, 8:12, :]
        odt = set_a[:, 12:16, :]
        sq_od = set_a[:, 16:20, :]
        u_act = set_a[:, 0:4, :]
        vg = set_a[:, 4:8, :].rearrange("p (t c) s -> p t (c s)", t=2)
        hid = bufC[0:32, 0, 0:256]
        gT = bufC[0:32, 1, 0:256]
        xb32 = bufA[:, :, :].rearrange("p a b -> p (a b)")[:, 0:480]
        cmpl = bufB[:, 0, 0:240]

        first_ada = [raw[:, i // 2, (i % 2) * D:(i % 2 + 1) * D] for i in range(6)]
        first_ada += [t.rearrange("p a s -> p (a s)") for t in
                      (set_b[:, 0:4, :], set_b[:, 4:8, :], set_b[:, 8:12, :], set_a[:, 8:12, :], set_a[:, 12:16, :],
                       set_a[:, 16:20, :], merged[:, 0:4, :], merged[:, 4:8, :], ff[:, :, :])]
        first_ada += [adat[:, 1, :]]

        class Instance:

            def __init__(self, q, k, units, scale, turns, values, pair_units, rows, double_turn, fused=False):
                self.q, self.k, self.units, self.scale = q, k, units, scale
                self.turns, self.values, self.pair_units = turns, values, pair_units
                self.rows, self.double_turn, self.fused = rows, double_turn, fused

        def head_values(v, h, kb):
            return v[:, kb, HD * h:HD * h + HD]

        moba = Instance(q_moba, k_moba, 8, HD ** -0.5, 8, lambda u, kb: head_values(va, u, kb), 2,
                        lambda u: (64 * (u % 2), 64 * (u % 2) + 64), True)
        mla = Instance(q_mla, k_mla, 8, MLA_QK ** -0.5, 8, lambda u, kb: head_values(vm, u, kb), 2,
                       lambda u: (64 * (u % 2), 64 * (u % 2) + 64), False)
        nsa = Instance(q_nsa, k_nsa, 16, HD ** -0.5, 16,
                       lambda u, kb: (v_slc, v_win)[u % 2][:, kb, 128 + HD * (u // 8):128 + HD * (u // 8) + HD], 4,
                       lambda u: (64 * (u // 2 % 2), 64 * (u // 2 % 2) + 64), True)
        diff = Instance(q_sb, k_sb, 8, HD ** -0.5, 4, lambda u, kb: vb[:, kb, 128 * u:128 * u + 128], 1,
                        lambda u: (0, 128), False, fused=True)

        @block.sync
        def _(sp):
            T = Tally(sp, sems)
            sp.dma_start(cact[:, :], cin.partition_broadcast(P)).then_inc(s_c, 16)
            for i in range(0, 4):
                sp.dma_start(first_ada[i], ada[i]).then_inc(s_first[i // 4], 16)
            sp.dma_start(x[:, :, :], xin).then_inc(s_x, 16)
            for i in range(8, 12):
                sp.dma_start(first_ada[i], ada[i]).then_inc(s_first[i // 4], 16)
            for j in range(RING):
                sp.wait_ge(sems["first_used"], 2 * j + 2)
                sp.dma_start(raw[:, j, :], w[j]).then_inc(sems[f"raw_full{j}"], 16)
            with sp.Fori(0, N_TILES // RING - 1) as turn:
                for j in range(RING):
                    sp.wait_ge(sems["lo_ready"], turn * RING + j + 1)
                    sp.dma_start(raw[:, j, :], w[bass.ds(turn * RING + (RING + j), 1), :, :]
                                 .rearrange("a p n -> p (a n)")).then_inc(sems[f"raw_full{j}"], 16)
            sp.wait_ge(s_final, 1)
            sp.dma_start(out, tmp).then_inc(s_out, 16)
            sp.wait_ge(s_out, 16)

        @block.tensor
        def _(pe):
            T = Tally(pe, sems)
            mm = nc.tensor.matmul
            free6 = [None]
            fresh_h = [False]

            def blocks(out_ap, pairs, start=True, stop=True, skip=False):
                last = None
                for i, (sh, sl, mh, ml) in enumerate(pairs):
                    first, end = i == 0, i == len(pairs) - 1
                    mm(out_ap, sh, mh, start=start and first, stop=False, skip_group_check=skip)
                    mm(out_ap, sh, ml, start=False, stop=False, skip_group_check=skip)
                    last = mm(out_ap, sl, mh, start=False, stop=stop and end, skip_group_check=skip)
                return last

            def tile():
                slot = T.n["lo_ready"] % RING
                pe.wait_ge(*T.next("lo_ready"))
                return slot

            def wait_bank6():
                if free6[0]:
                    pe.wait_ge(*T.nth(*free6[0]))

            def open_fill():
                k = T.n["fills"]
                T.n["fills"] += 1
                if k >= 2:
                    pe.wait_ge(*T.nth("pj_out", k - 1))
                return 4 + k % 2

            def features(bank, slot, width=256, nk=KD, chunks=2):
                for i in range(chunks):
                    if fresh_h[0] and i == 0:
                        for k in range(KD):
                            pe.wait_ge(*T.next("h_ready"))
                            blocks(ps[:, bank, 0:S],
                                   [(whi[:, slot, k * width:k * width + P], wlo[:, slot, k * width:k * width + P],
                                     hhi[:, k, :], hlo[:, k, :])], start=(k == 0), stop=(k == KD - 1))
                        fresh_h[0] = False
                        continue
                    last = blocks(ps[:, bank, i * S:(i + 1) * S],
                                  [(whi[:, slot, k * width + i * P:k * width + (i + 1) * P],
                                    wlo[:, slot, k * width + i * P:k * width + (i + 1) * P],
                                    hhi[:, k, :], hlo[:, k, :]) for k in range(nk)])
                return last

            def tokens(bank, slot):
                for t in range(2):
                    last = blocks(ps[:, bank, t * S:(t + 1) * S],
                                  [(hhi[:, k, t * P:(t + 1) * P], hlo[:, k, t * P:(t + 1) * P],
                                    whi[:, slot, k * S:(k + 1) * S], wlo[:, slot, k * S:(k + 1) * S])
                                   for k in range(KD)])
                return last

            def project(kind):
                slot = tile()
                bank = open_fill()
                last = features(bank, slot) if kind == "features" else tokens(bank, slot)
                last.then_inc(*T.counts("tile_used"))

            def mean():
                T.n["sq_ready"] += 4
                for i in range(4):
                    if i % 2 == 0:
                        pe.wait_ge(*T.next("sum_ready"))
                    last = mm(stat[:, 0, :], c("inv1024"), sq[:, i // 2 * 4 + i % 2, :], start=(i == 0), stop=(i == 3))
                last.then_inc(*T.counts("stat_ready"))

            def wait_h(n):
                pe.wait_ge(*T.next("h_ready", n))

            def rotate(perm, src, out_ap):
                wait_bank6()
                k = T.n["rot_ready"]
                if k >= 1:
                    pe.wait_ge(*T.nth("rope_done", k))
                mm(out_ap, perm, src, start=True, stop=True).then_inc(*T.counts("rot_ready"))
                free6[0] = ("rope_done", T.n["rot_ready"])

            def aux(emit):
                wait_bank6()
                emit().then_inc(*T.counts("aux_ready"))
                free6[0] = ("aux_out", T.n["aux_ready"])

            def scores(ins, u):
                k = T.n["s_ready"]
                if u >= 2:
                    pe.wait_ge(*T.nth("sm_ready", k - 1))
                bank = k % 2
                mm(ps[:, bank, 0:128], ins.q(u, 0, 128), ins.k(u, 0, 128), start=True, stop=True)
                mm(ps[:, bank, 128:384], ins.q(u, 128, 256), ins.k(u, 0, 256), start=True, stop=True)\
                    .then_inc(*T.counts("s_ready"))

            def turn(ins, u):
                k = T.n["t_ready"]
                pe.wait_ge(*T.next("p_ready"))
                back = 1 if ins.double_turn else 0
                if u > back:
                    pe.wait_ge(*T.nth("pt_ready", k - back))
                bank = 7 if ins.double_turn and u % 2 else 2
                src = bufB[:, 0 if ins.fused else u % 2, :]
                for i in range(3):
                    last = nc.tensor.transpose(ps[:, bank, i * P:(i + 1) * P], src[:, i * P:(i + 1) * P], ident)
                last.then_inc(*T.counts("t_ready"))

            def weigh(ins, u, before=None):
                per = ins.pair_units
                if u % per == 0:
                    k = T.n["pairs"]
                    T.n["pairs"] += 1
                    if k >= 1:
                        pe.wait_ge(*T.nth("y_ready", k))
                pe.wait_ge(*T.next("pt_ready"))
                a, b = ins.rows(u)
                o = ps[a:b, 3, 0:S]
                pT = bufC[:, u % 2, :]
                first = True
                if before:
                    before(o)
                    first = False
                if per == 4 and u % 2:
                    first = False
                mm(o, ins.values(u, 0), pT[:, 0:256], start=first, stop=False, skip_group_check=True)
                mm(o[:, 128:256], ins.values(u, 1), pT[:, 256:384], start=False, stop=True, skip_group_check=True)\
                    .then_inc(*T.counts("o_ready"))

            def attend(ins, beside, before=lambda u: None):
                for s in range(ins.units + (2 if ins.fused else 3)):
                    if s < ins.units:
                        scores(ins, s)
                    if not ins.fused:
                        if 2 <= s <= ins.units + 1:
                            turn(ins, s - 2)
                        if s >= 3:
                            weigh(ins, s - 3, before(s - 3))
                    beside(s)
                    if ins.fused:
                        if 1 <= s <= ins.units and s % 2 == 0:
                            turn(ins, s // 2 - 1)
                        if s >= 3 and s % 2:
                            weigh(ins, s // 2 - 1)

            def sticks(beside):
                for s in range(HEADS + 3):
                    if s < HEADS:
                        k = T.n["z_ready"]
                        if s >= 2:
                            pe.wait_ge(*T.nth("zm_ready", k - 1))
                        mm(ps[:, k % 2, 0:256], k_sb(s, 0, 128), q_sb(s, 0, 256), start=True, stop=True)
                        mm(ps[:, k % 2, 256:384], k_sb(s, 128, 256), q_sb(s, 128, 256), start=True, stop=True)\
                            .then_inc(*T.counts("z_ready"))
                    beside(s)
                    if 1 <= s <= HEADS:
                        u = s - 1
                        pe.wait_ge(*T.next("sp_ready"))
                        if u >= 1:
                            pe.wait_ge(*T.nth("arg_ready", T.n["r_ready"]))
                        sp_ = bufB[:, u % 2, :]
                        mm(ps[:, 2, 0:256], c1("neg_lower"), sp_[:, 0:256], start=True, stop=False,
                           skip_group_check=True)
                        mm(ps[:, 2, 128:256], c1("neg_ones"), sp_[:, 256:384], start=False, stop=True,
                           skip_group_check=True)
                        mm(ps[:, 2, 256:384], c1("neg_lower"), sp_[:, 256:384], start=True, stop=True,
                           skip_group_check=True).then_inc(*T.counts("r_ready"))
                    if s >= 3:
                        u = s - 3
                        if u % 2 == 0:
                            k = T.n["pairs"]
                            T.n["pairs"] += 1
                            if k >= 1:
                                pe.wait_ge(*T.nth("y_ready", k))
                        pe.wait_ge(*T.next("w_ready"))
                        a = HD * (u % 2)
                        o = ps[a:a + HD, 3, 0:S]
                        mm(o, vb[:, 0, HD * u:HD * u + HD], bufC[:, u % 2, 0:256], start=True, stop=False,
                           skip_group_check=True)
                        mm(o[:, 128:256], vb[:, 1, HD * u:HD * u + HD], bufC[:, u % 2, 256:384], start=False,
                           stop=True, skip_group_check=True).then_inc(*T.counts("o_ready"))

            def merge_gate():
                project("features")

            def merge_branch(n):
                slot = tile()
                k = T.n["merges"]
                T.n["merges"] += 1
                if k >= 1:
                    pe.wait_ge(*T.nth("m_free", k))
                for i in range(4):
                    last = blocks(ps[:, 6 + i // 2, (i % 2) * S:(i % 2 + 1) * S],
                                  [(whi[:, slot, kk * 512 + i * P:kk * 512 + (i + 1) * P],
                                    wlo[:, slot, kk * 512 + i * P:kk * 512 + (i + 1) * P],
                                    yhi[:, n % 2, kk, :], ylo[:, n % 2, kk, :]) for kk in range(4)])
                last.then_inc(*T.counts("tile_used"))
                free6[0] = ("m_free", T.n["merges"])

            def wait_pairs():
                pe.wait_ge(*T.nth("y_ready", T.n["pairs"]))

            def output_projection():
                for i in range(4):
                    slot = tile()
                    if i == 0:
                        pe.wait_ge(*T.next("ml_ready"))
                    for j in range(2):
                        last = blocks(acc[:, 2 * i + j, :],
                                      [(whi[:, slot, k * 256 + j * P:k * 256 + (j + 1) * P],
                                        wlo[:, slot, k * 256 + j * P:k * 256 + (j + 1) * P],
                                        hhi[:, k, :], hlo[:, k, :]) for k in range(KD)])
                    last.then_inc(*T.counts("tile_used"))

            def gate_up():
                if T.n["g_chunks"] >= 1:
                    pe.wait_ge(*T.nth("gu_free", T.n["g_chunks"]))
                T.n["g_chunks"] += 1
                for bank in (4, 5):
                    slot = tile()
                    features(bank, slot).then_inc(*T.counts("tile_used"))

            def down(parity, first=False, end=False):
                slot = tile()
                pe.wait_ge(*T.next("a_ready"))
                for m in range(KD):
                    last = blocks(acc[:, m, :],
                                  [(whi[:, slot, cc * D + m * P:cc * D + (m + 1) * P],
                                    wlo[:, slot, cc * D + m * P:cc * D + (m + 1) * P],
                                    yhi[:, parity, cc, :], ylo[:, parity, cc, :]) for cc in range(2)],
                                  start=first and m % 2 == 0, stop=end, skip=True)
                last.then_inc(*T.counts("tile_used"))

            def ffn():
                gate_up()
                gate_up()
                down(0, first=True)
                with T.loop((NJ - 3) // 2, FFN_BODY):
                    for parity in (1, 0):
                        gate_up()
                        down(parity)
                gate_up()
                down(1)
                down(0, end=True)

            pe.wait_ge(s_const, 16)
            pe.wait_ge(s_blk1, 32)
            mean()
            with T.loop(DEPTH, LAYER1):
                fresh_h[0] = True
                ffn()
                mean()
                mean()
                fresh_h[0] = True
                free6[0] = None
                for i in range(4):
                    project("features")
                    if i:
                        pe.wait_ge(*T.nth("pj_out", T.n["fills"] - 1))
                        rotate(c1("perm_moba"), set_a[:, 2 * i - 2:2 * i, :], ps[:, 6, :])
                project("tokens")
                pe.wait_ge(*T.nth("pj_out", T.n["fills"] - 1))
                rotate(c1("perm_moba"), set_a[:, 6:8, :], ps[:, 6, :])
                project("tokens")
                pe.wait_ge(*T.nth("pj_out", T.n["fills"]))
                pe.wait_ge(*T.nth("rope_done", T.n["rot_ready"]))

                def beside_moba(s):
                    if s < 4:
                        project("features")
                    elif s < 6:
                        project("tokens")
                    elif s == 6:
                        project("features")
                    elif s == 7:
                        slot = tile()
                        features(open_fill(), slot, width=128, chunks=1).then_inc(*T.counts("tile_used"))

                attend(moba, beside_moba)
                pe.wait_ge(*T.nth("pj_out", T.n["fills"]))

                def beside_sticks(s):
                    if s == 0:
                        slot = tile()
                        bank = open_fill()
                        blocks(ps[0:96, bank, 0:S], [(whi[:, slot, k * 96:(k + 1) * 96],
                                                      wlo[:, slot, k * 96:(k + 1) * 96],
                                                      hhi[:, k, :], hlo[:, k, :]) for k in range(KD)])\
                            .then_inc(*T.counts("tile_used"))
                        wait_bank6()
                        pe.wait_ge(*T.next("sq_ready", 2))
                        mm(stat[:, 0, :], c1("inv256"), sq[:, 0, :], start=True, stop=False)
                        mm(stat[:, 0, :], c1("inv256"), sq[:, 1, :], start=False, stop=True)
                        mm(stat[:, 1, :], c1("inv128"), sq[:, 2, :], start=True, stop=True)\
                            .then_inc(*T.counts("stat_ready"))
                        free6[0] = None
                    elif s == 1:
                        slot = tile()
                        wait_h(3)
                        for i in range(4):
                            bank = open_fill()
                            for j in range(2):
                                col = (2 * i + j) * MLA_QK
                                last = blocks(ps[0:96, bank, j * S:(j + 1) * S],
                                              [(whi[:, slot, k * 768 + col:k * 768 + col + MLA_QK],
                                                wlo[:, slot, k * 768 + col:k * 768 + col + MLA_QK],
                                                smallhi[:, k * S:(k + 1) * S], smalllo[:, k * S:(k + 1) * S])
                                               for k in range(2)])
                            last.then_inc(*T.counts("tile_used" if i == 3 else "part_ready"))
                        pe.wait_ge(*T.nth("pj_out", T.n["fills"] - 4))
                        rotate(c1("perm_mla")[64:96, 64:128], kr, ps[64:128, 6, 0:S])
                    elif s == 2:
                        slot = tile()
                        for i in range(4):
                            bank = open_fill()
                            for j in range(2):
                                col = (2 * i + j) * P
                                last = blocks(ps[:, bank, j * S:(j + 1) * S],
                                              [(whi[:, slot, col:col + P], wlo[:, slot, col:col + P],
                                                smallhi[:, 512:768], smalllo[:, 512:768])])
                            last.then_inc(*T.counts("part_ready"))
                        for t in range(2):
                            bank = open_fill()
                            wv = [w_[:, slot, 0:1024].rearrange("p (h c) -> p h c", c=P)[:, :, HD:P]
                                  for w_ in (whi, wlo)]
                            last = blocks(ps[:, bank, :],
                                          [(smallhi[:, 512 + t * P:512 + (t + 1) * P],
                                            smalllo[:, 512 + t * P:512 + (t + 1) * P], wv[0], wv[1])])
                            last.then_inc(*T.counts("tile_used" if t == 1 else "part_ready"))
                        for i in range(4):
                            rotate(c1("perm_mla")[64:96, 64:128], set_a[64:96, 2 * i:2 * i + 2, :], ps[64:128, 6, :])
                    elif s < 9:
                        if s % 3 == 2:
                            if s == 5:
                                wait_bank6()
                            merge_branch(0)
                        else:
                            merge_gate()

                sticks(beside_sticks)
                wait_pairs()
                pe.wait_ge(*T.nth("pj_out", T.n["fills"]))
                pe.wait_ge(*T.nth("rope_done", T.n["rot_ready"]))
                pe.wait_ge(*T.next("kr_ready"))

                def beside_mla(s):
                    if s < 6:
                        if s % 3 == 2:
                            merge_branch(1)
                        else:
                            merge_gate()

                attend(mla, beside_mla)
                for half in range(2):
                    merge_gate()
                    merge_gate()
                    if half == 0:
                        wait_pairs()
                    merge_branch(2)
                output_projection()
                wait_bank6()
                free6[0] = None
                mean()
                mean()
                fresh_h[0] = True
                ffn()
                mean()
                mean()

            with T.loop(DEPTH, LAYER2) as layer:
                fresh_h[0] = True
                pe.wait_ge(s_blk2, layer * 16 + 16)
                free6[0] = None
                project("features")
                project("features")
                pe.wait_ge(*T.nth("pj_out", T.n["fills"] - 1))
                rotate(c2("perm_half"), set_a[:, 0:2, :], ps[:, 6, :])
                project("features")
                pe.wait_ge(*T.nth("pj_out", T.n["fills"] - 1))
                rotate(c2("perm_half"), set_a[:, 2:4, :], ps[:, 6, :])
                for i in range(2):
                    slot = tile()
                    features(open_fill(), slot, chunks=1).then_inc(*T.counts("part_ready"))
                    tokens(open_fill(), slot).then_inc(*T.counts("tile_used"))
                    pe.wait_ge(*T.nth("pj_out", T.n["fills"] - 1))
                    rotate(c2("perm_half"), set_a[:, 8 + 2 * i:10 + 2 * i, :], ps[:, 6, :])
                slot = tile()
                features(open_fill(), slot, width=128, chunks=1).then_inc(*T.counts("tile_used"))
                pe.wait_ge(*T.nth("pj_out", T.n["fills"]))

                def gates_by_token():
                    for t in range(2):
                        last = mm(ps[:, 6, t * 32:t * 32 + 24], gT[0:24, t * P:(t + 1) * P],
                                  c("ident", 24)[:, 0:24], start=True, stop=True)
                    return last

                aux(gates_by_token)
                for kind in range(2):
                    pe.wait_ge(*T.next("xb_ready"))
                    bank = open_fill()
                    for i in range(2):
                        slot = tile()
                        last = blocks(ps[:, bank, 0:S],
                                      [(smallhi[:, (8 * i + k) * 30:(8 * i + k) * 30 + P],
                                        smalllo[:, (8 * i + k) * 30:(8 * i + k) * 30 + P],
                                        whi[:, slot, k * S:(k + 1) * S], wlo[:, slot, k * S:(k + 1) * S])
                                       for k in range(8)], start=(i == 0), stop=(i == 1))
                        last.then_inc(*T.counts("tile_used"))
                    pe.wait_ge(*T.nth("pj_out", T.n["fills"]))

                    def hidden_by_feature():
                        for k in range(2):
                            last = mm(ps[:, 6, k * 32:k * 32 + 30], hid[0:30, k * P:(k + 1) * P],
                                      c("ident", 30)[:, 0:30], start=True, stop=True)
                        return last

                    aux(hidden_by_feature)
                    pe.wait_ge(*T.nth("aux_out", T.n["aux_ready"]))

                    def second_layer():
                        if kind == 0:
                            for k in range(2):
                                last = mm(ps[:, 6, 0:30], c2("w2k")[:, k * P:(k + 1) * P], hidT[:, k, :],
                                          start=(k == 0), stop=(k == 1))
                            return last
                        for g in range(G):
                            for k in range(2):
                                last = mm(ps[0:N_CMP, 6, g * HD:(g + 1) * HD], hidT[:, k, g * N_CMP:(g + 1) * N_CMP],
                                          c2("w2v")[:, k * HD:(k + 1) * HD], start=(k == 0), stop=(k == 1))
                        return last

                    aux(second_layer)
                pe.wait_ge(*T.nth("aux_out", T.n["aux_ready"]))
                for h in range(HEADS):
                    a = HD * (h % 2)
                    for t in range(2):
                        col = (h - h % 2 + t) * N_CMP
                        last = mm(ps[:, 6 + h % 2, col:col + N_CMP], set_a[a:a + HD, h // 2, t * P:(t + 1) * P],
                                  kcT[a:a + HD, (h // 4) * N_CMP:(h // 4 + 1) * N_CMP], start=True, stop=True)
                last.then_inc(*T.counts("cl_ready"))
                pe.wait_ge(*T.next("cp_ready"))
                for h in range(HEADS):
                    for t in range(2):
                        i = 2 * h + t
                        last = nc.tensor.transpose(ps[0:N_CMP, i // 4, (i % 4) * P:(i % 4 + 1) * P],
                                                   cmpl[:, i * N_CMP:(i + 1) * N_CMP], ident)
                last.then_inc(*T.counts("ct_ready"))
                pe.wait_ge(*T.next("ct_out"))
                pe.wait_ge(*T.nth("pj_out", T.n["fills"]))
                pe.wait_ge(*T.nth("rope_done", T.n["rot_ready"]))

                def beside_nsa(s):
                    if s in (1, 3, 5, 7):
                        project("features")
                    elif s in (9, 11):
                        project("tokens")

                def compressed(u):
                    if u % 2:
                        return None
                    h = u // 2
                    return lambda o: mm(o, vcm[0:N_CMP, h // 4, :], pcT[:, 2 * h:2 * h + 2, :]
                                        .rearrange("p a t -> p (a t)"), start=True, stop=False,
                                        skip_group_check=True)

                attend(nsa, beside_nsa, compressed)
                pe.wait_ge(*T.nth("pj_out", T.n["fills"]))
                for i in range(4):
                    rotate(c2("perm_half"), set_b[:, 2 * i:2 * i + 2, :], ps[:, 6, :])
                wait_pairs()
                pe.wait_ge(*T.nth("rope_done", T.n["rot_ready"]))

                def beside_diff(s):
                    if s < 2:
                        project("features")
                    elif s < 4:
                        project("tokens")
                    elif s < 10:
                        if (s - 4) % 3 == 2:
                            if s == 6:
                                wait_bank6()
                            merge_branch(0)
                        else:
                            merge_gate()

                attend(diff, beside_diff)
                wait_bank6()
                for i in range(2):
                    pe.wait_ge(*T.next("sq_ready"))
                    if i:
                        pe.wait_ge(*T.nth("rstd_ready", T.n["stat_ready"]))
                    for j in range(2):
                        last = mm(stat[:, j, :], c2("inv128"), sq_od[:, 2 * i + j, :], start=True, stop=True)
                    last.then_inc(*T.counts("stat_ready"))
                pe.wait_ge(*T.next("vs_ready"))
                pe.wait_ge(*T.next("wt_ready"))
                for g in range(4):
                    for n in range(2):
                        last = mm(ps[:, g // 2, (g % 2) * S + n * P:(g % 2) * S + (n + 1) * P],
                                  vg[:, n, g * P:(g + 1) * P], c2("sgu_wT")[:, g * P:(g + 1) * P],
                                  start=True, stop=True)
                last.then_inc(*T.counts("sg_ready"))
                pe.wait_ge(*T.next("ol_ready"))
                free6[0] = None
                for n in (1, 2):
                    for half in range(2):
                        merge_gate()
                        merge_gate()
                        if n == 2 and half == 0:
                            pe.wait_ge(*T.next("gl_ready"))
                        merge_branch(n)
                output_projection()
                wait_bank6()
                free6[0] = None
                mean()
                fresh_h[0] = True
                ffn()
                mean()

        @block.scalar
        def _(act):
            T = Tally(act, sems)
            A = nc.scalar.activation

            def split_high():
                k = T.n["hi_ready"]
                slot = k % RING
                act.wait_ge(*T.next(f"raw_full{slot}"))
                if k - (RING - 1) >= 1:
                    act.wait_ge(*T.nth("tile_used", k - (RING - 1)))
                A(whi[:, slot, :], raw[:, slot, :], ACT.Copy).then_inc(*T.counts("hi_ready"))

            def split_ahead():
                if T.n["hi_ready"] < T.n["tile_used"] + RING:
                    split_high()

            def tile_done(wait=True):
                split_ahead()
                if wait:
                    act.wait_ge(*T.next("tile_used"))
                else:
                    T.n["tile_used"] += 1

            def last_tile_done(more, wait):
                if more is None:
                    split_ahead()
                else:
                    with act.If(more):
                        split_ahead()
                tile_done(wait)

            def taken(rows=P):
                bank = 4 + T.n["pj_out"] % 2
                return ps[0:rows, bank, :]

            def take(dst, scale=1.0, rows=P):
                A(dst, taken(rows).rearrange("p (a s) -> p a s", a=2) if len(dst.shape) == 3 else taken(rows),
                  ACT.Copy, scale=scale).then_inc(*T.counts("pj_out"))

            def squares(src, n, ready, dst=None):
                for j in range(n // 2):
                    if ready:
                        act.wait_ge(*T.next(ready))
                    A((sq if dst is None else dst)[:, 2 * j:2 * j + 2, :], src[:, 2 * j:2 * j + 2, :], ACT.Square)\
                        .then_inc(*T.counts("sq_ready"))

            def use_ln_exp():
                act.preload_act_table_set("natural_log_exp_and_others")

            def use_exp_tanh():
                act.preload_act_table_set("exp_and_others")

            def root(n=1):
                act.wait_ge(*T.next("stat_ready"))
                A(rstd[:, 0:n, :], stat[:, 0:n, :], ACT.Ln, bias=c("eps"))
                act.drain()
                A(rstd[:, 0:n, :], rstd[:, 0:n, :], ACT.Exp, scale=-0.5).then_inc(*T.counts("rstd_ready"))

            def high_parts(shift=None):
                for m in range(KD):
                    act.wait_ge(*T.next("t2_ready"))
                    if shift is None:
                        A(hhi[:, m, :], tmp[:, m, :], ACT.Copy).then_inc(*T.counts("hh_ready"))
                    else:
                        A(hhi[:, m, :], tmp[:, m, :], ACT.Identity, bias=modf[:, shift, m:m + 1])\
                            .then_inc(*T.counts("hh_ready"))

            def pair_taken(dst, n_units):
                T.n["o_ready"] += n_units
                act.wait_ge(*T.nth("o_ready", T.n["o_ready"]))
                A(dst, ps[:, 3, 0:S], ACT.Copy).then_inc(*T.counts("yhi_ready"))

            def exps(ins, u, t0):
                act.wait_ge(*T.next("sm_ready"))
                if u >= 2:
                    act.wait_ge(*T.nth("t_ready", t0 + (u // 2 if ins.fused else u - 1)))
                for i, (a, b) in enumerate(((0, 128), (128, 384))):
                    last = A(bufB[:, u % 2, a:b], bufA[:, u % 2, a:b], ACT.Exp, bias=nmax[:, u % 2, i:i + 1],
                             scale=-1.0, accum_out=esum[:, u % 2, i:i + 1])
                last.then_inc(*T.counts("e_ready"))

            def turned(ins, u, o0):
                act.wait_ge(*T.next("t_ready"))
                if u >= 2:
                    act.wait_ge(*T.nth("o_ready", o0 + u - 1))
                bank = 7 if ins.double_turn and u % 2 else 2
                A(bufC[:, u % 2, :], ps[:, bank, 0:384], ACT.Copy).then_inc(*T.counts("pt_ready"))

            def attend(ins, n, beside):
                t0, o0 = T.n["t_ready"], T.n["o_ready"]
                for s in range(ins.units + (2 if ins.fused else 3)):
                    split_ahead()
                    if s < ins.units:
                        exps(ins, s, t0)
                    if not ins.fused:
                        if 2 <= s <= ins.units + 1:
                            turned(ins, s - 2, o0)
                        if s >= 3 and (s - 2) % ins.pair_units == 0:
                            pair_taken(yhi[:, n % 2, (s - 3) // ins.pair_units, :], ins.pair_units)
                    beside(s)
                    if ins.fused:
                        if 1 <= s <= ins.units and s % 2 == 0:
                            turned(ins, s // 2 - 1, o0)

            def sticks(n, beside):
                r0, o0 = T.n["r_ready"], T.n["o_ready"]
                for s in range(HEADS + 3):
                    split_ahead()
                    if 2 <= s <= HEADS + 1:
                        u = s - 2
                        act.wait_ge(*T.next("arg_ready"))
                        if u >= 2:
                            act.wait_ge(*T.nth("o_ready", o0 + u - 1))
                        A(bufC[:, u % 2, :], bufA[:, u % 2, :], ACT.Exp).then_inc(*T.counts("w_ready"))
                    if s < HEADS:
                        act.wait_ge(*T.next("zm_ready"))
                        if s >= 2:
                            act.wait_ge(*T.nth("r_ready", r0 + s - 1))
                        l = bufB[:, s % 2, :]
                        A(l, bufA[:, s % 2, :], ACT.Abs)
                        act.drain()
                        A(l, l, ACT.Exp, scale=-1.0)
                        act.drain()
                        A(l, l, ACT.Ln, bias=1.0).then_inc(*T.counts("l_ready"))
                    beside(s)
                    if s >= 3 and s % 2 == 0:
                        pair_taken(yhi[:, n % 2, (s - 4) // 2, :], 2)
                T.n["r_ready"] += HEADS

            def gate(i, columns, later):
                tile_done()
                if T.n["gates"] >= 2 and i == 0:
                    act.wait_ge(*T.nth("m_free", T.n["gates"] // 2))
                T.n["gates"] += 1
                bank = taken()
                for j in range(2):
                    last = A(gs[:, 2 * i + j, :], bank[:, j * S:(j + 1) * S], ACT.Identity if later else ACT.Tanh,
                             scale=0.5, bias=columns[:, j:j + 1])
                last.then_inc(*T.counts("pj_out"))

            def merge_step(k, n, half, later=False):
                if k < 2:
                    c0 = n * KD + 4 * half + 2 * k
                    gate(k, gate_b[:, c0:c0 + 2], later)
                else:
                    tile_done(False)
                    if later:
                        act.drain()
                        A(gs[:, :, :], gs[:, :, :], ACT.Tanh).then_inc(*T.counts("gt_ready"))
                        use_ln_exp()

            def merged_parts():
                act.wait_ge(*T.nth("m_free", T.n["gates"] // 2))
                A(hhi[:, :, :], merged[:, :, :], ACT.Copy, scale=0.5).then_inc(*T.counts("mh_ready"))

            def output_projection():
                for i in range(4):
                    tile_done(wait=(i == 3))

            def ffn(more=None):
                def gate_up():
                    tile_done()
                    if T.n["sil_ready"] >= 1:
                        act.wait_ge(*T.nth("gu_free", T.n["sil_ready"]))
                    A(sil, ps[:, 4, :].rearrange("p (c s) -> p c s", c=2), ACT.Silu)\
                        .then_inc(*T.counts("sil_ready"))
                    tile_done(False)

                gate_up()
                gate_up()
                tile_done(False)
                with T.loop((NJ - 3) // 2, FFN_BODY):
                    for _ in range(2):
                        gate_up()
                        tile_done(False)
                gate_up()
                use_ln_exp()
                last_tile_done(more, False)
                last_tile_done(more, True)

            act.dma_start(pos_in, posin.partition_broadcast(P)).then_inc(s_pos, 16)
            act.dma_start(const[:, :], const_in).then_inc(s_const, 16)
            for i in (*range(4, 8), *range(12, 16)):
                act.dma_start(first_ada[i], ada[i]).then_inc(s_first[i // 4], 16)
            act.wait_ge(s_const, 16)
            act.wait_ge(s_c, 16)
            A(cact[:, :], cact[:, :], ACT.Silu).then_inc(*T.counts("c_ready"))
            act.wait_ge(*T.next("ang_ready"))
            A(tables2[:, :, :], tables2[:, :, :], ACT.Sin).then_inc(*T.counts("tab_ready"))
            use_ln_exp()
            squares(x, KD, "x_ready")
            root()
            split_high()
            split_high()
            with T.loop(DEPTH, LAYER1):
                high_parts(0)
                ffn()
                squares(acc, KD, None)
                root()
                squares(x, KD, "x_ready")
                root()
                high_parts(1)
                for i in range(4):
                    tile_done()
                    take(set_a[:, 2 * i:2 * i + 2, :])
                for i in range(2):
                    tile_done()
                    take(va[:, :, i * S:(i + 1) * S])

                def beside_moba(s):
                    if s >= 8:
                        return
                    tile_done()
                    if s < 4:
                        take(set_b[:, 2 * s:2 * s + 2, :], scale=HD ** -0.5 if s < 2 else 1.0)
                    elif s < 6:
                        take(vb[:, :, (s - 4) * S:(s - 3) * S])
                    elif s == 6:
                        take(cq_raw[:, 0:2, :])
                    else:
                        A(cq_raw[:, 2, :], taken()[:, 0:S], ACT.Copy).then_inc(*T.counts("pj_out"))

                attend(moba, 0, beside_moba)

                def beside_sticks(s):
                    if s == 0:
                        A(sq[:, 0:2, :], cq_raw[:, 0:2, :], ACT.Square).then_inc(*T.counts("sq_ready"))
                        A(sq[:, 2, :], cq_raw[:, 2, :], ACT.Square).then_inc(*T.counts("sq_ready"))
                        root(2)
                        tile_done()
                        A(kr, ps[64:96, 4 + T.n["pj_out"] % 2, 0:S], ACT.Copy).then_inc(*T.counts("pj_out"))
                        for i in range(3):
                            act.wait_ge(*T.next("t2_ready"))
                            A(smallhi[:, i * S:(i + 1) * S], set_a[:, 4 + i, :], ACT.Copy)\
                                .then_inc(*T.counts("hh_ready"))
                    elif s == 1:
                        for i in range(4):
                            if i < 3:
                                act.wait_ge(*T.next("part_ready"))
                            else:
                                tile_done()
                            take(set_a[0:96, 2 * i:2 * i + 2, :], rows=96)
                    elif s == 2:
                        for i in range(4):
                            act.wait_ge(*T.next("part_ready"))
                            take(set_a[0:64, 8 + 2 * i:10 + 2 * i, :], rows=64)
                        act.wait_ge(*T.next("part_ready"))
                        take(vm[:, 0, :])
                        tile_done()
                        take(vm[:, 1, :])
                        act.wait_ge(*T.next("kr_ready"))
                    elif s < 9:
                        merge_step(s % 3, 0, s // 6, True)

                sticks(1, beside_sticks)

                def beside_mla(s):
                    if s < 6:
                        merge_step(s % 3, 1, s // 3)

                use_exp_tanh()
                attend(mla, 2, beside_mla)
                for half in range(2):
                    for k in range(3):
                        merge_step(k, 2, half)
                merged_parts()
                use_ln_exp()
                output_projection()
                squares(acc, KD, None)
                root()
                squares(x, KD, "x_ready")
                root()
                high_parts(2)
                ffn()
                squares(acc, KD, None)
                root()
                squares(x, KD, "x_ready")
                root()

            with T.loop(DEPTH, LAYER2) as layer:
                high_parts()
                act.wait_ge(s_blk2, layer * 16 + 16)
                act.wait_ge(*T.next("lam_pre"))
                A(lam[:, 2:4], lam[:, 0:2], ACT.Exp).then_inc(*T.counts("lam_exp"))
                use_exp_tanh()
                for i in range(2):
                    tile_done()
                    take(set_a[:, 2 * i:2 * i + 2, :])
                tile_done()
                bank = taken()
                for i in range(2):
                    for g in range(G):
                        A(x2[0:64, i, g, :], bank[64 * g:64 * g + 64, i * S:(i + 1) * S], ACT.Copy)
                        last = A(x2[64:128, i, g, 0:255], bank[64 * g:64 * g + 64, i * S + 1:(i + 1) * S], ACT.Copy)
                last.then_inc(*T.counts("pj_out"))
                for i in range(2):
                    act.wait_ge(*T.next("part_ready"))
                    bank = taken()
                    for g in range(G):
                        for half in range(2):
                            last = A(set_a[64 * half:64 * half + 64, 8 + 2 * i + g, :],
                                     bank[64 * g:64 * g + 64, 0:S], ACT.Copy)
                    last.then_inc(*T.counts("pj_out"))
                    tile_done()
                    take((v_slc, v_win)[i])
                tile_done()
                A(gT[0:24, :], taken(24)[:, 0:S], ACT.Tanh, scale=0.5).then_inc(*T.counts("pj_out"))

                def aux(dst, src):
                    act.wait_ge(*T.next("aux_ready"))
                    A(dst, src, ACT.Copy).then_inc(*T.counts("aux_out"))

                bank6 = ps[:, 6, 0:64].rearrange("p (a b) -> p a b", a=2)
                aux(gts[:, :, :], bank6[:, :, 0:24])
                for kind in range(2):
                    act.wait_ge(*T.next("xb32_ready"))
                    A(smallhi[:, 0:480], xb32, ACT.Copy).then_inc(*T.counts("hx_ready"))
                    tile_done(False)
                    tile_done()
                    A(hid[0:30, :], taken(30)[:, 0:S], ACT.Gelu_apprx_tanh).then_inc(*T.counts("pj_out"))
                    aux(hidT[:, :, :], bank6[:, :, 0:30])
                    if kind == 0:
                        aux(kcT[:, :], ps[:, 6, 0:30])
                    else:
                        aux(vcm[0:N_CMP, :, :], ps[0:N_CMP, 6, 0:128].rearrange("p (g d) -> p g d", g=G))
                use_exp_tanh()
                act.wait_ge(*T.next("cs_ready"))
                A(cmpl, cmpl, ACT.Exp).then_inc(*T.counts("cx_ready"))
                act.wait_ge(*T.next("ct_ready"))
                A(merged[0:N_CMP, :, :].rearrange("p a b -> p (a b)"), ps[0:N_CMP, 0:4, :].rearrange("p a b -> p (a b)"),
                  ACT.Copy).then_inc(*T.counts("ct_out"))

                def beside_nsa(s):
                    if s in (1, 3, 5, 7):
                        tile_done()
                        take(set_b[:, s - 1:s + 1, :])
                    elif s in (9, 11):
                        tile_done()
                        take(vb[:, :, (s - 9) * 128:(s - 9) * 128 + S])

                attend(nsa, 0, beside_nsa)

                def beside_diff(s):
                    if s < 2:
                        tile_done()
                        take(u_act[:, 2 * s:2 * s + 2, :])
                    elif s < 4:
                        tile_done()
                        take(vg[:, :, (s - 2) * S:(s - 1) * S])
                    elif s < 10:
                        merge_step((s - 4) % 3, 0, (s - 4) // 3)

                attend(diff, 1, beside_diff)
                T.n["o_ready"] += 4
                A(vg[:, :, :], vg[:, :, :], ACT.Gelu_apprx_tanh)
                act.wait_ge(*T.next("y_ready", 8))
                squares(od, 4, None, sq_od)
                act.drain()
                for t in range(2):
                    last = A(bufA[:, t, 0:256], vg[:, t, 0:256], ACT.Square, accum_out=esum[:, t, 0:1])
                    last = A(bufB[:, t, 0:256], vg[:, t, 256:512], ACT.Square, accum_out=esum[:, t, 1:2])
                last.then_inc(*T.counts("vq_ready"))
                A(u_act, u_act, ACT.Gelu_apprx_tanh).then_inc(*T.counts("ug_ready"))
                use_ln_exp()
                act.wait_ge(*T.next("vsum_ready"))
                A(rsum[:, 0, :], rsum[:, 0, :], ACT.Ln, bias=c("eps"), scale=1.0 / 512)
                act.drain()
                A(rsum[:, 0, :], rsum[:, 0, :], ACT.Exp, scale=-0.5).then_inc(*T.counts("vr_ready"))
                for i in range(2):
                    root(2)
                    for j in range(2):
                        act.wait_ge(*T.next("odt_ready"))
                        A(yhi[:, 1, 2 * i + j, :], odt[:, 2 * i + j, :], ACT.Copy, scale=lam[:, 5:6])\
                            .then_inc(*T.counts("oh_ready"))
                use_exp_tanh()
                for half in range(2):
                    for k in range(3):
                        merge_step(k, 1, half)
                    if half == 0:
                        act.wait_ge(*T.next("gh_pre"))
                        A(yhi[:, 0, :, :], set_b[:, 0:4, :], ACT.Copy).then_inc(*T.counts("gh_ready"))
                for half in range(2):
                    for k in range(3):
                        merge_step(k, 2, half)
                merged_parts()
                use_ln_exp()
                output_projection()
                squares(x, KD, "x_ready")
                root()
                high_parts()
                ffn(layer < DEPTH - 1)
                squares(x, KD, "x_ready")
                root()

        @block.vector
        def _(v):
            T = Tally(v, sems)
            tt, ts, stt = nc.vector.tensor_tensor, nc.vector.tensor_scalar, nc.vector.scalar_tensor_tensor

            def over(ap, n, axis=1):
                shape = list(ap.shape)
                shape.insert(axis, n)
                return ap.unsqueeze(axis).broadcast_to(shape)

            def apart():
                nc.vector.memset(spare[:, :], 0.0)
                v.drain()

            def split_low():
                slot = T.n["lo_ready"] % RING
                v.wait_ge(*T.next("hi_ready"))
                tt(wlo[:, slot, :], raw[:, slot, :], whi[:, slot, :].bitcast(F32), ALU.subtract)\
                    .then_inc(*T.counts("lo_ready"))

            def tile_done(wait=True):
                if T.n["lo_ready"] < T.n["tile_used"] + RING:
                    split_low()
                if wait:
                    v.wait_ge(*T.next("tile_used"))
                else:
                    T.n["tile_used"] += 1

            def last_tile_done(more, wait):
                if more is None:
                    split_low()
                else:
                    apart()
                    with v.If(more):
                        split_low()
                tile_done(wait)

            def ada_unit(out_ap):
                slot = T.n["ada_used"] % 2
                v.wait_ge(*T.next(f"ada_full{slot}"))
                nc.vector.tensor_tensor_reduce(adat[:, slot, :], adat[:, slot, :], cact[:, :], 1.0, 0.0,
                                               ALU.mult, ALU.add, out_ap).then_inc(*T.counts("ada_used"))

            def shift_scale(s):
                v.drain()
                tt(modf[:, s, 0:16], modc[:, s, 0:16], p1("ada_b", 24 * s, 16), ALU.add)
                v.drain()
                stt(out=modf[:, s, 8:16], in0=modf[:, s, 8:16], scalar=1.0, in1=p1("norm_pre", 8 * s, 8),
                    op0=ALU.add, op1=ALU.mult)
                v.drain()

            def gate_of(s, weight):
                v.drain()
                tt(modf[:, s, 16:24], modc[:, s, 16:24], p1("ada_b", 24 * s + 16, 8), ALU.add)
                v.drain()
                stt(out=modf[:, s, 16:24], in0=modf[:, s, 16:24], scalar=1.0, in1=p1("norm_post", 8 * s, 8),
                    op0=ALU.add, op1=ALU.mult)
                if weight != 1.0:
                    v.drain()
                    ts(modf[:, s, 16:24], modf[:, s, 16:24], weight, None, ALU.mult)
                v.drain()

            def square_sums():
                for i in (0, 4):
                    v.wait_ge(*T.next("sq_ready", 2))
                    tt(sq[:, i:i + 2, :], sq[:, i:i + 2, :], sq[:, i + 2:i + 4, :], ALU.add)\
                        .then_inc(*T.counts("sum_ready"))

            def root():
                v.wait_ge(*T.next("rstd_ready"))

            def normed(gain, shift=None):
                root()
                for i in range(KD + 1):
                    if i < KD:
                        stt(out=tmp[:, i, :], in0=x[:, i, :], scalar=gain[:, i:i + 1], in1=rstd[:, 0, :],
                            op0=ALU.mult, op1=ALU.mult).then_inc(*T.counts("t2_ready"))
                    m = i - 1
                    if m < 0:
                        continue
                    v.wait_ge(*T.next("hh_ready"))
                    if shift is None:
                        last = tt(hlo[:, m, :], tmp[:, m, :], hhi[:, m, :].bitcast(F32), ALU.subtract)
                    else:
                        last = stt(out=hlo[:, m, :], in0=tmp[:, m, :], scalar=shift[:, m:m + 1],
                                   in1=hhi[:, m, :].bitcast(F32), op0=ALU.add, op1=ALU.subtract)
                    last.then_inc(*T.counts("h_ready"))

            def add_normed(gate_):
                square_sums()
                root()
                for m in range(KD):
                    stt(out=tmp[:, m, :], in0=acc[:, m, :], scalar=gate_[:, m:m + 1], in1=rstd[:, 0, :],
                        op0=ALU.mult, op1=ALU.mult)
                v.drain()
                for j in range(4):
                    tt(x[:, 2 * j:2 * j + 2, :], x[:, 2 * j:2 * j + 2, :], tmp[:, 2 * j:2 * j + 2, :], ALU.add)\
                        .then_inc(*T.counts("x_ready"))
                square_sums()

            def add_plain():
                for j in range(4):
                    tt(x[:, 2 * j:2 * j + 2, :], x[:, 2 * j:2 * j + 2, :], acc[:, 2 * j:2 * j + 2, :], ALU.add)\
                        .then_inc(*T.counts("x_ready"))
                square_sums()

            def rope(dst, src, rot, cos, sin, scratch):
                v.wait_ge(*T.next("rot_ready"))
                tt(dst, src, cos, ALU.mult)
                tt(scratch, rot, sin, ALU.mult)
                v.drain()
                tt(dst, dst, scratch, ALU.add).then_inc(*T.counts("rope_done"))
                v.drain()

            rot6 = ps[:, 6, :].rearrange("p (c s) -> p c s", c=2)

            def masks(ins, u, e0):
                bank = T.n["s_ready"] % 2
                v.wait_ge(*T.next("s_ready"))
                if u >= 2:
                    v.wait_ge(*T.nth("e_ready", e0 + u - 1))
                apart()
                for i, (a, b, m) in enumerate(((0, 128, c("negmask")[:, 128:256]), (128, 384, c("negmask")))):
                    last = nc.vector.tensor_tensor_reduce(bufA[:, u % 2, a:b], ps[:, bank, a:b], m, -ins.scale, 3e38,
                                                          ALU.add, ALU.min, nmax[:, u % 2, i:i + 1])
                last.then_inc(*T.counts("sm_ready"))

            def norms(ins, u, factor):
                v.wait_ge(*T.next("e_ready"))
                r = rsum[:, u % 2, :]
                nc.vector.reciprocal(r, esum[:, u % 2, :])
                v.drain()
                if factor is not None:
                    tt(r, r, factor, ALU.mult)
                    v.drain()
                elif ins.fused and u % 2:
                    ts(r, r, lam[:, 4:5], None, ALU.mult)
                    v.drain()
                for i, (a, b) in enumerate(((0, 128), (128, 384))):
                    if ins.fused and u % 2:
                        last = stt(out=bufB[:, 0, a:b], in0=bufB[:, 1, a:b], scalar=r[:, i:i + 1],
                                   in1=bufB[:, 0, a:b], op0=ALU.mult, op1=ALU.add)
                    else:
                        last = ts(bufB[:, u % 2, a:b], bufB[:, u % 2, a:b], r[:, i:i + 1], None, ALU.mult)
                if not ins.fused or u % 2:
                    last.then_inc(*T.counts("p_ready"))

            def pair_low(n, pair):
                v.wait_ge(*T.next("yhi_ready"))
                tt(ylo[:, n % 2, pair, :], ps[:, 3, 0:S],
                   yhi[:, n % 2, pair, :].bitcast(F32), ALU.subtract).then_inc(*T.counts("y_ready"))

            def attend(ins, n, beside, factor=lambda u: None):
                e0, o0 = T.n["e_ready"], T.n["o_ready"]
                for s in range(ins.units + (2 if ins.fused else 3)):
                    if s < ins.units:
                        masks(ins, s, e0)
                    if 1 <= s <= ins.units:
                        norms(ins, s - 1, factor(s - 1))
                    beside(s)
                    if ins.fused:
                        if s >= 3 and s % 2:
                            v.wait_ge(*T.nth("o_ready", o0 + s // 2))
                            nc.vector.tensor_copy(od[:, s // 2 - 1, :], ps[:, 3, 0:S])\
                                .then_inc(*T.counts("y_ready"))
                    elif s >= 3 and (s - 2) % ins.pair_units == 0:
                        pair_low(n, (s - 3) // ins.pair_units)
                T.n["o_ready"] += ins.turns

            def sticks(n, beside):
                w0 = T.n["w_ready"]
                for s in range(HEADS + 3):
                    if 2 <= s <= HEADS + 1:
                        u = s - 2
                        v.wait_ge(*T.next("r_ready"))
                        tt(bufA[:, u % 2, :], bufA[:, u % 2, :], ps[:, 2, 0:384], ALU.add)\
                            .then_inc(*T.counts("arg_ready"))
                    if s < HEADS:
                        bank = T.n["z_ready"] % 2
                        v.wait_ge(*T.next("z_ready"))
                        if s >= 2:
                            v.wait_ge(*T.nth("w_ready", w0 + s - 1))
                        tt(bufA[:, s % 2, :], ps[:, bank, 0:384], c1("negmask_sb"), ALU.add)\
                            .then_inc(*T.counts("zm_ready"))
                    if 1 <= s <= HEADS:
                        u = s - 1
                        v.wait_ge(*T.next("l_ready"))
                        stt(out=bufB[:, u % 2, :], in0=bufA[:, u % 2, :], scalar=0.0, in1=bufB[:, u % 2, :],
                            op0=ALU.max, op1=ALU.add).then_inc(*T.counts("sp_ready"))
                    beside(s)
                    if s >= 4 and s % 2 == 0:
                        pair_low(n, (s - 4) // 2)
                T.n["w_ready"] += HEADS
                T.n["o_ready"] += HEADS

            def merge_step(k, n, half, later=False):
                if k < 2:
                    tile_done(False)
                    T.n["pj_out"] += 1
                    return
                tile_done()
                v.wait_ge(*T.nth("pj_out", T.n["pj_out"]))
                m = merged[:, 4 * half:4 * half + 4, :]
                branch = ps[:, 6:8, :].rearrange("p b (c s) -> p (b c) s", c=2)
                if later:
                    v.wait_ge(*T.next("gt_ready"))
                if n == 0:
                    stt(out=m, in0=gs[:, :, :], scalar=1.0, in1=branch, op0=ALU.add, op1=ALU.mult)\
                        .then_inc(*T.counts("m_free"))
                else:
                    stt(out=gs[:, :, :], in0=gs[:, :, :], scalar=1.0, in1=branch, op0=ALU.add, op1=ALU.mult)
                    v.drain()
                    tt(m, m, gs[:, :, :], ALU.add).then_inc(*T.counts("m_free"))
                v.drain()

            def last_modulation(i):
                ada_unit(modc[:, 2, i:i + 1])

            def merged_parts():
                v.wait_ge(*T.next("mh_ready"))
                stt(out=hlo[:, :, :], in0=merged[:, :, :], scalar=0.5, in1=hhi[:, :, :].bitcast(F32),
                    op0=ALU.mult, op1=ALU.subtract)\
                    .then_inc(*T.counts("ml_ready"))

            def output_projection(after=lambda: None):
                for i in range(4):
                    if i == 3:
                        after()
                    tile_done(wait=(i == 3))

            def ffn(ada_units=0, ada_if=None, after=lambda: None, more=None):
                chunk = [0]
                modulations = modc[:, :, :].rearrange("p a b -> p (a b)")

                def unit(i):
                    if ada_units == 3:
                        ada_unit(adac[:, i:i + 1])

                def ada(step, turn=None, count=ada_units):
                    def units():
                        for i in range(2 if ada_units == 3 else 0, count):
                            ada_unit(adac[:, i:i + 1])
                        v.drain()
                        at = 16 + 3 * step if ada_units == 3 else 2 * (step - 2)
                        if turn is not None:
                            at = turn * (2 * ada_units) + at
                        nc.vector.tensor_copy(modulations[:, bass.ds(at, count)], adac[:, 0:count])
                        v.drain()

                    if ada_units == 0 or (ada_units == 2 and turn is None):
                        return
                    if ada_if is None:
                        units()
                    else:
                        apart()
                        with v.If(ada_if):
                            units()

                def gate_up():
                    v.drain()
                    tile_done(False)
                    unit(0)
                    tile_done()
                    v.wait_ge(*T.next("sil_ready"))
                    tt(a32, sil, ps[:, 5, :].rearrange("p (c s) -> p c s", c=2), ALU.mult)\
                        .then_inc(*T.counts("gu_free"))
                    v.drain()
                    parity = chunk[0] % 2
                    chunk[0] += 1
                    nc.vector.tensor_copy(yhi[:, parity, 0:2, :], a32)
                    v.drain()
                    tt(ylo[:, parity, 0:2, :], a32, yhi[:, parity, 0:2, :].bitcast(F32), ALU.subtract)\
                        .then_inc(*T.counts("a_ready"))
                    unit(1)

                gate_up()
                ada(0)
                gate_up()
                tile_done(False)
                ada(1)
                extra = {3: ADA_BESIDE_1, 2: ADA_BESIDE_2, 0: {}}[ada_units]
                with T.loop((NJ - 3) // 2, {**FFN_BODY, **extra}) as turn:
                    for i in range(2):
                        gate_up()
                        tile_done(False)
                        ada(2 + i, turn)
                gate_up()
                last_tile_done(more, False)
                ada(10, count=2)
                after()
                last_tile_done(more, True)

            v.wait_ge(s_const, 16)
            v.wait_ge(s_pos, 16)
            posf, ang, kf = bufA[:, 0, 0:S], bufA[:, 1, 0:S], bufB[:, 0, 0:S]
            nc.vector.tensor_copy(posf, pos_in[:, :])
            v.drain()
            ts(ang, posf, c("invf"), None, ALU.mult)
            v.drain()
            for i, quarter in enumerate((0.25, 0.0)):
                ts(kf, ang, 1.0 / (2 * math.pi), quarter, ALU.mult, ALU.add)
                v.drain()
                ts(kf, kf, ROUND, ROUND, ALU.add, ALU.subtract)
                v.drain()
                r = tables2[:, i, :]
                stt(out=r, in0=kf, scalar=-PI2[0], in1=ang, op0=ALU.mult, op1=ALU.add)
                v.drain()
                stt(out=r, in0=kf, scalar=-PI2[1], in1=r, op0=ALU.mult, op1=ALU.add)
                v.drain()
                stt(out=r, in0=kf, scalar=-PI2[2], in1=r, op0=ALU.mult, op1=ALU.add)
                v.drain()
                if i == 0:
                    ts(r, r, math.pi / 2, None, ALU.add)
                else:
                    ts(r, r, c("rsign"), None, ALU.mult)
                v.drain()
                last = ts(r, r, -3.1415925, 3.1415925, ALU.max, ALU.min)
            last.then_inc(*T.counts("ang_ready"))
            v.wait_ge(*T.next("c_ready"))
            for i in range(16):
                if i % 4 == 0:
                    v.wait_ge(s_first[i // 4], 64)
                if i == 4:
                    v.wait_ge(s_x, 16)
                    for j in range(4):
                        v.nop().then_inc(*T.counts("x_ready"))
                nc.vector.tensor_tensor_reduce(first_ada[i], first_ada[i], cact[:, :], 1.0, 0.0, ALU.mult, ALU.add,
                                               modc[:, 0, i:i + 1]).then_inc(*T.counts("first_used"))
                if i == 7:
                    square_sums()
            split_low()
            split_low()
            v.wait_ge(s_blk1, 32)
            v.wait_ge(s_load, 16 * N_LOADS)
            cos1, sin1 = tables[:, 0, :], tables[:, 1, :]
            cosm, sinm = tables[64:96, 2, :], tables[64:96, 3, :]
            with T.loop(DEPTH, LAYER1) as layer:
                nc.vector.tensor_copy(par1[:, :], par1_all[:, bass.ds(layer * N_PAR1, N_PAR1)])
                shift_scale(0)
                ts(gate_b[:, 0:24], p1("b_gate"), 0.5, None, ALU.mult)
                normed(modf[:, 0, 8:16], modf[:, 0, 0:8])
                ffn(ada_units=3, after=lambda: (gate_of(0, 0.5), shift_scale(1)))
                add_normed(modf[:, 0, 16:24])
                normed(modf[:, 1, 8:16], modf[:, 1, 0:8])
                for i in range(4):
                    tile_done(False)
                    if i:
                        rope(set_a[:, 2 * i - 2:2 * i, :], set_a[:, 2 * i - 2:2 * i, :], rot6, over(cos1, 2),
                             over(sin1, 2), rstd[:, :, :])
                tile_done(False)
                rope(set_a[:, 6:8, :], set_a[:, 6:8, :], rot6, over(cos1, 2), over(sin1, 2), rstd[:, :, :])
                tile_done(False)
                T.n["pj_out"] += 6

                def beside_moba(s):
                    if s < 8:
                        tile_done(False)
                        T.n["pj_out"] += 1
                        last_modulation(s)

                attend(moba, 0, beside_moba)

                def beside_sticks(s):
                    if s == 0:
                        tile_done(False)
                        T.n["pj_out"] += 1
                        T.n["sq_ready"] += 2
                        root()
                        for i in range(3):
                            g = p1("q_norm", i, 1) if i < 2 else p1("kv_norm")
                            stt(out=set_a[:, 4 + i, :], in0=cq_raw[:, i, :], scalar=g, in1=rstd[:, i // 2, :],
                                op0=ALU.mult, op1=ALU.mult).then_inc(*T.counts("t2_ready"))
                        v.drain()
                        for i in range(3):
                            v.wait_ge(*T.next("hh_ready"))
                            tt(smalllo[:, i * S:(i + 1) * S], set_a[:, 4 + i, :],
                               smallhi[:, i * S:(i + 1) * S].bitcast(F32), ALU.subtract)\
                                .then_inc(*T.counts("h_ready"))
                    elif s == 1:
                        tile_done(False)
                        T.n["pj_out"] += 4
                        rope(kr, kr, ps[64:96, 6, 0:S], cosm, sinm, rstd[64:96, 0, :])
                        nc.vector.tensor_copy(set_a[64:96, 8:16, :], over(kr, HEADS))\
                            .then_inc(*T.counts("kr_ready"))
                    elif s == 2:
                        tile_done(False)
                        T.n["pj_out"] += 6
                        for i in range(4):
                            q_ = set_a[64:96, 2 * i:2 * i + 2, :]
                            rope(q_, q_, rot6[64:96], over(cosm, 2), over(sinm, 2), rstd[64:96, :, :])
                    elif s < 9:
                        merge_step(s % 3, 0, s // 6, True)
                    if s < 8:
                        last_modulation(8 + s)

                sticks(1, beside_sticks)

                def beside_mla(s):
                    if s < 6:
                        merge_step(s % 3, 1, s // 3)
                        last_modulation(16 + s)

                attend(mla, 2, beside_mla)
                for half in range(2):
                    for k in range(3):
                        merge_step(k, 2, half)
                    last_modulation(22 + half)
                merged_parts()
                output_projection(lambda: (gate_of(1, 1.0), shift_scale(2)))
                add_normed(modf[:, 1, 16:24])
                normed(modf[:, 2, 8:16], modf[:, 2, 0:8])
                ffn(ada_units=2, ada_if=layer < DEPTH - 1, after=lambda: gate_of(2, 0.5))
                add_normed(modf[:, 2, 16:24])

            v.nop().then_inc(*T.counts("block1_over"))
            v.wait_ge(*T.next("tab_ready"))
            cos2, sin2 = tables2[:, 0, :], tables2[:, 1, :]
            with T.loop(DEPTH, LAYER2) as layer:
                nc.vector.tensor_copy(norms2[:, :], norms2_all[:, bass.ds(layer * 16, 16)])
                nc.vector.tensor_copy(lam[:, 6:8], c("lam_init")[:, bass.ds(layer * 2, 2)])
                v.drain()
                normed(norms2[:, 0:8])
                v.wait_ge(s_blk2, layer * 16 + 16)
                ts(gate_b[:, 0:24], c2("b_merge"), 0.5, None, ALU.mult)
                lv = c2("lvec")
                for i in range(2):
                    last = nc.vector.tensor_tensor_reduce(lv[:, 128 * i:128 * i + 64], lv[:, 128 * i:128 * i + 64],
                                                          lv[:, 128 * i + 64:128 * i + 128], 1.0, 0.0,
                                                          ALU.mult, ALU.add, lam[:, i:i + 1])
                last.then_inc(*T.counts("lam_pre"))
                for i in range(2):
                    tile_done(False)
                rope(set_a[:, 4:6, :], set_a[:, 0:2, :], rot6, over(cos2, 2), over(sin2, 2), rstd[:, :, :])
                tile_done()
                T.n["pj_out"] += 3
                v.wait_ge(*T.nth("pj_out", T.n["pj_out"]))
                rope(set_a[:, 6:8, :], set_a[:, 2:4, :], rot6, over(cos2, 2), over(sin2, 2), rstd[:, :, :])
                v.wait_ge(*T.next("lam_exp"))
                stt(out=lam[:, 4:5], in0=lam[:, 3:4], scalar=lam[:, 2:3], in1=lam[:, 6:7],
                    op0=ALU.subtract, op1=ALU.subtract)
                tt(lam[:, 5:6], c2("subln"), lam[:, 7:8], ALU.mult)
                for i in range(2):
                    tile_done(False)
                    k_ = set_a[:, 8 + 2 * i:10 + 2 * i, :]
                    rope(k_, k_, rot6, over(cos2, 2), over(sin2, 2), rstd[:, :, :])
                tile_done(False)
                T.n["pj_out"] += 5
                for kind in range(2):
                    pos = c2("pos")[:, 16 * kind:16 * kind + 16]
                    for g in range(G):
                        for half in range(2):
                            src = x2[:, kind, g, 16 * half:16 * half + 240].rearrange("p (n c) -> p c n", c=16)
                            dst = xb32.rearrange("p (c g n) -> p c g n", g=G, n=N_CMP)[:, 8 * half:8 * half + 8, g, :]
                            last = tt(dst, src[:, 0:16:2, :], over(pos[:, 8 * half:8 * half + 8], N_CMP, 2), ALU.add)
                    last.then_inc(*T.counts("xb32_ready"))
                    v.drain()
                    v.wait_ge(*T.next("hx_ready"))
                    tt(smalllo[:, 0:480], xb32, smallhi[:, 0:480].bitcast(F32), ALU.subtract)\
                        .then_inc(*T.counts("xb_ready"))
                    v.drain()
                    tile_done(False)
                    tile_done()
                T.n["pj_out"] += 2
                v.wait_ge(*T.next("cl_ready"))
                l30 = cmpl.rearrange("p (h a) -> p h a", h=HEADS)
                l15 = cmpl.rearrange("p (a n) -> p a n", n=N_CMP)
                for i in range(2):
                    stt(out=l30[:, i:HEADS:2, :], in0=ps[:, 6 + i, 0:120].rearrange("p (h a) -> p h a", h=HEADS // 2),
                        scalar=HD ** -0.5, in1=over(c("cmask"), HEADS // 2), op0=ALU.mult, op1=ALU.add)
                v.drain()
                nc.vector.tensor_reduce(cml[:, 0, :], l15, AX.X, ALU.max)
                v.drain()
                tt(l15, l15, over(cml[:, 0, :], N_CMP, 2), ALU.subtract).then_inc(*T.counts("cs_ready"))
                v.wait_ge(*T.next("cx_ready"))
                nc.vector.tensor_reduce(cml[:, 1, :], l15, AX.X, ALU.add)
                v.drain()
                nc.vector.reciprocal(cml[:, 2, :], cml[:, 1, :])
                v.drain()
                v.wait_ge(*T.next("aux_out", 5))
                ts(gts[:, :, :], gts[:, :, :], 0.5, 0.5, ALU.mult, ALU.add)
                v.drain()
                tt(cml[:, 2, :].rearrange("p (h t) -> p h t", t=2), cml[:, 2, :].rearrange("p (h t) -> p h t", t=2),
                   gts[:, :, :].rearrange("p t (h b) -> p h t b", b=3)[:, :, :, 0], ALU.mult)
                v.drain()
                tt(l15, l15, over(cml[:, 2, :], N_CMP, 2), ALU.mult)
                v.drain()
                tt(l30, l30, over(c("cmask01"), HEADS), ALU.mult).then_inc(*T.counts("cp_ready"))

                def beside_nsa(s):
                    if s in (1, 3, 5, 7, 9, 11):
                        tile_done(False)
                        T.n["pj_out"] += 1

                def branch_gate(u):
                    return gts[:, :, 3 * (u // 2) + 1 + u % 2]

                attend(nsa, 0, beside_nsa, branch_gate)
                for i in range(4):
                    q_ = set_b[:, 2 * i:2 * i + 2, :]
                    rope(q_, q_, rot6, over(cos2, 2), over(sin2, 2), rstd[:, :, :])

                def beside_diff(s):
                    if s < 4:
                        tile_done(False)
                        T.n["pj_out"] += 1
                    elif s < 10:
                        merge_step((s - 4) % 3, 0, (s - 4) // 3)

                attend(diff, 1, beside_diff)
                v.wait_ge(*T.next("vq_ready"))
                tt(rsum[:, 0, :], esum[:, :, 0], esum[:, :, 1], ALU.add).then_inc(*T.counts("vsum_ready"))
                T.n["sq_ready"] += 2
                for i in range(2):
                    root()
                    for j in range(2):
                        tt(odt[:, 2 * i + j, :], od[:, 2 * i + j, :], rstd[:, j, :], ALU.mult)\
                            .then_inc(*T.counts("odt_ready"))
                v.wait_ge(*T.next("vr_ready"))
                for t in range(2):
                    last = ts(vg[:, t, :], vg[:, t, :], rsum[:, 0, t:t + 1], None, ALU.mult)
                last.then_inc(*T.counts("vs_ready"))
                for i in range(4):
                    v.wait_ge(*T.next("oh_ready"))
                    last = stt(out=ylo[:, 1, i, :], in0=odt[:, i, :], scalar=lam[:, 5:6],
                               in1=yhi[:, 1, i, :].bitcast(F32), op0=ALU.mult, op1=ALU.subtract)
                last.then_inc(*T.counts("ol_ready"))
                v.wait_ge(*T.next("sg_ready"))
                sg = ps[:, 0:2, :].rearrange("p b (g s) -> p (b g) s", g=2)
                for g in range(4):
                    stt(out=set_b[:, g, :].rearrange("p (n t) -> p n t", n=2),
                        in0=sg[:, g, :].rearrange("p (n t) -> p n t", n=2), scalar=c2("sgu_norm")[:, g:g + 1],
                        in1=over(c2("sgu_b")[:, g * P:(g + 1) * P], 2), op0=ALU.mult, op1=ALU.add)
                v.drain()
                v.wait_ge(*T.next("ug_ready"))
                tt(set_b[:, 0:4, :], set_b[:, 0:4, :], u_act, ALU.mult).then_inc(*T.counts("gh_pre"))
                v.drain()
                for half in range(2):
                    for k in range(3):
                        merge_step(k, 1, half)
                    if half == 0:
                        v.wait_ge(*T.next("gh_ready"))
                        tt(ylo[:, 0, :, :], set_b[:, 0:4, :], yhi[:, 0, :, :].bitcast(F32), ALU.subtract)\
                            .then_inc(*T.counts("gl_ready"))
                for half in range(2):
                    for k in range(3):
                        merge_step(k, 2, half)
                v.nop().then_inc(*T.counts("mix_done"))
                merged_parts()
                output_projection()
                add_plain()
                normed(norms2[:, 8:16])
                ffn(more=layer < DEPTH - 1)
                add_plain()
            root()
            for m in range(KD):
                last = stt(out=tmp[:, m, :], in0=x[:, m, :], scalar=final_norm[:, m:m + 1], in1=rstd[:, 0, :],
                           op0=ALU.mult, op1=ALU.mult)
            last.then_inc(s_final, 1)

        @block.gpsimd
        def _(g):
            g.dma_start(par1_all[:, :], par1_in).then_inc(s_load, 16)
            g.dma_start(norms2_all[:, :], norms2_in[:, 0:16 * DEPTH]).then_inc(s_load, 16)
            g.dma_start(final_norm[:, :], norms2_in[:, 16 * DEPTH:16 * DEPTH + KD]).then_inc(s_load, 16)
            g.dma_start(tables[:, :, :], block1_in[:, N_BLOCK1:N_BLOCK1 + 4 * S]
                        .rearrange("p (a s) -> p a s", a=4)).then_inc(s_blk1, 16)
            g.dma_start(blk[:, 0:N_BLOCK1], block1_in[:, 0:N_BLOCK1]).then_inc(s_blk1, 16)
            g.wait_ge(sems["first_used"], 16)
            for i in range(2):
                g.dma_start(adat[:, i, :], ada[16 + i]).then_inc(sems[f"ada_full{i}"], 16)
            with g.Fori(0, (ADA_UNITS - 16) // 2 - 1) as turn:
                for i in range(2):
                    g.wait_ge(sems["ada_used"], turn * 2 + i + 1)
                    g.dma_start(adat[:, i, :], ada[bass.ds(turn * 2 + (18 + i), 1), :, :]
                                .rearrange("a p n -> p (a n)")).then_inc(sems[f"ada_full{i}"], 16)
            g.wait_ge(sems["ada_used"], ADA_UNITS - 16)
            g.wait_ge(sems["block1_over"], 1)
            for l in range(DEPTH):
                if l:
                    g.wait_ge(sems["mix_done"], l)
                g.dma_start(blk[:, 0:N_BLOCK2], block2_in[l]).then_inc(s_blk2, 16)
                g.wait_ge(s_blk2, 16 * (l + 1))
                wt = c2("sgu_wT").rearrange("p (g t) -> p g t", g=4)
                g.affine_select(out=wt, in_=wt, compare_op=ALU.is_ge, fill=0.0, base=0, pattern=[[0, 4], [1, P]],
                                channel_multiplier=-1).then_inc(sems["wt_ready"], 1)


PI2 = (6.28125, 2029.0 / 2 ** 20, 2 * math.pi - 6.28125 - 2029.0 / 2 ** 20)
ROUND = 1.5 * 2.0 ** 23


def constants():
    f = np.float32
    c = np.zeros((P, N_CONST), f)
    i = np.arange(P)

    def put(into, table, name, value):
        a, b = table[name]
        into[:, a:b] = value

    put(c, CONSTS, "ident", np.eye(P))
    put(c, CONSTS, "inv1024", 1.0 / D)
    put(c, CONSTS, "eps", EPS)
    mask = np.zeros((P, S), f)
    mask[:, P:] = np.where(i[None, :] <= i[:, None], 0.0, NEG)
    put(c, CONSTS, "negmask", mask)
    ends = 16 * np.arange(N_CMP) + 31
    seen = np.concatenate([ends[None, :] <= (i[:, None] + t * P) for t in range(2)], axis=1)
    put(c, CONSTS, "cmask", np.where(seen, 0.0, NEG))
    put(c, CONSTS, "cmask01", seen.astype(f))
    half = HD // 2
    inv = (f(10000.0) ** (-np.arange(half, dtype=f) / f(half))).astype(f)
    put(c, CONSTS, "invf", inv[i % half][:, None])
    put(c, CONSTS, "rsign", np.where(i % HD < half, -1.0, 1.0)[:, None])
    put(c, CONSTS, "lam_init", np.array([v for l in range(DEPTH)
                                         for v in (0.8 - 0.6 * math.exp(-0.3 * l), 1 - (0.8 - 0.6 * math.exp(-0.3 * l)))]))

    b1 = np.zeros((P, N_BLOCK1 + 4 * S), f)

    def swap(size, start, halfrot):
        m = np.zeros((P, P), f)
        for p in range(P):
            q = p % size - start
            if 0 <= q < 2 * halfrot:
                m[p + halfrot if q < halfrot else p - halfrot, p] = 1.0
        return m

    def rotation(n_rot, size, start):
        h = n_rot // 2
        fr = np.power(f(500000.0), -np.arange(0, n_rot, 2, dtype=f) / f(n_rot)).astype(f)
        ang = (np.arange(S, dtype=f)[:, None] * fr[None, :]).astype(f)
        cos, sin = np.cos(ang).astype(f).T, np.sin(ang).astype(f).T
        ct, st = np.ones((P, S), f), np.zeros((P, S), f)
        for p in range(P):
            q = p % size - start
            if 0 <= q < n_rot:
                ct[p] = cos[q % h]
                st[p] = -sin[q % h] if q < h else sin[q % h]
        return ct, st

    put(b1, BLOCK1, "perm_moba", swap(HD, 0, HD // 8))
    put(b1, BLOCK1, "perm_mla", swap(P, MLA_NOPE, MLA_ROPE // 2))
    put(b1, BLOCK1, "neg_lower", np.where(i[:, None] >= i[None, :], -1.0, 0.0))
    put(b1, BLOCK1, "neg_ones", -1.0)
    put(b1, BLOCK1, "inv256", 1.0 / 256)
    put(b1, BLOCK1, "inv128", 1.0 / 128)
    sbm = np.zeros((P, 384), f)
    tri = np.where(i[:, None] < i[None, :], 0.0, NEG)
    sbm[:, 0:128] = tri
    sbm[:, 256:384] = tri
    put(b1, BLOCK1, "negmask_sb", sbm)
    ct, st = rotation(HD // 4, HD, 0)
    cm, sm = rotation(MLA_ROPE, P, MLA_NOPE)
    b1[:, N_BLOCK1:] = np.stack([ct, st, cm, sm], axis=1).reshape(P, 4 * S)
    return c, b1, swap(HD, 0, half)


def columns(vec):
    return np.asarray(vec).reshape(-1, P).T


def slab(wm, c0, n=256):
    k = wm.shape[0] // P
    return wm[:, c0:c0 + n].reshape(k, P, n).transpose(1, 0, 2).reshape(P, k * n)


def weight_tiles(inp):
    tiles = np.zeros((N_TILES, P, TW), np.float32)
    n = [0]

    def put(a):
        tiles[n[0], :, :a.shape[1]] = a
        n[0] += 1

    def ffn(wg, wu, wd):
        def down(j):
            put(slab(wd[256 * j:256 * j + 256], 0, D))

        for j in range(NJ):
            put(slab(wg, 256 * j))
            put(slab(wu, 256 * j))
            if j >= 1:
                down(j - 1)
        down(NJ - 1)

    def merge(gates, g0, branch, n_):
        for half in range(2):
            put(slab(gates, g0 + n_ * D + 512 * half))
            put(slab(gates, g0 + n_ * D + 512 * half + 256))
            put(slab(branch, 512 * half, 512))

    for l in range(DEPTH):
        ffn(inp["ffn_w_gate"][l, 0], inp["ffn_w_up"][l, 0], inp["ffn_w_down"][l, 0])
        w = inp["mix_w_in"][l]
        for j in range(12):
            put(slab(w, 256 * j))
        c_q, c_kv, k_r, gates = 3072, 3328, 3456, 3488
        put(slab(w, c_q))
        put(slab(w, c_kv, P))
        put(slab(w, k_r - 64, 96))
        put(slab(inp["mla_w_uq"][l], 0, HEADS * MLA_QK))
        put(slab(inp["mla_w_ukv"][l], 0, HEADS * P))
        for b in range(3):
            merge(w, gates, inp["mix_w_branch"][l, b], b)
        for j in range(4):
            put(slab(inp["mix_w_out"][l], 256 * j))
        ffn(inp["ffn_w_gate"][l, 1], inp["ffn_w_up"][l, 1], inp["ffn_w_down"][l, 1])
    for l in range(DEPTH):
        w = inp["w_in_2"][l]
        for j in range(5):
            put(slab(w, 256 * j))
        put(slab(w, 1280, P))
        for name in ("cmp_k_w1_2", "cmp_v_w1_2"):
            put(slab(inp[name][l][0:1024], 0))
            put(slab(inp[name][l][1024:2048], 0))
        for j in range(10):
            put(slab(w, 1304 + 256 * j))
        for b, name in enumerate(("w_branch_a_2", "w_branch_b_2", "w_branch_c_2")):
            merge(inp["w_merge_2"][l], 0, inp[name][l], b)
        for j in range(4):
            put(slab(inp["w_out_2"][l], 256 * j))
        ffn(inp["w_ffn1_2"][l], inp["w_ffn3_2"][l], inp["w_ffn2_2"][l])
    assert n[0] == N_TILES, n[0]
    return tiles


def pack(table, width, parts):
    out = np.zeros((P, width), np.float32)
    for name, value in parts.items():
        a, b = table[name]
        out[:, a:b] = value
    return out


def kernel(**inputs):
    from concourse import bacc
    from concourse.bass_utils import run_bass_kernel_spmd

    inp = {k: np.asarray(v) for k, v in inputs.items()}
    const, block1, perm_half = constants()
    ada = inp["ada_w"].reshape(DEPTH, D, 3 * ADA_PER_SUB, P).transpose(0, 2, 3, 1).reshape(ADA_UNITS, P, D)
    par1 = np.concatenate([pack(PAR1, N_PAR1, {
        "ada_b": columns(inp["ada_b"][l]), "norm_pre": columns(inp["norm_pre"][l]),
        "norm_post": columns(inp["norm_post"][l]), "b_gate": columns(inp["mix_b_gate"][l]),
        "q_norm": columns(inp["mla_q_norm"][l]), "kv_norm": columns(inp["mla_kv_norm"][l])}) for l in range(DEPTH)], axis=1)
    block2 = []
    for l in range(DEPTH):
        w2k = inp["cmp_k_w2_2"][l].reshape(2, P, HD).transpose(1, 0, 2)
        block2.append(pack(BLOCK2, N_BLOCK2, {
            "perm_half": perm_half, "inv128": 1.0 / 128, "b_merge": columns(inp["b_merge_2"][l]),
            "subln": columns(inp["diff_subln_2"][l]), "sgu_norm": columns(inp["sgu_norm_2"][l]),
            "lvec": np.concatenate([inp[f"diff_{k}_2"][l] for k in ("lq1", "lk1", "lq2", "lk2")])[None, :],
            "sgu_b": inp["sgu_b_2"][l].reshape(1, 512),
            "sgu_wT": inp["sgu_w_2"][l].transpose(2, 0, 1).reshape(P, 512),
            "w2k": np.concatenate([w2k, w2k], axis=2).reshape(P, 256),
            "w2v": inp["cmp_v_w2_2"][l].reshape(2, P, HD).transpose(1, 0, 2).reshape(P, 128),
            "pos": np.concatenate([inp[k][l].reshape(16, 2 * HD).T for k in ("cmp_pos_k_2", "cmp_pos_v_2")], axis=1)}))
    norms2 = np.concatenate([columns(inp[k][l]) for l in range(DEPTH) for k in ("attn_norm_2", "ffn_norm_2")]
                            + [columns(inp["final_norm_2"])], axis=1)
    arrays = {
        "w": weight_tiles(inp), "ada": ada,
        "x": inp["x"][0].T.reshape(KD, P, S).transpose(1, 0, 2),
        "c": inp["c"].reshape(D), "positions": inp["positions_2"].reshape(S),
        "const": const, "block1": block1, "par1": par1, "block2": np.stack(block2), "norms2": norms2,
    }
    arrays = {f"in_{k}": np.ascontiguousarray(v) for k, v in arrays.items()}
    nc = bacc.Bacc("TRN2", target_bir_lowering=False, num_devices=1)
    args = [nc.dram_tensor(k, v.shape, mybir.dt.from_np(v.dtype), kind="ExternalInput").ap() for k, v in arrays.items()]
    args.append(nc.dram_tensor("out_x", (P, KD, S), F32, kind="ExternalOutput").ap())
    build(nc, *args)
    r = run_bass_kernel_spmd(nc, [arrays], core_ids=[0])
    got = r.results[0]["out_x"]
    return got.transpose(2, 1, 0).reshape(1, S, D)
```
